# Optimizing a Trainium2 kernel written in Bass

```python
import jax
import jax.numpy as jnp
from jax import lax
import numpy as np
import math
import jax, jax.numpy as jnp

D_MODEL = 1024
BATCH = 1
SEQ = 256
DEPTH = 1

CONV_WIDTH = 512
CONV_K = 31
HGRN_HEADS = 4
HGRN_DK = 128
HGRN_DV = 128
HGRN_KW = HGRN_HEADS * HGRN_DK
HGRN_VW = HGRN_HEADS * HGRN_DV
CHUNK = 64
MEM_LEN = 256
XA_HEADS = 4
XA_HEAD_DIM = D_MODEL // XA_HEADS
N_GROUPS = 4
EXPERTS_PER_GROUP = 8
N_EXPERTS = N_GROUPS * EXPERTS_PER_GROUP
TOP_K = 2
D_FF = 512
EPS = 1e-6
ROUTER_BIAS_SCALE = 0.01

_COLS = (CONV_WIDTH, CONV_WIDTH, HGRN_KW, HGRN_KW, HGRN_VW, HGRN_VW, D_MODEL, D_MODEL)
IN_COLS = sum(_COLS)
SPLITS = [sum(_COLS[:i]) for i in range(1, len(_COLS))]


def rms_norm(x, g):
    xf = x.astype(jnp.float32)
    y = xf * lax.rsqrt(jnp.mean(xf * xf, axis=-1, keepdims=True) + EPS)
    return (y * g.astype(jnp.float32)).astype(x.dtype)

def layer_norm(x, g, b):
    xf = x.astype(jnp.float32)
    mu = jnp.mean(xf, axis=-1, keepdims=True)
    var = jnp.mean(jnp.square(xf - mu), axis=-1, keepdims=True)
    y = (xf - mu) * lax.rsqrt(var + EPS)
    return (y * g.astype(jnp.float32) + b.astype(jnp.float32)).astype(x.dtype)

def causal_depthwise_conv(u, w, b):
    y = lax.conv_general_dilated(
        u, w[:, None, :].astype(u.dtype), window_strides=(1,),
        padding=[(CONV_K - 1, 0)], dimension_numbers=('NWC', 'WIO', 'NWC'),
        feature_group_count=u.shape[-1])
    return y + b.astype(u.dtype)

def conformer_conv_branch(a, gate, w_dw, b_dw, ln_g, ln_b, w_proj):
    u = a * jax.nn.sigmoid(gate)
    u = causal_depthwise_conv(u, w_dw, b_dw)
    u = jax.nn.silu(layer_norm(u, ln_g, ln_b))
    return u @ w_proj

def hgrn2_chunkwise(q, k, v, logf):
    b, s, h, dk = q.shape
    dv = v.shape[-1]
    nc = s // CHUNK

    def to_chunks(t):
        return t.reshape(b, nc, CHUNK, h, t.shape[-1]).transpose(1, 0, 3, 2, 4)

    causal = jnp.tril(jnp.ones((CHUNK, CHUNK), dtype=bool))[None, None, :, :, None]

    def step(state, inp):
        qb, kb, vb, fb = inp
        cum = jnp.cumsum(fb, axis=2)
        o_inter = jnp.einsum('bhtk,bhkv->bhtv', qb * jnp.exp(cum), state)
        diff = cum[:, :, :, None, :] - cum[:, :, None, :, :]
        decay = jnp.exp(jnp.where(causal, diff, -jnp.inf))
        scores = jnp.einsum('bhtk,bhtsk,bhsk->bhts', qb, decay, kb)
        o = o_inter + jnp.einsum('bhts,bhsv->bhtv', scores, vb)
        last = cum[:, :, -1:, :]
        state = (jnp.exp(last[:, :, 0, :])[..., None] * state
                 + jnp.einsum('bhsk,bhsv->bhkv', kb * jnp.exp(last - cum), vb))
        return state, o

    s0 = jnp.zeros((b, h, dk, dv), jnp.float32)
    _, o = lax.scan(step, s0, (to_chunks(q), to_chunks(k), to_chunks(v), to_chunks(logf)))
    return o.transpose(1, 0, 3, 2, 4).reshape(b, s, h, dv)

def hgrn2_branch(q_raw, f_raw, i_raw, g_raw, lower_bound, onorm_g, w_o):
    b, s, _ = q_raw.shape

    def heads(t, d):
        return t.reshape(b, s, HGRN_HEADS, d)

    f = lower_bound + (1.0 - lower_bound) * jax.nn.sigmoid(f_raw.astype(jnp.float32))
    q = jax.nn.silu(q_raw.astype(jnp.float32))
    o = hgrn2_chunkwise(heads(q, HGRN_DK), heads(1.0 - f, HGRN_DK),
                        heads(i_raw.astype(jnp.float32), HGRN_DV), heads(jnp.log(f), HGRN_DK))
    o = rms_norm(o, onorm_g) * jax.nn.silu(heads(g_raw.astype(jnp.float32), HGRN_DV))
    return o.reshape(b, s, HGRN_VW).astype(q_raw.dtype) @ w_o

def memory_cross_attention(h, mem_n, w_q, w_k, w_v, w_o):
    b, s, d = h.shape
    m = mem_n.shape[1]
    q = (h @ w_q).reshape(b, s, XA_HEADS, XA_HEAD_DIM)
    k = (mem_n @ w_k).reshape(b, m, XA_HEADS, XA_HEAD_DIM)
    v = (mem_n @ w_v).reshape(b, m, XA_HEADS, XA_HEAD_DIM)
    scores = jnp.einsum('bshd,bmhd->bhsm', q, k).astype(jnp.float32) * (XA_HEAD_DIM ** -0.5)
    p = jax.nn.softmax(scores, axis=-1).astype(v.dtype)
    o = jnp.einsum('bhsm,bmhd->bshd', p, v).reshape(b, s, d)
    return o @ w_o

def hierarchical_moe(h, w_group, b_group, w_expert, b_expert, w_gate, w_up, w_down):
    b, s, d = h.shape
    t = h.reshape(b * s, d)
    n = t.shape[0]
    group_probs = jax.nn.softmax((t @ w_group).astype(jnp.float32) + b_group.astype(jnp.float32), axis=-1)
    g_p, g_idx = lax.top_k(group_probs, 1)
    e_logits = ((t @ w_expert).astype(jnp.float32) + b_expert.astype(jnp.float32))
    e_logits = e_logits.reshape(n, N_GROUPS, EXPERTS_PER_GROUP)
    in_group = jnp.take_along_axis(e_logits, g_idx[:, :, None], axis=1)[:, 0]
    e_p, e_idx = lax.top_k(jax.nn.softmax(in_group, axis=-1), TOP_K)
    e_p = e_p / jnp.sum(e_p, axis=-1, keepdims=True)
    weights = g_p * e_p
    expert_ids = g_idx * EXPERTS_PER_GROUP + e_idx
    combine = jnp.zeros((n, N_EXPERTS), jnp.float32).at[
        jnp.arange(n)[:, None], expert_ids].add(weights).astype(t.dtype)
    y = jnp.zeros_like(t)
    for e in range(N_EXPERTS):
        hid = jax.nn.silu(t @ w_gate[e]) * (t @ w_up[e])
        y = y + combine[:, e:e + 1] * (hid @ w_down[e])
    return y.reshape(b, s, d)

def first_inputs(seed: int = 0) -> dict:
    key = jax.random.key(seed)
    ks = iter(jax.random.split(key, 32))

    def nrm(shape, fan_in):
        return jax.random.normal(next(ks), shape, jnp.float32) * (fan_in ** -0.5)

    def gain(shape):
        return 1.0 + 0.02 * jax.random.normal(next(ks), shape, jnp.float32)

    def small(shape, scale):
        return scale * jax.random.normal(next(ks), shape, jnp.float32)

    L = DEPTH
    return {
        'x': jax.random.normal(next(ks), (BATCH, SEQ, D_MODEL), jnp.float32),
        'mem': jax.random.normal(next(ks), (BATCH, MEM_LEN, D_MODEL), jnp.float32),
        'norm_mix_g': gain((L, D_MODEL)),
        'w_in': nrm((L, D_MODEL, IN_COLS), D_MODEL),
        'conv_w': nrm((L, CONV_K, CONV_WIDTH), CONV_K),
        'conv_b': small((L, CONV_WIDTH), 0.02),
        'conv_ln_g': gain((L, CONV_WIDTH)),
        'conv_ln_b': small((L, CONV_WIDTH), 0.02),
        'conv_w_out': nrm((L, CONV_WIDTH, D_MODEL), CONV_WIDTH),
        'hgrn_lb_logits': small((L + 1, HGRN_KW), 0.5),
        'hgrn_onorm_g': gain((L, HGRN_DV)),
        'hgrn_w_out': nrm((L, HGRN_VW, D_MODEL), HGRN_VW),
        'w_mix_out': nrm((L, D_MODEL, D_MODEL), D_MODEL),
        'norm_xa_g': gain((L, D_MODEL)),
        'norm_mem_g': gain((L, D_MODEL)),
        'xa_w_q': nrm((L, D_MODEL, D_MODEL), D_MODEL),
        'xa_w_k': nrm((L, D_MODEL, D_MODEL), D_MODEL),
        'xa_w_v': nrm((L, D_MODEL, D_MODEL), D_MODEL),
        'xa_w_o': nrm((L, D_MODEL, D_MODEL), D_MODEL),
        'norm_ffn_g': gain((L, D_MODEL)),
        'router_group_w': nrm((L, D_MODEL, N_GROUPS), D_MODEL),
        'router_group_b': small((L, N_GROUPS), ROUTER_BIAS_SCALE),
        'router_expert_w': nrm((L, D_MODEL, N_EXPERTS), D_MODEL),
        'router_expert_b': small((L, N_EXPERTS), ROUTER_BIAS_SCALE),
        'moe_w_gate': nrm((L, N_EXPERTS, D_MODEL, D_FF), D_MODEL),
        'moe_w_up': nrm((L, N_EXPERTS, D_MODEL, D_FF), D_MODEL),
        'moe_w_down': nrm((L, N_EXPERTS, D_FF, D_MODEL), D_FF),
        'final_norm_g': gain((D_MODEL,)),
    }

def first_block(x, mem, norm_mix_g, w_in, conv_w, conv_b, conv_ln_g, conv_ln_b, conv_w_out,
              hgrn_lb_logits, hgrn_onorm_g, hgrn_w_out, w_mix_out, norm_xa_g, norm_mem_g,
              xa_w_q, xa_w_k, xa_w_v, xa_w_o, norm_ffn_g, router_group_w, router_group_b,
              router_expert_w, router_expert_b, moe_w_gate, moe_w_up, moe_w_down, final_norm_g):
    lower_bounds = jnp.cumsum(jax.nn.softmax(hgrn_lb_logits.astype(jnp.float32), axis=0), axis=0)
    for l in range(DEPTH):
        h = rms_norm(x, norm_mix_g[l])
        proj = h @ w_in[l]
        c_a, c_g, q_r, f_r, i_r, g_r, gate_c, gate_r = jnp.split(proj, SPLITS, axis=-1)
        y_conv = conformer_conv_branch(c_a, c_g, conv_w[l], conv_b[l], conv_ln_g[l],
                                       conv_ln_b[l], conv_w_out[l])
        y_rec = hgrn2_branch(q_r, f_r, i_r, g_r, lower_bounds[l], hgrn_onorm_g[l], hgrn_w_out[l])
        merged = jax.nn.sigmoid(gate_c) * y_conv + jax.nn.sigmoid(gate_r) * y_rec
        x = x + merged @ w_mix_out[l]
        h = rms_norm(x, norm_xa_g[l])
        mem_n = rms_norm(mem, norm_mem_g[l])
        x = x + memory_cross_attention(h, mem_n, xa_w_q[l], xa_w_k[l], xa_w_v[l], xa_w_o[l])
        h = rms_norm(x, norm_ffn_g[l])
        x = x + hierarchical_moe(h, router_group_w[l], router_group_b[l], router_expert_w[l],
                                 router_expert_b[l], moe_w_gate[l], moe_w_up[l], moe_w_down[l])
    return rms_norm(x, final_norm_g)


DEPTH_2 = 2

GRID_W = 64
CTX_LEN = 256
HEAD_DIM = 64
NA_HEADS = D_MODEL // 2 // HEAD_DIM
NA_WIN_ROWS = 8
NA_WIN_COLS = 16
DIFF_HEAD_DIM = 64
DIFF_V_DIM = 2 * DIFF_HEAD_DIM
DIFF_HEADS = D_MODEL // 2 // DIFF_V_DIM
NA_WIDTH = NA_HEADS * HEAD_DIM
DIFF_QK_WIDTH = DIFF_HEADS * 2 * DIFF_HEAD_DIM
DIFF_V_WIDTH = DIFF_HEADS * DIFF_V_DIM
ATTN_IN_WIDTH = 3 * NA_WIDTH + 2 * DIFF_QK_WIDTH + DIFF_V_WIDTH
ATTN_OUT_WIDTH = NA_WIDTH + DIFF_V_WIDTH
ATTN_SPLITS = [NA_WIDTH, 2 * NA_WIDTH, 3 * NA_WIDTH,
               3 * NA_WIDTH + DIFF_QK_WIDTH, 3 * NA_WIDTH + 2 * DIFF_QK_WIDTH]
CONV_WIDTH_2 = 3
D_FF_2 = 2816
ROPE_THETA = 10000.0
ATTN_BLOCK = 128
N_MOD = 9
N_ATTN_LAYERS = (DEPTH_2 + 1) // 2
N_CONV_LAYERS = DEPTH_2 // 2
NEG_INF = -1e30


def rmsnorm(x, g):
    x32 = x.astype(jnp.float32)
    y = x32 * lax.rsqrt(jnp.mean(x32 * x32, axis=-1, keepdims=True) + EPS)
    return (y * g.astype(jnp.float32)).astype(x.dtype)

def modulate(x, g, shift, scale):
    return rmsnorm(x, g) * (1 + scale) + shift

def swiglu(x, w_gate, w_up, w_down):
    return (jax.nn.silu(x @ w_gate) * (x @ w_up)) @ w_down

def macaron_ffn(xs, g, shift, scale, gate, w_gate, w_up, w_down):
    return xs + 0.5 * gate * swiglu(modulate(xs, g, shift, scale), w_gate, w_up, w_down)

def axial_rope(n):
    t = jnp.arange(n)
    row = (t // GRID_W).astype(jnp.float32)
    col = (t % GRID_W).astype(jnp.float32)
    n_freq = DIFF_HEAD_DIM // 4
    inv = ROPE_THETA ** (-jnp.arange(n_freq, dtype=jnp.float32) / n_freq)
    ang = jnp.concatenate([row[:, None] * inv, col[:, None] * inv], axis=-1)
    return jnp.cos(ang)[:, None, None, :], jnp.sin(ang)[:, None, None, :]

def apply_rope(x, cos, sin):
    x32 = x.astype(jnp.float32)
    x1, x2 = x32[..., 0::2], x32[..., 1::2]
    out = jnp.stack([x1 * cos - x2 * sin, x1 * sin + x2 * cos], axis=-1)
    return out.reshape(x.shape).astype(x.dtype)

def split_attn_proj(p):
    b, t, _ = p.shape
    qa, ka, va, qb, kb, vb = jnp.split(p, ATTN_SPLITS, axis=-1)
    na = lambda a: a.reshape(b, t, NA_HEADS, HEAD_DIM)
    dqk = lambda a: a.reshape(b, t, DIFF_HEADS, 2, DIFF_HEAD_DIM)
    return (na(qa), na(ka), na(va), dqk(qb), dqk(kb), vb.reshape(b, t, DIFF_HEADS, DIFF_V_DIM))

def dense_attend(q, k, v):
    s = jnp.einsum('bqhd,bkhd->bhqk', q * q.shape[-1] ** -0.5, k)
    p = jax.nn.softmax(s.astype(jnp.float32), axis=-1).astype(v.dtype)
    return jnp.einsum('bhqk,bkhd->bqhd', p, v)

def diff_attend(q, k, v, lam):
    s = jnp.einsum('bqhmd,bkhmd->bhmqk', q * q.shape[-1] ** -0.5, k)
    p = jax.nn.softmax(s.astype(jnp.float32), axis=-1)
    pd = (p[:, :, 0] - lam * p[:, :, 1]).astype(v.dtype)
    return jnp.einsum('bhqk,bkhe->bqhe', pd, v)

def neighbourhood_attention(q, k, v, k_ctx, v_ctx, rpb):
    b, n, h, d = q.shape
    rows = n // GRID_W
    kr = min(NA_WIN_ROWS, rows)
    qg = (q * d ** -0.5).reshape(b, rows, GRID_W, h, d)
    kg = k.reshape(b, rows, GRID_W, h, d)
    vg = v.reshape(b, rows, GRID_W, h, d)
    qc = jnp.arange(GRID_W)
    col_start = jnp.clip(qc - NA_WIN_COLS // 2, 0, GRID_W - NA_WIN_COLS)
    col_mask = (qc[None, :] >= col_start[:, None]) & (qc[None, :] < col_start[:, None] + NA_WIN_COLS)
    dc_idx = jnp.clip(qc[None, :] - qc[:, None] + NA_WIN_COLS - 1, 0, 2 * NA_WIN_COLS - 2)

    def row_block(r):
        start = jnp.clip(r - kr // 2, 0, rows - kr)
        q_r = lax.dynamic_index_in_dim(qg, r, axis=1, keepdims=False)
        k_band = lax.dynamic_slice_in_dim(kg, start, kr, axis=1)
        v_band = lax.dynamic_slice_in_dim(vg, start, kr, axis=1)
        s_band = jnp.einsum('bqhd,brkhd->bhqrk', q_r, k_band).astype(jnp.float32)
        dr_idx = start + jnp.arange(kr) - r + NA_WIN_ROWS - 1
        bias = rpb[:, dr_idx[None, :, None], dc_idx[:, None, :]].astype(jnp.float32)
        s_band = jnp.where(col_mask[:, None, :], s_band + bias, NEG_INF)
        s_ctx = jnp.einsum('bqhd,blhd->bhql', q_r, k_ctx).astype(jnp.float32)
        s = jnp.concatenate([s_band.reshape(b, h, GRID_W, kr * GRID_W), s_ctx], axis=-1)
        p = jax.nn.softmax(s, axis=-1).astype(v.dtype)
        p_band = p[..., :kr * GRID_W].reshape(b, h, GRID_W, kr, GRID_W)
        p_ctx = p[..., kr * GRID_W:]
        return (jnp.einsum('bhqrk,brkhd->bqhd', p_band, v_band)
                + jnp.einsum('bhql,blhd->bqhd', p_ctx, v_ctx))

    out = lax.map(row_block, jnp.arange(rows))
    return jnp.moveaxis(out, 0, 1).reshape(b, n, h, d)

def attn_mixer(xn, xn_ctx, w_in, w_out, rpb, lam_vec, subln_g, lam_init, cos, sin, ctx_out):
    b, n, _ = xn.shape
    qa, ka, va, qb, kb, vb = split_attn_proj(xn @ w_in)
    qa_c, ka_c, va_c, qb_c, kb_c, vb_c = split_attn_proj(xn_ctx @ w_in)
    qb, kb = apply_rope(qb, cos, sin), apply_rope(kb, cos, sin)
    l32 = lam_vec.astype(jnp.float32)
    lam = jnp.exp(jnp.sum(l32[0] * l32[1])) - jnp.exp(jnp.sum(l32[2] * l32[3])) + lam_init

    a_lat = neighbourhood_attention(qa, ka, va, ka_c, va_c, rpb)
    k_all = jnp.concatenate([kb, kb_c], axis=1)
    v_all = jnp.concatenate([vb, vb_c], axis=1)
    nb = n // ATTN_BLOCK
    q_blocks = jnp.moveaxis(qb.reshape(b, nb, ATTN_BLOCK, DIFF_HEADS, 2, DIFF_HEAD_DIM), 1, 0)
    d_lat = lax.map(lambda q_blk: diff_attend(q_blk, k_all, v_all, lam), q_blocks)
    d_lat = jnp.moveaxis(d_lat, 0, 1).reshape(b, n, DIFF_HEADS, DIFF_V_DIM)

    def merge(a, dd):
        t = a.shape[1]
        dd = rmsnorm(dd, subln_g) * (1.0 - lam_init)
        return jnp.concatenate([a.reshape(b, t, NA_WIDTH), dd.reshape(b, t, DIFF_V_WIDTH)], axis=-1) @ w_out

    y_lat = merge(a_lat, d_lat)
    if ctx_out:
        y_ctx = merge(dense_attend(qa_c, ka_c, va_c), diff_attend(qb_c, kb_c, vb_c, lam))
    else:
        y_ctx = None
    return y_lat, y_ctx

def conv_mixer(xn, w_in, w_out, conv_w):
    bg, cg, h = jnp.split(xn @ w_in, 3, axis=-1)
    u = cg * h
    v = lax.conv_general_dilated(u, conv_w[:, None, :].astype(u.dtype), window_strides=(1,),
                                 padding=((CONV_WIDTH_2 // 2, CONV_WIDTH_2 // 2),),
                                 dimension_numbers=('NWC', 'WIO', 'NWC'),
                                 feature_group_count=u.shape[-1])
    return (bg * v) @ w_out

def second_inputs(seed: int = 0) -> dict:
    key = jax.random.key(seed)
    ks = jax.random.split(key, 20)
    nrm = lambda k, shape, s: jax.random.normal(k, shape, jnp.float32) * s
    D = D_MODEL
    return {
        "x": nrm(ks[0], (BATCH, SEQ, D), 1.0),
        "c": nrm(ks[1], (BATCH, D), 1.0),
        "ctx": nrm(ks[2], (BATCH, CTX_LEN, D), 1.0),
        "c_ctx": nrm(ks[3], (D,), 1.0),
        "mod_w": nrm(ks[4], (DEPTH_2, D, N_MOD * D), D ** -0.5),
        "mod_b": nrm(ks[5], (DEPTH_2, N_MOD * D), 0.01),
        "norm_g": 1.0 + nrm(ks[6], (DEPTH_2, 3, D), 0.1),
        "ffn_w_gate": nrm(ks[7], (DEPTH_2, 2, D, D_FF_2), D ** -0.5),
        "ffn_w_up": nrm(ks[8], (DEPTH_2, 2, D, D_FF_2), D ** -0.5),
        "ffn_w_down": nrm(ks[9], (DEPTH_2, 2, D_FF_2, D), D_FF_2 ** -0.5),
        "attn_w_in": nrm(ks[10], (N_ATTN_LAYERS, D, ATTN_IN_WIDTH), D ** -0.5),
        "attn_w_out": nrm(ks[11], (N_ATTN_LAYERS, ATTN_OUT_WIDTH, D), ATTN_OUT_WIDTH ** -0.5),
        "na_rpb": nrm(ks[12], (N_ATTN_LAYERS, NA_HEADS, 2 * NA_WIN_ROWS - 1, 2 * NA_WIN_COLS - 1), 0.2),
        "diff_lambda": nrm(ks[13], (N_ATTN_LAYERS, 4, DIFF_HEAD_DIM), 0.1),
        "diff_subln_g": 1.0 + nrm(ks[14], (N_ATTN_LAYERS, DIFF_V_DIM), 0.1),
        "conv_w_in": nrm(ks[15], (N_CONV_LAYERS, D, 3 * D), D ** -0.5),
        "conv_w_out": nrm(ks[16], (N_CONV_LAYERS, D, D), D ** -0.5),
        "conv_w": nrm(ks[17], (N_CONV_LAYERS, CONV_WIDTH_2, D), CONV_WIDTH_2 ** -0.5),
        "final_g": 1.0 + nrm(ks[18], (D,), 0.1),
    }

def second_block(x, c, ctx, c_ctx, mod_w, mod_b, norm_g, ffn_w_gate, ffn_w_up, ffn_w_down,
              attn_w_in, attn_w_out, na_rpb, diff_lambda, diff_subln_g,
              conv_w_in, conv_w_out, conv_w, final_g):
    n = x.shape[1]
    cos, sin = axial_rope(n)
    x_lat, x_ctx = x, ctx
    for i in range(DEPTH_2):
        last = i == DEPTH_2 - 1
        is_attn = i % 2 == 0
        ctx_live = is_attn or not last
        j = i // 2
        m = jnp.split((jax.nn.silu(c) @ mod_w[i] + mod_b[i])[:, None, :], N_MOD, axis=-1)
        if ctx_live:
            mc = jnp.split(jax.nn.silu(c_ctx) @ mod_w[i] + mod_b[i], N_MOD, axis=-1)

        x_lat = macaron_ffn(x_lat, norm_g[i, 0], m[0], m[1], m[2],
                            ffn_w_gate[i, 0], ffn_w_up[i, 0], ffn_w_down[i, 0])
        if ctx_live:
            x_ctx = macaron_ffn(x_ctx, norm_g[i, 0], mc[0], mc[1], mc[2],
                                ffn_w_gate[i, 0], ffn_w_up[i, 0], ffn_w_down[i, 0])

        xn = modulate(x_lat, norm_g[i, 1], m[3], m[4])
        if is_attn:
            xn_c = modulate(x_ctx, norm_g[i, 1], mc[3], mc[4])
            lam_init = 0.8 - 0.6 * math.exp(-0.3 * i)
            y, y_c = attn_mixer(xn, xn_c, attn_w_in[j], attn_w_out[j], na_rpb[j], diff_lambda[j],
                                diff_subln_g[j], lam_init, cos, sin, ctx_out=not last)
        else:
            y = conv_mixer(xn, conv_w_in[j], conv_w_out[j], conv_w[j])
            if not last:
                y_c = conv_mixer(modulate(x_ctx, norm_g[i, 1], mc[3], mc[4]),
                                 conv_w_in[j], conv_w_out[j], conv_w[j])
        x_lat = x_lat + m[5] * y
        if not last:
            x_ctx = x_ctx + mc[5] * y_c

        x_lat = macaron_ffn(x_lat, norm_g[i, 2], m[6], m[7], m[8],
                            ffn_w_gate[i, 1], ffn_w_up[i, 1], ffn_w_down[i, 1])
        if not last:
            x_ctx = macaron_ffn(x_ctx, norm_g[i, 2], mc[6], mc[7], mc[8],
                                ffn_w_gate[i, 1], ffn_w_up[i, 1], ffn_w_down[i, 1])
    return rmsnorm(x_lat, final_g)


def setup_inputs(seed=0):
    out = dict(first_inputs(seed))
    for name, value in second_inputs(seed + 1).items():
        if name != "x":
            out[name + "_2"] = value
    return out


def reference(
    x, mem, norm_mix_g, w_in, conv_w, conv_b, conv_ln_g, conv_ln_b, conv_w_out, hgrn_lb_logits,
    hgrn_onorm_g, hgrn_w_out, w_mix_out, norm_xa_g, norm_mem_g, xa_w_q, xa_w_k, xa_w_v, xa_w_o,
    norm_ffn_g, router_group_w, router_group_b, router_expert_w, router_expert_b, moe_w_gate,
    moe_w_up, moe_w_down, final_norm_g, c_2, ctx_2, c_ctx_2, mod_w_2, mod_b_2, norm_g_2,
    ffn_w_gate_2, ffn_w_up_2, ffn_w_down_2, attn_w_in_2, attn_w_out_2, na_rpb_2, diff_lambda_2,
    diff_subln_g_2, conv_w_in_2, conv_w_out_2, conv_w_2, final_g_2,
):
    x = first_block(
        x, mem, norm_mix_g, w_in, conv_w, conv_b, conv_ln_g, conv_ln_b, conv_w_out,
        hgrn_lb_logits, hgrn_onorm_g, hgrn_w_out, w_mix_out, norm_xa_g, norm_mem_g, xa_w_q,
        xa_w_k, xa_w_v, xa_w_o, norm_ffn_g, router_group_w, router_group_b, router_expert_w,
        router_expert_b, moe_w_gate, moe_w_up, moe_w_down, final_norm_g,
    )
    return second_block(
        x, c_2, ctx_2, c_ctx_2, mod_w_2, mod_b_2, norm_g_2, ffn_w_gate_2, ffn_w_up_2,
        ffn_w_down_2, attn_w_in_2, attn_w_out_2, na_rpb_2, diff_lambda_2, diff_subln_g_2,
        conv_w_in_2, conv_w_out_2, conv_w_2, final_g_2,
    )


_drawn_inputs = setup_inputs


def setup_inputs(seed=0):
    import zlib

    import numpy as np

    out = dict(_drawn_inputs(seed))
    spreads = {}
    factors = {'norm_mix_g': 2.85,
     'conv_ln_b': 13.709,
     'hgrn_onorm_g': 5.743,
     'norm_xa_g': 8.0,
     'norm_mem_g': 3.864,
     'router_group_b': 64.0,
     'router_expert_b': 21.376,
     'na_rpb_2': 4.899,
     'conv_b': 8.0,
     'conv_ln_g': 8.0,
     'norm_ffn_g': 8.0}
    for name, (base, spread) in spreads.items():
        noise = np.random.default_rng([zlib.crc32(name.encode()), seed]).standard_normal(out[name].shape)
        drawn = base * np.exp(spread * noise) if base else spread * noise
        out[name] = jnp.asarray(drawn.astype(out[name].dtype))
    for name, factor in factors.items():
        out[name] = (out[name] * factor).astype(out[name].dtype)
    return out
```

```python
from contextlib import ExitStack

import concourse.bass as bass
from concourse import mybir

F32 = mybir.dt.float32
U32 = mybir.dt.uint32
I32 = mybir.dt.int32
ALU = mybir.AluOpType
ACT = mybir.ActivationFunctionType
AX = mybir.AxisListType

P = 128
T = 256
TT = T // P
D = 1024
KC = D // P
CW = 512
CC = CW // P
TAPS = 31
CHUNK = 64
XH = 4
XD = D // XH
GROUPS, PER_GROUP = 4, 8
EXPERTS = GROUPS * PER_GROUP
FF = 512
PLACES = 64
FF2 = 2816
FCHUNK = 256
NCHUNK = FF2 // FCHUNK
NMOD = 9
NAH, HD = 8, 64
DH = 4
GRID = 64
KEYS = 2 * T
EPS = 1e-6
LAM_INIT = 0.2

RING = 6
UNIT = 4096

U_IN, U_CONV, U_HGRN, U_MIX = 0, 10, 11, 12
U_XQ, U_XK, U_XV, U_XO = 14, 16, 18, 20
U_MOE = 22
U_MOD = U_MOE + 3 * EXPERTS
FFN_UNITS = NCHUNK + (NCHUNK + 1) // 2
U_FFN = [0] * 5
U_FFN[0] = U_MOD + 2 * 2 * NMOD
U_FFN[1] = U_FFN[0] + FFN_UNITS
U_ATT = U_FFN[1] + FFN_UNITS
U_ATTO = U_ATT + 6
U_FFN[2] = U_ATTO + 2
U_FFN[3] = U_FFN[2] + FFN_UNITS
U_CM = U_FFN[3] + FFN_UNITS
U_CMO = U_CM + 6
U_FFN[4] = U_CMO + 2

R_MIX, R_XA, R_MEM, R_FFN = 0, 8, 16, 24
R_CONVB, R_LNG, R_LNB, R_LB, R_ONORM, R_SUBLN, R_NG2, R_C, R_CCTX, R_END = 32, 36, 40, 44, 52, 53, 54, 102, 110, 118
R2_TAPS, R2_END = 0, TAPS * CC
R3_MODB, R3_CONV2, R3_END = 0, 72, 96
R4_END = 72

SCRATCH = 14336


def program(nc, x_in, mem, norm_mix_g, w_in, conv_w, conv_b, conv_ln_g, conv_ln_b, conv_w_out, hgrn_lb_logits,
            hgrn_onorm_g, hgrn_w_out, w_mix_out, norm_xa_g, norm_mem_g, xa_w_q, xa_w_k, xa_w_v, xa_w_o, norm_ffn_g,
            router_group_w, router_group_b, router_expert_w, router_expert_b, moe_w_gate, moe_w_up, moe_w_down,
            final_norm_g, c_2, ctx_2, c_ctx_2, mod_w_2, mod_b_2, norm_g_2, ffn_w_gate_2, ffn_w_up_2, ffn_w_down_2,
            attn_w_in_2, attn_w_out_2, rpb_pad, diff_lambda_2, diff_subln_g_2, conv_w_in_2, conv_w_out_2, conv_w_2,
            final_g_2, k_mats, k_masks, k_rope, k_window, k_desc, k_rank, out):
    ctx = ExitStack()
    with ctx:
        def sb(name, shape, dt=F32):
            return ctx.enter_context(nc.sbuf_tensor(name, shape, dt))

        def sem(name):
            return ctx.enter_context(nc.semaphore(name))

        ring = sb("ring", [P, RING, UNIT])
        x = sb("x", [P, TT, D])
        side = sb("side", [P, 2, TT * D])
        cx = side[:, 0, :].rearrange("p (t d) -> p t d", t=TT)
        xn = side[:, 1, :].rearrange("p (t d) -> p t d", t=TT)
        ht = sb("ht", [P, KC, KEYS])
        scratch = sb("scratch", [P, SCRATCH])
        gate_b = sb("gate_b", [P, D])
        mats = sb("mats", [P, 3, P])
        desc = sb("desc", [P, PER_GROUP])
        cols = sb("cols", [P, 4, P])
        means = sb("means", [P, 2, P])
        tmp = sb("tmp", [P, 512])
        eps = sb("eps", [P, 1])
        overflow = sb("overflow", [P, 1], I32)
        ss = sb("ss", [P, TT])
        std = sb("std", [P, TT])
        rstd = sb("rstd", [P, TT])
        router_w = sb("router_w", [P, KC, GROUPS + EXPERTS])
        router_b = sb("router_b", [P, GROUPS + EXPERTS])
        comb = sb("comb", [P, TT, EXPERTS])
        mod = sb("mod", [P, 2, NMOD, 2, KC])
        mod_scale = sb("mod_scale", [P, 8, KC])
        silu_c = sb("silu_c", [P, KC, 32])
        small = sb("small", [P, 96])
        lbc = sb("lbc", [P, 2, CC])
        subln = sb("subln", [P, 1])
        zero = sb("zero", [P, 1])
        masks = ht[:, :, T:T + P]
        rows = tmp[:].rearrange("p (a b) -> p a b", b=P)
        cos, sin = silu_c[:].rearrange("p a b -> p (a b)"), router_w[:].rearrange("p a b -> p (a b)")[:, 0:T]
        window, lam_in = tmp[:, 0:T], tmp[:, T:2 * T].rearrange("p (a b) -> p a b", a=4)

        lo = ctx.enter_context(nc.psum_tensor("lo", [P, 4, 512], F32))
        hi = ctx.enter_context(nc.psum_tensor("hi", [P, 4, 512], F32))

        ident, flip8, rot = mats[:, 0, :], mats[:, 1, :], mats[:, 2, :]

        def part(at, *shape):
            n = 1
            for s in shape:
                n *= s
            v = scratch[:, at:at + n]
            if len(shape) == 1:
                return v
            if len(shape) == 2:
                return v.rearrange("p (a b) -> p a b", a=shape[0])
            return v.rearrange("p (a b c) -> p a b c", a=shape[0], b=shape[1])

        def htpart(at, *shape):
            v = ht[:, :, :].rearrange("p a b -> p (a b)")
            n = 1
            for s in shape:
                n *= s
            v = v[:, at:at + n]
            return v if len(shape) == 1 else v.rearrange("p (a b) -> p a b", a=shape[0])

        unit_loaded = [sem(f"unit_loaded{s}") for s in range(RING)]
        unit_used = [sem(f"unit_used{s}") for s in range(RING)]
        x_loaded, mem_loaded, ctx_loaded = sem("x_loaded"), sem("mem_loaded"), sem("ctx_loaded")
        rows_loaded, consts_loaded, bias_loaded = sem("rows_loaded"), sem("consts_loaded"), sem("bias_loaded")
        gain_loaded, out_stored = sem("gain_loaded"), sem("out_stored")
        dve_chain, act_chain = sem("dve_chain"), sem("act_chain")
        set_up = sem("set_up")
        cols_turned, cols_ready = sem("cols_turned"), sem("cols_ready")
        col_math = sem("col_math")
        norm_sq, norm_std, norm_xn = sem("norm_sq"), sem("norm_std"), sem("norm_xn")
        norm_turned, norm_ready = sem("norm_turned"), sem("norm_ready")
        x_ready, ctx_ready = sem("x_ready"), sem("ctx_ready")
        gate_turned, gate_ready = sem("gate_turned"), sem("gate_ready")

        def unit_of(n):
            return ring[:, n % RING, :]

        def as_cols(n):
            return unit_of(n).rearrange("p (k n) -> p k n", k=KC)

        def as_rows(n):
            return unit_of(n).rearrange("p (k n) -> p k n", k=4)

        def wait_unit(pe, n, i=None):
            v = n // RING + 1
            pe.wait_ge(unit_loaded[n % RING], 32 * v if i is None else (i + v) * 32)

        def wait_used(eng, n, i=None):
            v = n // RING + 1
            eng.wait_ge(unit_used[n % RING], v if i is None else i + v)

        class Link:

            def __init__(self, eng, chain):
                self.eng, self.chain, self.n = eng, chain, 0

            def __call__(self, ins):
                self.n += 1
                ins.then_inc(self.chain, 1)
                self.eng.wait_ge(self.chain, self.n)

        block = ctx.enter_context(nc.Block())

        sg, upad, acc = part(0, CC, T), part(1024, CC, 286), part(2168, CC, T)
        qT, kT, cum = part(3192, CC, T), part(4216, CC, T), part(5240, CC, T)
        eb = [part(6264, CC, T), part(0, CC, T)]
        qk = [part(7288, CC, T), part(1024, CC, T)]
        grT = part(8312, CC, T)
        vtok = side[:, 1, 0:TT * CW].rearrange("p (t n) -> p t n", t=TT)
        gcT, grT2 = part(9336, KC, T), part(11384, KC, T)
        ST = ht[:, 0:CC, 0:T].rearrange("p h (t s) -> p h t s", t=TT)
        S01 = ht[:, CC:CC + 2, 0:T].rearrange("p a (b s) -> p a b s", b=2)
        oN = part(4216, CC, T)
        reset = gate_b[:]
        merged = side[:, 1, :].rearrange("p (c t) -> p c t", c=KC)
        LEVELS = 7
        xq, xk, xv = part(0, KC, T), part(2048, KC, T), part(4096, TT, D)
        xp, xpt, xo = part(6144, XH, TT, T), part(8192, 2, 2, T), part(9216, KC, T)
        ffn_sg, ffn_h = part(0, 4, T), part(1024, 4, T)
        lg = part(4096, TT, GROUPS + EXPERTS)
        hg, onehot, weighted, back = part(0, KC, 2 * PLACES), part(1024, TT, 2, PLACES), part(1280, TT, 2, PLACES), part(1536, T)
        ex_sg, ex_h, ex_hT, ex_y = part(2048, FF), part(2560, FF), part(3072, 4, 2 * PLACES), part(5120, D)
        place, chosen, count = part(4608, TT, EXPERTS + 2), part(4736, TT, EXPERTS), part(4800, TT, EXPERTS)
        before_me, numbers = part(13440, P), part(13440 + P, PLACES)
        dn_w = part(0, 3, UNIT)
        dn_sg, dn_h = part(3 * UNIT, 4, T), part(3 * UNIT + 4 * T, 4, T)
        mrow = part(0, 3, T)
        qe, qo, kaT, va = part(0, CC, T), part(1024, CC, T), part(2048, CC, KEYS), part(4096, 4, CW)
        qbe, qbo, kbT, vb = part(6144, CC, T), part(7168, CC, T), part(8192, CC, KEYS), part(10240, 4, CW)
        ap_, apt = part(12288, 4, KEYS), htpart(3072, 4, T)
        rawq, rawk = part(12288, CC, T), part(13312, CC, T)
        rtmp = htpart(2048, CC, T)
        dO, dsq = part(0, CC, T), part(1024, CC, T)
        bias = side[:, :, :].rearrange("p a (h n) -> p (a h) n", n=T)
        mergeT = htpart(0, KC, T)
        cgs, up2, vm = part(0, KC, T), part(2048, KC, T + 2), part(4112, KC, T)

        mix_u = sem("mix_u")
        mix_cg, mix_q, mix_f, mix_v, mix_g, mix_gate = (sem("mix_" + n) for n in ("cg", "q", "f", "v", "g", "gate"))
        mix_fk, mix_ln_f, mix_scan, conv_step = (sem(n) for n in ("mix_fk", "mix_ln_f", "mix_scan", "conv_step"))
        at_zero, rope_loaded = sem("at_zero"), sem("rope_loaded")
        lev_diff, lev_exp, lev_qk, lev_s, lev_kept = (sem("lev_" + n) for n in ("diff", "exp", "qk", "s", "kept"))
        cn_mean, cn_d, cn_sq, cn_var, cn_std, cn_y, cn_act = (sem("cn_" + n) for n in ("mean", "d", "sq", "var", "std", "y", "act"))
        ho_o, ho_sq, ho_ms, ho_std, ho_n = (sem("ho_" + n) for n in ("o", "sq", "ms", "std", "n"))
        mg_conv, mg_all = sem("mg_conv"), sem("mg_all")
        xa_q, xa_k, xa_v, xa_v1, xa_s, xa_nm, xa_e, xa_p, xa_t, xa_pt, xa_pv, xa_o = (
            sem("xa_" + n) for n in ("q", "k", "v", "v1", "s", "nm", "e", "p", "t", "pt", "pv", "o"))
        rt_logits, rt_d, rt_e, rt_d2, rt_e2 = (sem("rt_" + n) for n in ("logits", "d", "e", "d2", "e2"))
        rt_comb, rt_rank, rt_flag = (sem("rt_" + n) for n in ("comb", "rank", "flag"))
        ex_onehot, ex_weighted, ex_gathered, ex_hg, ex_sgd, ex_hd, ex_turned, ex_hTd, ex_back_turned, ex_back, ex_yd, ex_done = (
            sem("ex_" + n) for n in ("onehot", "weighted", "gathered", "hg", "sg", "h", "turned", "hT", "back_turned", "back", "y", "done"))
        dn_loaded, dn_gu, dn_sgd, dn_hd, dn_down, dn_added = (sem("dn_" + n) for n in ("loaded", "gu", "sg", "h", "down", "added"))
        moe_done = sem("moe_done")
        md_rows, md_copied, md_turned, md_done, md_scales = (sem("md_" + n) for n in ("rows", "copied", "turned", "done", "scales"))
        ffn_gu, ffn_sgd, ffn_hd = sem("ffn_gu"), sem("ffn_sg"), sem("ffn_h")
        at_qa, at_ka, at_va, at_qb, at_kb, at_vb, at_rot, at_rope = (
            sem("at_" + n) for n in ("qa", "ka", "va", "qb", "kb", "vb", "rot", "rope"))
        na_bias, na_s, na_nm, na_e, na_p, na_t, na_pt, na_pv, na_o = (
            sem("na_" + n) for n in ("bias", "s", "nm", "e", "p", "t", "pt", "pv", "o"))
        df_s, df_nm, df_e, df_p, df_t, df_pt, df_pv, df_o, df_sq, df_ms, df_std, df_n = (
            sem("df_" + n) for n in ("s", "nm", "e", "p", "t", "pt", "pv", "o", "sq", "ms", "std", "n"))
        lam_d, lam_e = sem("lam_d"), sem("lam_e")
        cm_cg, cm_u, cm_bg = sem("cm_cg"), sem("cm_u"), sem("cm_bg")
        gain_used = sem("gain_used")

        @block.sync
        def _(sp):
            sp.dma_start(x[:], x_in[0].rearrange("(t p) d -> p t d", p=P)).then_inc(x_loaded, 16)

            def load(n, halves, i=None):
                if i is not None:
                    sp.wait_ge(unit_used[n % RING], i + n // RING)
                elif n >= RING:
                    sp.wait_ge(unit_used[n % RING], n // RING)
                for dst, src in halves():
                    sp.dma_start(dst, src).then_inc(unit_loaded[n % RING], 16)

            def split(v, s, half):
                return (v[:, 0:half], s[:, 0:half]), (v[:, half:2 * half], s[:, half:2 * half])

            def cols_unit(n, w, at, i=None, step=0):
                def halves():
                    cut = slice(at, at + 512) if i is None else bass.ds(i * step + at, 512)
                    return split(as_cols(n), w[:, cut].rearrange("(k p) n -> p k n", p=P), 4)
                load(n, halves, i)

            def rows_unit(n, w):
                load(n, lambda: split(as_rows(n), w.rearrange("(k p) n -> p k n", p=P), 2))

            for j in range(10):
                cols_unit(U_IN + j, w_in[0], 512 * j)
            rows_unit(U_CONV, conv_w_out[0])
            rows_unit(U_HGRN, hgrn_w_out[0])
            for u, w in ((U_MIX, w_mix_out), (U_XQ, xa_w_q), (U_XK, xa_w_k), (U_XV, xa_w_v), (U_XO, xa_w_o)):
                for j in range(2):
                    cols_unit(u + j, w[0], 512 * j)

            def expert_of(w, at):
                return w[0, at].rearrange("e (k p) n -> p (e k) n", p=P)

            with sp.Fori(0, EXPERTS // 2) as i:
                for j, w, view, half in ((0, moe_w_gate, as_cols, 4), (2, moe_w_up, as_cols, 4), (4, moe_w_down, as_rows, 2)):
                    for e in range(2):
                        n = U_MOE + j + e
                        load(n, lambda: split(view(n), expert_of(w, bass.ds(i * 2 + e, 1)), half), i)
            sp.wait_ge(rt_flag, 2)
            with sp.If(sp.value_load(overflow[0:1, 0:1], min_val=0, max_val=1)):
                with sp.Fori(0, EXPERTS) as e:
                    sp.wait_ge(dn_added, e + 1)
                    for j, w, k in ((0, moe_w_gate, KC), (1, moe_w_up, KC), (2, moe_w_down, 4)):
                        sp.dma_start(dn_w[:, j, :].rearrange("p (k n) -> p k n", k=k), expert_of(w, bass.ds(e, 1))).then_inc(dn_loaded, 16)

            for l in range(2):
                with sp.Fori(0, NMOD // 3) as i:
                    for j in range(6):
                        cols_unit(U_MOD + 18 * l + j, mod_w_2[l], 512 * j, i, 3 * D)

            def ffn_units(f, l, j):
                wg, wu, wd = ffn_w_gate_2[l, j], ffn_w_up_2[l, j], ffn_w_down_2[l, j]

                def gate_up(n, c, i=None):
                    def halves():
                        v = unit_of(n).rearrange("p (a k n) -> p a k n", a=2, k=KC)
                        cut = bass.ds(c * FCHUNK if i is None else i * (4 * FCHUNK) + c * FCHUNK, FCHUNK)
                        return tuple((v[:, a], w[:, cut].rearrange("(k p) n -> p k n", p=P)) for a, w in ((0, wg), (1, wu)))
                    load(n, halves, i)

                def down(n, c, chunks, i=None):
                    def halves():
                        size = chunks * FCHUNK
                        cut = bass.ds(c * FCHUNK if i is None else i * (4 * FCHUNK) + c * FCHUNK, size)
                        return split(as_rows(n), wd[cut, :].rearrange("(k p) n -> p k n", p=P), chunks)
                    load(n, halves, i)

                n = U_FFN[f]
                with sp.Fori(0, 2) as i:
                    for h in range(2):
                        gate_up(n + 3 * h, 2 * h, i)
                        down(n + 3 * h + 1, 2 * h, 2, i)
                        gate_up(n + 3 * h + 2, 2 * h + 1, i)
                gate_up(n + 12, 8)
                down(n + 13, 8, 2)
                gate_up(n + 14, 9)
                gate_up(n + 15, 10)
                down(n + 16, 10, 1)

            ffn_units(0, 0, 0)
            ffn_units(1, 0, 0)
            for j in range(6):
                cols_unit(U_ATT + j, attn_w_in_2[0], 512 * j)
            for j in range(2):
                cols_unit(U_ATTO + j, attn_w_out_2[0], 512 * j)
            ffn_units(2, 0, 1)
            ffn_units(3, 1, 0)
            for j, c in enumerate((2, 4, 3, 5, 0, 1)):
                cols_unit(U_CM + j, conv_w_in_2[0], 512 * c)
            for j in range(2):
                cols_unit(U_CMO + j, conv_w_out_2[0], 512 * j)
            ffn_units(4, 1, 1)
            sp.wait_ge(x_ready, 11)
            sp.dma_start(out[0].rearrange("(t p) d -> p t d", p=P), xn).then_inc(out_stored, 16)
            sp.wait_ge(out_stored, 16)

        @block.gpsimd
        def _(pool):
            vec = [(R_MIX, norm_mix_g), (R_XA, norm_xa_g), (R_MEM, norm_mem_g), (R_FFN, norm_ffn_g), (R_CONVB, conv_b),
                   (R_LNG, conv_ln_g), (R_LNB, conv_ln_b), (R_LB, hgrn_lb_logits), (R_ONORM, hgrn_onorm_g),
                   (R_SUBLN, diff_subln_g_2), (R_C, c_2)]
            pool.dma_start(mats[:], k_mats).then_inc(consts_loaded, 16)
            for at, v in vec:
                s = v.rearrange("a (c p) -> (a c) p", p=P)
                pool.dma_start(rows[at:at + s.shape[0], 0, :], s).then_inc(rows_loaded, 16)
            pool.dma_start(rows[R_NG2:R_C, 0, :], norm_g_2.rearrange("l j (c p) -> (l j c) p", p=P)).then_inc(rows_loaded, 16)
            pool.dma_start(rows[R_CCTX:R_END, 0, :], c_ctx_2.rearrange("(c p) -> c p", p=P)).then_inc(rows_loaded, 16)
            pool.dma_start(rows[0:R2_END, 1, :], conv_w[0].rearrange("j (c p) -> (j c) p", p=P)).then_inc(rows_loaded, 16)
            pool.dma_start(rows[0:R3_CONV2, 2, :], mod_b_2[0].rearrange("(c p) -> c p", p=P)).then_inc(rows_loaded, 16)
            pool.dma_start(rows[R3_CONV2:R3_END, 2, :], conv_w_2[0].rearrange("j (c p) -> (j c) p", p=P)).then_inc(rows_loaded, 16)
            pool.dma_start(rows[0:R4_END, 3, :], mod_b_2[1].rearrange("(c p) -> c p", p=P)).then_inc(rows_loaded, 16)
            for dst, src in ((masks, k_masks), (desc[:], k_desc), (scratch[:, 13440:13440 + P + PLACES], k_rank)):
                pool.dma_start(dst, src).then_inc(consts_loaded, 16)
            pool.dma_start(cx, mem[0].rearrange("(t p) d -> p t d", p=P)).then_inc(mem_loaded, 16)
            pool.dma_start(router_w[:, :, 0:GROUPS], router_group_w[0].rearrange("(k p) n -> p k n", p=P)).then_inc(consts_loaded, 16)
            pool.dma_start(router_w[:, :, GROUPS:], router_expert_w[0].rearrange("(k p) n -> p k n", p=P)).then_inc(consts_loaded, 16)
            pool.dma_start(router_b[:, 0:GROUPS], router_group_b[0].partition_broadcast(P)).then_inc(consts_loaded, 16)
            pool.dma_start(router_b[:, GROUPS:], router_expert_b[0].partition_broadcast(P)).then_inc(consts_loaded, 16)
            pool.wait_ge(mix_scan, 1)
            pool.dma_start(gate_b[:], final_norm_g.partition_broadcast(P)).then_inc(gain_loaded, 16)
            pool.wait_ge(norm_xn, 6)
            pool.dma_start(cx, ctx_2[0].rearrange("(t p) d -> p t d", p=P)).then_inc(ctx_loaded, 16)
            pool.wait_ge(x_ready, 5)
            for dst, src in ((cos, k_rope[:, 0, :]), (sin, k_rope[:, 1, :]), (window, k_window), (lam_in, diff_lambda_2[0].partition_broadcast(P))):
                pool.dma_start(dst, src).then_inc(rope_loaded, 16)
            pool.wait_ge(norm_turned, 4 * 8)
            for t in range(TT):
                for r in range(2):
                    for a in range(T // GRID):
                        src = bass.AP(rpb_pad.tensor, (7 + a - 2 * t - r) * P, [[1, GRID], [15 * P, NAH], [1, GRID]])
                        pool.dma_start(bias[GRID * r:GRID * r + GRID, t::2, GRID * a:GRID * a + GRID], src).then_inc(bias_loaded, 16)
            pool.wait_ge(x_ready, 10)
            pool.dma_start(gate_b[:], final_g_2.partition_broadcast(P)).then_inc(gain_loaded, 16)
        @block.scalar
        def _(act):
            link = Link(act, act_chain)

            def col(r, n=1, t=0):
                return cols[:, t, r:r + n]

            def norm_stats(r, src, turned):
                if turned:
                    act.wait_ge(norm_turned, turned)
                for t in range(TT):
                    act.activation(xn[:, t, :], src[:, t, :], ACT.Square, accum_out=ss[:, t:t + 1]).then_inc(norm_sq, 1)
                act.wait_ge(norm_sq, TT * (r + 1))
                act.activation(std[:], ss[:], ACT.Sqrt, bias=eps[:], scale=1.0 / D).then_inc(norm_std, 1)

            def norm_out(i, off, scale, shift=None):
                for c in range(4, KC):
                    act.wait_ge(norm_turned, 4 * i + c // 2 + 1)
                    act.activation(ht[:, c, off:off + T], hi[:, c // 2, (c % 2) * T:(c % 2 + 1) * T], ACT.Identity,
                                   scale=scale[:, c:c + 1], bias=shift[:, c:c + 1] if shift is not None else 0.0
                                   ).then_inc(norm_ready, 1)

            act.wait_ge(set_up, 5)
            act.wait_ge(x_loaded, 16)
            norm_stats(0, x, 0)
            act.wait_ge(cols_ready, 5)
            act.activation(silu_c[:, :, 0], col(R_C, KC), ACT.Silu).then_inc(col_math, 1)
            act.activation(silu_c[:, :, 1], col(R_CCTX, KC), ACT.Silu).then_inc(col_math, 1)
            act.activation(lbc[:, 0, :], small[:, 0:CC], ACT.Sigmoid).then_inc(col_math, 1)

            norm_out(0, 0, col(R_MIX, KC))

            wait_used(act, U_IN + 1)
            act.activation(sg, lo[:, 2:4, :], ACT.Sigmoid).then_inc(mix_cg, 1)
            wait_used(act, U_IN + 2)
            act.activation(qT, lo[:, 0:2, :], ACT.Silu).then_inc(mix_q, 1)
            wait_used(act, U_IN + 3)
            act.activation(cum, lo[:, 2:4, :], ACT.Sigmoid).then_inc(mix_f, 1)
            act.wait_ge(mix_fk, 1)
            act.activation(eb[0], qk[0], ACT.Ln).then_inc(mix_ln_f, 1)
            wait_used(act, U_IN + 5)
            act.activation(grT, lo[:, 2:4, :], ACT.Silu).then_inc(mix_g, 1)
            for j in range(4):
                wait_used(act, U_IN + 6 + j)
                dst = (gcT if j < 2 else grT2)[:, 4 * (j % 2):4 * (j % 2) + 4, :]
                act.activation(dst, lo[:, 2 * (j % 2):2 * (j % 2) + 2, :], ACT.Sigmoid).then_inc(mix_gate, 1)
            for v in range(1, LEVELS + 2):
                act.wait_ge(lev_diff, v)
                act.activation(eb[v % 2], eb[v % 2], ACT.Exp).then_inc(lev_exp, 1)
            act.wait_ge(cn_d, 1)
            act.activation(eb[0], acc, ACT.Square).then_inc(cn_sq, 1)
            act.wait_ge(cn_var, 1)
            act.activation(eb[1][:, 0, :], hi[:, 1, 0:T], ACT.Sqrt, bias=eps[:], scale=1.0).then_inc(cn_std, 1)
            act.wait_ge(cn_y, 1)
            for c in range(CC):
                act.activation(acc[:, c, :], acc[:, c, :], ACT.Silu, scale=col(R_LNG + c), bias=col(R_LNB + c)).then_inc(cn_act, 1)
            act.wait_ge(ho_o, 1)
            act.activation(eb[0], hi[:, 2:4, :], ACT.Square).then_inc(ho_sq, 1)
            act.wait_ge(ho_ms, 1)
            act.activation(eb[0], hi[:, 0:2, :], ACT.Sqrt, bias=eps[:], scale=1.0).then_inc(ho_std, 1)

            act.wait_ge(x_ready, 1)
            norm_stats(1, x, 4)
            norm_out(1, 0, col(R_XA, KC))
            act.wait_ge(mem_loaded, 16)
            norm_stats(2, cx, 8)
            norm_out(2, T, col(R_MEM, KC))
            for j in range(2):
                wait_used(act, U_XQ + j)
                act.activation(xq[:, 4 * j:4 * j + 4, :], lo[:, 2 * j:2 * j + 2, :], ACT.Copy).then_inc(xa_q, 1)
            wait_used(act, U_XV)
            act.activation(xv[:, :, 0:512], lo[:, 0:2, :], ACT.Copy).then_inc(xa_v, 1)
            for h in range(XH):
                act.wait_ge(xa_nm, h + 1)
                for t in range(TT):
                    act.activation(xp[:, h, t, :], hi[:, h, t * T:t * T + T], ACT.Exp, scale=XD ** -0.5,
                                   bias=small[:, 16 + 2 * h + t:17 + 2 * h + t],
                                   accum_out=small[:, 24 + 2 * h + t:25 + 2 * h + t]).then_inc(xa_e, 1)
            for h in range(XH):
                act.wait_ge(xa_t, h + 1)
                act.activation(xpt[:, h % 2], lo[:, h % 2, :], ACT.Copy).then_inc(xa_pt, 1)

            act.wait_ge(x_ready, 2)
            norm_stats(3, x, 12)
            norm_out(3, 0, col(R_FFN, KC))
            act.wait_ge(rt_d, 1)
            act.activation(part(4200, TT, GROUPS), part(4192, TT, GROUPS), ACT.Exp).then_inc(rt_e, 1)
            act.wait_ge(rt_d2, 1)
            act.activation(small[:, 34:36], small[:, 32:34], ACT.Exp).then_inc(rt_e2, 1)
            for h in range(2):
                act.activation(ex_y[:, h * 512:h * 512 + 512], zero[:].broadcast_to([P, 512]), ACT.Copy).then_inc(ex_yd, 1)
            act.activation(back, zero[:].broadcast_to([P, T]), ACT.Copy).then_inc(ex_back, 1)
            with act.Fori(0, EXPERTS // 2) as i:
                for e in range(2):
                    wait_used(act, U_MOE + e, i)
                act.activation(ex_sg, lo[:, 0, :], ACT.Silu).then_inc(ex_sgd, 1)
                act.wait_ge(ex_turned, i + 1)
                act.activation(ex_hT, lo[:, 0, :], ACT.Copy).then_inc(ex_hTd, 1)
                act.wait_ge(ex_back_turned, i + 2)
                act.activation(back, lo[:, 1, 0:T], ACT.Copy).then_inc(ex_back, 1)
                for e in range(2):
                    wait_used(act, U_MOE + 4 + e, i)
                for h in range(2):
                    act.activation(ex_y[:, h * 512:h * 512 + 512], lo[:, 2 + h, :], ACT.Copy).then_inc(ex_yd, 1)
            act.wait_ge(rt_flag, 2)
            with act.If(act.value_load(overflow[0:1, 0:1], min_val=0, max_val=1)):
                with act.Fori(0, EXPERTS) as e:
                    for f in range(4):
                        act.wait_ge(dn_gu, e * 4 + (f + 1))
                        act.activation(dn_sg[:, f, :], lo[:, f, 0:T], ACT.Silu).then_inc(dn_sgd, 1)

            act.wait_ge(x_ready, 3)
            norm_stats(4, x, 16)

            def ffn(f, i, r, src, ready, at, scale, shift, half_gate):
                act.wait_ge(*ready)
                norm_stats(r, src, 4 * i)
                norm_out(i, 0, scale, shift)
                gate(half_gate, 0.5)
                with act.Fori(0, NCHUNK) as c:
                    for b in range(2):
                        act.wait_ge(ffn_gu, c * 2 + (2 * NCHUNK * f + b + 1))
                        act.activation(ffn_sg[:, b, :], lo[:, b, 0:T], ACT.Silu).then_inc(ffn_sgd, 1)

            def gate(g, scale):
                act.wait_ge(gate_turned, g + 1)
                act.wait_ge(gain_used, g + 1)
                act.activation(gate_b[:], lo[:, 2:4, :], ACT.Copy, scale=scale).then_inc(gate_ready, 1)

            act.wait_ge(md_scales, 1)
            act.wait_ge(ctx_loaded, 16)
            ffn(0, 4, 5, cx, (ctx_loaded, 16), 0, mod_scale[:, 0], mod[:, 0, 0, 1], 0)
            ffn(1, 5, 6, x, (x_ready, 4), 1, mod_scale[:, 1], mod[:, 0, 0, 0], 1)

            act.wait_ge(x_ready, 5)
            norm_stats(7, x, 24)
            norm_out(6, 0, mod_scale[:, 2], mod[:, 0, 3, 0])
            act.wait_ge(ctx_ready, 1)
            norm_stats(8, cx, 28)
            norm_out(7, T, mod_scale[:, 3], mod[:, 0, 3, 1])
            wait_used(act, U_ATT)
            act.activation(qe[0:HD], lo[0:HD, 0:2, :], ACT.Copy).then_inc(at_qa, 1)
            act.activation(qo[HD:P], lo[HD:P, 0:2, :], ACT.Copy).then_inc(at_qa, 1)
            wait_used(act, U_ATT + 1)
            act.activation(kaT, hi[:, :, :], ACT.Copy).then_inc(at_ka, 1)
            wait_used(act, U_ATT + 3)
            act.activation(rawq, hi[:, 0:2, :], ACT.Copy).then_inc(at_qb, 1)
            wait_used(act, U_ATT + 4)
            act.activation(rawk, lo[:, :, 0:T], ACT.Copy).then_inc(at_kb, 1)
            act.activation(kbT[:, :, T:KEYS], lo[:, :, T:KEYS], ACT.Copy).then_inc(at_kb, 1)
            wait_used(act, U_ATT + 5)
            act.activation(vb, hi[:, :, :], ACT.Copy).then_inc(at_vb, 1)
            gate(2, 1.0)
            act.wait_ge(lam_d, 1)
            act.activation(small[:, 42:44], small[:, 40:42], ACT.Exp).then_inc(lam_e, 1)
            act.wait_ge(at_rope, 3)

            def na_exp(h):
                b = 2 * (h % 2)
                act.wait_ge(na_nm, h + 1)
                for t in range(TT):
                    act.activation(ap_[:, b + t, :], hi[:, b + t, :], ACT.Exp, scale=HD ** -0.5,
                                   bias=small[:, 48 + b + t:49 + b + t],
                                   accum_out=small[:, 52 + b + t:53 + b + t]).then_inc(na_e, 1)

            def na_copy(h):
                act.wait_ge(na_t, h + 1)
                act.activation(apt, lo[:, 0:2, :], ACT.Copy).then_inc(na_pt, 1)

            na_exp(0)
            for h in range(NAH):
                if h + 1 < NAH:
                    na_exp(h + 1)
                na_copy(h)
            for h in range(DH):
                act.wait_ge(df_nm, h + 1)
                for m in range(4):
                    act.activation(ap_[:, m, :], hi[:, m, :], ACT.Exp, scale=HD ** -0.5, bias=small[:, 48 + m:49 + m],
                                   accum_out=small[:, 52 + m:53 + m]).then_inc(df_e, 1)
                act.wait_ge(df_t, h + 1)
                act.activation(apt, lo[:, 0:2, :], ACT.Copy).then_inc(df_pt, 1)
            act.wait_ge(df_o, DH)
            act.activation(dsq, dO, ACT.Square).then_inc(df_sq, 1)
            act.wait_ge(df_ms, 1)
            act.activation(dsq, hi[:, 0:2, :], ACT.Sqrt, bias=eps[:], scale=1.0).then_inc(df_std, 1)

            ffn(2, 8, 9, x, (x_ready, 6), 2, mod_scale[:, 4], mod[:, 0, 6, 0], 3)
            ffn(3, 9, 10, x, (x_ready, 7), 3, mod_scale[:, 5], mod[:, 1, 0, 0], 4)

            act.wait_ge(x_ready, 8)
            norm_stats(11, x, 40)
            norm_out(10, 0, mod_scale[:, 6], mod[:, 1, 3, 0])
            for j in range(2):
                wait_used(act, U_CM + 2 * j)
                act.activation(cgs[:, 4 * j:4 * j + 4, :], (hi if j else lo)[:, 0:2, :], ACT.Copy).then_inc(cm_cg, 1)
            gate(5, 1.0)
            ffn(4, 11, 12, x, (x_ready, 9), 4, mod_scale[:, 7], mod[:, 1, 6, 0], 6)

            act.wait_ge(x_ready, 10)
            norm_stats(13, x, 48)

        @block.tensor
        def _(pe):
            def mm(dst, lhsT, rhs, start=True, stop=True, **kw):
                return pe.matmul(dst, lhsT, rhs, start=start, stop=stop, **kw)

            def to_features(n, dst, rhs, chunks, last=True):
                for f in range(4):
                    for k in range(chunks):
                        ins = mm(dst(f), as_cols(n)[:, k, f * P:f * P + P], rhs(k), k == 0, k == chunks - 1)
                ins.then_inc(unit_used[n % RING], 1)

            def to_rows(n, dst, lhsT, tiles=TT):
                for t in range(tiles):
                    for k in range(KC):
                        ins = mm(dst(t), lhsT(k, t), as_cols(n)[:, k, :], k == 0, k == KC - 1)
                ins.then_inc(unit_used[n % RING], 1)

            def pair(ps, b):
                return lambda f: ps[:, b + f // 2, (f % 2) * T:(f % 2 + 1) * T]

            def norm(i):
                for c in range(KC):
                    for t in range(TT):
                        if c == 0:
                            pe.wait_ge(norm_xn, TT * i + t + 1)
                        ins = pe.transpose(hi[:, c // 2, (c % 2) * T + t * P:(c % 2) * T + t * P + P], xn[:, t, c * P:c * P + P], ident)
                    if c % 2:
                        ins.then_inc(norm_turned, 1)

            def normed(i):
                pe.wait_ge(norm_ready, KC * (i + 1))

            def ht_all(k):
                return ht[:, k, 0:T]

            def ht_tile(k, t):
                return ht[:, k, t * P:t * P + P]

            pe.wait_ge(consts_loaded, 16 * 8)
            pe.wait_ge(rows_loaded, 16 * 17)
            for t, n in enumerate((R_END, R2_END, R3_END, R4_END)):
                ins = pe.transpose(lo[:, 0, t * P:t * P + n], rows[0:n, t, :], ident[0:n, 0:n])
            ins.then_inc(cols_turned, 1)
            norm(0)
            normed(0)
            pe.wait_ge(cols_ready, 4)

            before = [None, None, (mix_u, 1), (mix_cg, 1), (mix_q, 1), (mix_f, 1), (mix_v, 1), (mix_g, 1), (mix_gate, 1), (mix_gate, 2)]
            for j in range(10):
                n = U_IN + j
                wait_unit(pe, n)
                if before[j]:
                    pe.wait_ge(*before[j])
                if j == 4:
                    to_rows(n, lambda t: lo[:, t, :], ht_tile)
                else:
                    to_features(n, pair(lo, 2 * (j % 2)), ht_all, KC)

            def blocks(b):
                return lambda h, t: lo[:, b + h // 2, (h % 2) * T + t * P:(h % 2) * T + t * P + P]

            pe.wait_ge(mix_fk, 1)
            pe.wait_ge(mix_gate, 3)
            for h in range(CC):
                for t in range(TT):
                    ins = mm(blocks(0)(h, t), kT[:, h, t * P:t * P + P], qT[:, h, t * P:t * P + P])
            ins.then_inc(lev_s, 1)
            for v in range(1, LEVELS + 1):
                pe.wait_ge(lev_qk, v)
                if v == 1:
                    pe.wait_ge(mix_gate, 4)
                else:
                    pe.wait_ge(lev_kept, v - 1)
                for h in range(CC):
                    for t in range(TT):
                        z = qk[v % 2][:, h, t * P:t * P + P]
                        ins = mm(blocks(2 * (v % 2))(h, t), z, z)
                ins.then_inc(lev_s, 1)
            pe.wait_ge(lev_qk, LEVELS + 1)
            pe.wait_ge(lev_kept, LEVELS)
            for h in range(CC):
                ins = mm(lo[:, 0, h * P:h * P + P], qk[0][:, h, 0:P], qk[0][:, h, P:T])
            ins.then_inc(lev_s, 1)
            for c in range(CC):
                if c == 0:
                    pe.wait_ge(conv_step, TAPS * CC)
                ins = mm(hi[:, 0, 0:T], means[:, 0, :], acc[:, c, :], c == 0, c == CC - 1)
            ins.then_inc(cn_mean, 1)
            pe.wait_ge(cn_sq, 1)
            for c in range(CC):
                ins = mm(hi[:, 1, 0:T], means[:, 0, :], eb[0][:, c, :], c == 0, c == CC - 1)
            ins.then_inc(cn_var, 1)
            pe.wait_ge(lev_kept, LEVELS + 2)
            pe.wait_ge(mix_v, 1)
            for h in range(CC):
                o = hi[:, 2 + h // 2, (h % 2) * T:(h % 2 + 1) * T]
                v0, v1 = vtok[:, 0, h * P:h * P + P], vtok[:, 1, h * P:h * P + P]
                mm(o[:, 0:P], v0, ST[:, h, 0, :])
                mm(o[:, P:T], v0, S01[:, h // 2, h % 2, :], True, False)
                ins = mm(o[:, P:T], v1, ST[:, h, 1, :], False, True)
            ins.then_inc(ho_o, 1)
            wait_unit(pe, U_CONV)
            pe.wait_ge(cn_act, CC)

            def wide(n, dst, rhs):
                for f in range(KC):
                    for k in range(CC):
                        ins = mm(dst[:, f // 2, (f % 2) * T:(f % 2 + 1) * T], as_rows(n)[:, k, f * P:f * P + P], rhs[:, k, :], k == 0, k == CC - 1)
                ins.then_inc(unit_used[n % RING], 1)

            wide(U_CONV, lo, acc)
            pe.wait_ge(ho_sq, 1)
            pe.wait_ge(cn_std, 1)
            for b in range(2):
                ins = mm(hi[:, b, :], means[:, 1, :], eb[0][:, 2 * b:2 * b + 2, :])
            ins.then_inc(ho_ms, 1)
            wait_unit(pe, U_HGRN)
            pe.wait_ge(ho_n, 1)
            wide(U_HGRN, hi, oN)
            pe.wait_ge(mg_all, 1)
            for j in range(2):
                wait_unit(pe, U_MIX + j)
                to_rows(U_MIX + j, lambda t: hi[:, 2 * t + j, :], lambda k, t: merged[:, k, t * P:t * P + P])

            norm(1)
            normed(1)
            norm(2)
            for j in range(2):
                wait_unit(pe, U_XQ + j)
                if j == 0:
                    pe.wait_ge(mg_conv, 1)
                to_features(U_XQ + j, pair(lo, 2 * j), ht_all, KC)
            normed(2)
            for j in range(2):
                wait_unit(pe, U_XK + j)
                to_features(U_XK + j, pair(hi, 2 * j), lambda k: ht[:, k, T:KEYS], KC)
            for j in range(2):
                wait_unit(pe, U_XV + j)
                pe.wait_ge(xa_q, j + 1)
                to_rows(U_XV + j, lambda t: lo[:, 2 * j + t, :], lambda k, t: ht[:, k, T + t * P:T + t * P + P])
            pe.wait_ge(xa_k, 2)
            for h in range(XH):
                for t in range(TT):
                    for d in range(2):
                        ins = mm(hi[:, h, t * T:t * T + T], xq[:, 2 * h + d, t * P:t * P + P], xk[:, 2 * h + d, :], d == 0, d == 1)
                ins.then_inc(xa_s, 1)

            def xa_turn(h):
                pe.wait_ge(xa_p, TT * (h + 1))
                for t in range(TT):
                    for m in range(2):
                        ins = pe.transpose(lo[:, h % 2, m * T + t * P:m * T + t * P + P], xp[:, h, t, m * P:m * P + P], ident)
                ins.then_inc(xa_t, 1)

            def xa_value(h):
                pe.wait_ge(xa_pt, h + 1)
                if h >= 2:
                    pe.wait_ge(xa_o, h - 1)
                for d in range(2):
                    for m in range(2):
                        c = h * XD + d * P
                        ins = mm(lo[:, 2 + h % 2, d * T:d * T + T], xv[:, m, c:c + P], xpt[:, h % 2, m, :], m == 0, m == 1)
                ins.then_inc(xa_pv, 1)

            pe.wait_ge(xa_v, 1)
            pe.wait_ge(xa_v1, 1)
            xa_turn(0)
            for h in range(XH):
                if h + 1 < XH:
                    xa_turn(h + 1)
                xa_value(h)
            pe.wait_ge(xa_o, XH)
            for j in range(2):
                wait_unit(pe, U_XO + j)
                to_rows(U_XO + j, lambda t: hi[:, 2 * t + j, :], lambda k, t: xo[:, k, t * P:t * P + P])

            norm(3)
            normed(3)
            for t in range(TT):
                for k in range(KC):
                    ins = mm(lo[:, 0, t * 64:t * 64 + GROUPS + EXPERTS], ht_tile(k, t), router_w[:, k, :], k == 0, k == KC - 1)
            ins.then_inc(rt_logits, 1)
            pe.wait_ge(rt_comb, 1)
            ranks, counts = lo[:, 1, 0:TT * EXPERTS].rearrange("p (t n) -> p t n", t=TT), lo[:, 1, TT * EXPERTS:(TT + 1) * EXPERTS]
            mm(ranks[:, 0, :], before_me, chosen[:, 0, :])
            mm(ranks[:, 1, :], before_me, chosen[:, 1, :], True, False)
            mm(ranks[:, 1, :], means[:, 0, :], chosen[:, 0, :], False, True)
            for t in range(TT):
                ins = mm(counts, means[:, 0, :], chosen[:, t, :], t == 0, t == 1)
            ins.then_inc(rt_rank, 1)
            for t in range(TT):
                for h in range(2):
                    ins = mm(hi[:, 2 * t + h, :], zero[:].broadcast_to([P, P]), x[:, 0, 0:512], True, False, skip_group_check=True)
            ins.then_inc(ex_back_turned, 1)

            def gather():
                for c in range(KC):
                    for t in range(TT):
                        ins = mm(lo[:, 2 + c // 4, (c % 4) * P:(c % 4 + 1) * P], xn[:, t, c * P:c * P + P], onehot[:, t], t == 0, t == 1)
                    if c % 4 == 3:
                        ins.then_inc(ex_gathered, 1)

            def scatter(last):
                for t in range(TT):
                    for h in range(2):
                        ins = mm(hi[:, 2 * t + h, :], back[:, t * P:t * P + P], ex_y[:, h * 512:h * 512 + 512], False, last, skip_group_check=True)
                return ins

            pe.wait_ge(ex_onehot, 1)
            gather()
            with pe.Fori(0, EXPERTS // 2) as i:
                def places(e, n, bank, lhsT, k, rhs, chunks):
                    ins = mm(lo[PLACES * e:PLACES * e + PLACES, bank, :], lhsT[:, k, PLACES * e:PLACES * e + PLACES], rhs,
                             k == 0, k == chunks - 1, tile_position=(0, PLACES * e))
                    return ins

                pe.wait_ge(ex_hg, i * 2 + 2)
                for bank in range(2):
                    n = U_MOE + 2 * bank
                    if bank == 1:
                        pe.wait_ge(ex_back, i + 1)
                    for e in range(2):
                        wait_unit(pe, n + e, i)
                    for k in range(KC):
                        for e in range(2):
                            ins = places(e, n + e, bank, hg, k, as_cols(n + e)[:, k, :], KC)
                            if k == KC - 1:
                                ins.then_inc(unit_used[(n + e) % RING], 1)
                pe.wait_ge(ex_yd, i * 2 + 2)
                scatter(False)
                pe.wait_ge(ex_onehot, i + 2)
                gather()
                pe.wait_ge(ex_hd, i + 1)
                for f in range(4):
                    ins = pe.transpose(lo[:, 0, f * P:f * P + P], ex_h[:, f * P:f * P + P], ident)
                ins.then_inc(ex_turned, 1)
                pe.wait_ge(ex_weighted, i + 1)
                for t in range(TT):
                    ins = pe.transpose(lo[:, 1, t * P:t * P + P], weighted[:, t].rearrange("p e s -> p (e s)"), ident)
                ins.then_inc(ex_back_turned, 1)
                pe.wait_ge(ex_hTd, i + 1)
                pe.wait_ge(ex_hg, i * 2 + 4)
                n = U_MOE + 4
                for e in range(2):
                    wait_unit(pe, n + e, i)
                for h in range(2):
                    for k in range(4):
                        for e in range(2):
                            ins = places(e, n + e, 2 + h, ex_hT, k, as_rows(n + e)[:, k, h * 512:h * 512 + 512], 4)
                            if h == 1 and k == 3:
                                ins.then_inc(unit_used[(n + e) % RING], 1)
            pe.wait_ge(ex_yd, EXPERTS + 2)
            pe.wait_ge(ex_back, EXPERTS // 2 + 1)
            scatter(True).then_inc(ex_done, 1)
            pe.wait_ge(rt_flag, 2)
            with pe.If(pe.value_load(overflow[0:1, 0:1], min_val=0, max_val=1)):
                with pe.Fori(0, EXPERTS) as e:
                    pe.wait_ge(dn_loaded, e * 48 + 48)
                    for f in range(4):
                        for j in range(2):
                            w = dn_w[:, j, :].rearrange("p (k n) -> p k n", k=KC)
                            for k in range(KC):
                                ins = mm(lo[:, f, j * T:j * T + T], w[:, k, f * P:f * P + P], ht_all(k), k == 0, k == KC - 1)
                        ins.then_inc(dn_gu, 1)
                    w = dn_w[:, 2, :].rearrange("p (k n) -> p k n", k=4)
                    for f in range(4):
                        pe.wait_ge(dn_hd, e * 4 + (f + 1))
                        for t in range(TT):
                            for h in range(2):
                                ins = mm(hi[:, 2 * t + h, :], dn_h[:, f, t * P:t * P + P], w[:, f, h * 512:h * 512 + 512], f == 0, f == 3)
                    ins.then_inc(dn_down, 1)

            pe.wait_ge(moe_done, 1)
            for l in range(2):
                with pe.Fori(0, NMOD // 3) as i:
                    for b in range(3):
                        for j in range(2):
                            n = U_MOD + 18 * l + 2 * b + j
                            wait_unit(pe, n, i)
                            for k in range(KC):
                                for h in range(2):
                                    g = 2 * j + h
                                    ins = mm(lo[32 * g:32 * g + 32, b, 0:T], silu_c[:, k, :], as_cols(n)[:, k, h * T:h * T + T],
                                             k == 0, k == KC - 1, tile_position=(0, 32 * g))
                            ins.then_inc(unit_used[n % RING], 1)
                        pe.wait_ge(md_copied, i * 3 + (9 * l + b + 1))
                        for h in range(2):
                            ins = pe.transpose(hi[:, b, h * P:h * P + P], mrow[:, b, h * P:h * P + P], ident)
                        ins.then_inc(md_turned, 1)
            pe.wait_ge(md_scales, 1)

            def gate(l, i, v):
                for c in range(KC):
                    ins = mm(lo[:, 2 + c // 4, (c % 4) * P:(c % 4 + 1) * P], mod[:, l, i, v, c:c + 1].broadcast_to([P, P]), ident)
                ins.then_inc(gate_turned, 1)

            def ffn(f, i, l, m, v):
                norm(i)
                gate(l, m, v)
                normed(i)

                def up(n, c, it=None):
                    wait_unit(pe, n, it)
                    w = unit_of(n).rearrange("p (a k n) -> p a k n", a=2, k=KC)
                    for b in range(2):
                        for a in range(2):
                            for k in range(KC):
                                ins = mm(lo[:, b, a * T:a * T + T], w[:, a, k, b * P:b * P + P], ht_all(k), k == 0, k == KC - 1)
                        ins.then_inc(ffn_gu, 1)

                def down(n, nu, c, r, first, last, it=None):
                    for b in range(2):
                        done = 2 * NCHUNK * f + b + 1
                        pe.wait_ge(ffn_hd, done + 2 * c if it is None else it * 8 + (done + 2 * c))
                        if b == 0:
                            wait_unit(pe, n, it)
                        for t in range(TT):
                            for h in range(2):
                                ins = mm(hi[:, 2 * t + h, :], ffn_h[:, b, t * P:t * P + P], as_rows(n)[:, r + b, h * 512:h * 512 + 512],
                                         first and b == 0, last and b == 1, skip_group_check=True)
                                if b == 0 and t == 0 and h == 0:
                                    ins.then_inc(unit_used[nu % RING], 1)
                    return ins

                n = U_FFN[f]
                for t in range(TT):
                    for h in range(2):
                        mm(hi[:, 2 * t + h, :], zero[:].broadcast_to([P, P]), x[:, 0, 0:512], True, False, skip_group_check=True)
                with pe.Fori(0, 2) as it:
                    for h in range(2):
                        for e in range(2):
                            c = 2 * h + e
                            up(n + 3 * h + 2 * e, c, it)
                            ins = down(n + 3 * h + 1, n + 3 * h + 2 * e, c, 2 * e, False, False, it)
                        ins.then_inc(unit_used[(n + 3 * h + 1) % RING], 1)
                up(n + 12, 8)
                down(n + 13, n + 12, 8, 0, False, False)
                up(n + 14, 9)
                down(n + 13, n + 14, 9, 2, False, False).then_inc(unit_used[(n + 13) % RING], 1)
                up(n + 15, 10)
                down(n + 16, n + 15, 10, 0, False, True).then_inc(unit_used[(n + 16) % RING], 1)

            ffn(0, 4, 0, 2, 1)
            ffn(1, 5, 0, 2, 0)

            norm(6)
            normed(6)
            norm(7)
            wait_unit(pe, U_ATT)
            to_features(U_ATT, pair(lo, 0), ht_all, KC)
            normed(7)
            both = lambda k: ht[:, k, :]
            keys = lambda k, t: ht[:, k, t * P:t * P + P]
            wait_unit(pe, U_ATT + 1)
            to_features(U_ATT + 1, lambda f: hi[:, f, :], both, KC)
            wait_unit(pe, U_ATT + 2)
            pe.wait_ge(at_qa, 2)
            to_rows(U_ATT + 2, lambda t: lo[:, t, :], keys, 4)
            wait_unit(pe, U_ATT + 3)
            pe.wait_ge(at_ka, 1)
            to_features(U_ATT + 3, pair(hi, 0), ht_all, KC)
            wait_unit(pe, U_ATT + 4)
            pe.wait_ge(at_va, 1)
            to_features(U_ATT + 4, lambda f: lo[:, f, :], both, KC)
            wait_unit(pe, U_ATT + 5)
            pe.wait_ge(at_qb, 1)
            to_rows(U_ATT + 5, lambda t: hi[:, t, :], keys, 4)
            pe.wait_ge(at_kb, 2)
            for b in range(2):
                ins = mm(lo[:, b, :], rot, rawq[:, 2 * b:2 * b + 2, :])
            ins.then_inc(at_rot, 1)
            for b in range(2):
                ins = mm(lo[:, 2 + b, :], rot, rawk[:, 2 * b:2 * b + 2, :])
            ins.then_inc(at_rot, 1)
            pe.wait_ge(at_rope, 3)
            gate(0, 5, 0)

            pe.wait_ge(at_zero, 4)
            pe.wait_ge(na_bias, 1)
            pe.wait_ge(at_vb, 1)

            def na_score(h):
                if h >= 2:
                    pe.wait_ge(na_e, TT * (h - 1))
                b = 2 * (h % 2)
                for t in range(TT):
                    mm(hi[:, b + t, :], (qo if h % 2 else qe)[:, h // 2, t * P:t * P + P], kaT[:, h // 2, :], True, False)
                    ins = mm(hi[:, b + t, 0:T], flip8, bias[:, 2 * h + t, :], False, True)
                ins.then_inc(na_s, 1)

            def turn(h, rows_of, ready, done):
                pe.wait_ge(*ready)
                for t in range(TT):
                    for c in range(4):
                        at = c * T + t * P
                        ins = pe.transpose(lo[:, at // 512, at % 512:at % 512 + P], rows_of(t)[:, c * P:c * P + P], ident)
                ins.then_inc(done, 1)

            na_score(0)
            for h in range(NAH):
                if h + 1 < NAH:
                    na_score(h + 1)
                turn(h, lambda t: ap_[:, 2 * (h % 2) + t, :], (na_p, TT * (h + 1)), na_t)
                pe.wait_ge(na_pt, h + 1)
                if h == 0:
                    pe.wait_ge(gate_ready, 3)
                if h >= 4 and h % 2 == 0:
                    pe.wait_ge(na_o, h // 2 - 1)
                at = HD * (h % 2)
                for c in range(4):
                    ins = mm(lo[at:at + HD, 2 + (h // 2) % 2, 0:T], va[:, c, h * HD:h * HD + HD], apt[:, c, :], c == 0, c == 3,
                             tile_position=(0, at))
                ins.then_inc(na_pv, 1)

            for h in range(DH):
                pe.wait_ge(na_e, TT * NAH)
                if h:
                    pe.wait_ge(df_e, 4 * h)
                for m in range(2):
                    for t in range(TT):
                        ins = mm(hi[:, 2 * m + t, :], (qbo if m else qbe)[:, h, t * P:t * P + P], kbT[:, h, :])
                ins.then_inc(df_s, 1)
                turn(h, lambda t: ap_[:, t, :], (df_p, TT * (h + 1)), df_t)
                pe.wait_ge(df_pt, h + 1)
                pe.wait_ge(na_o, 4)
                if h >= 2:
                    pe.wait_ge(df_o, h - 1)
                for c in range(4):
                    ins = mm(lo[:, 2 + h % 2, 0:T], vb[:, c, h * P:h * P + P], apt[:, c, :], c == 0, c == 3)
                ins.then_inc(df_pv, 1)
            pe.wait_ge(df_sq, 1)
            for b in range(2):
                ins = mm(hi[:, b, :], means[:, 1, :], dsq[:, 2 * b:2 * b + 2, :])
            ins.then_inc(df_ms, 1)
            pe.wait_ge(df_n, 1)
            for j in range(2):
                wait_unit(pe, U_ATTO + j)
                to_rows(U_ATTO + j, lambda t: hi[:, 2 * t + j, :], lambda k, t: mergeT[:, k, t * P:t * P + P])

            ffn(2, 8, 0, 8, 0)
            ffn(3, 9, 1, 2, 0)

            norm(10)
            normed(10)
            for j, b in enumerate((lo[:, 0:2], lo[:, 2:4], hi[:, 0:2], hi[:, 2:4], lo[:, 0:2], lo[:, 2:4])):
                wait_unit(pe, U_CM + j)
                if j >= 4:
                    pe.wait_ge(cm_u, 1)
                to_features(U_CM + j, pair(b, 0), ht_all, KC)
            pe.wait_ge(cm_bg, 2)
            gate(1, 5, 0)
            for j in range(2):
                wait_unit(pe, U_CMO + j)
                to_rows(U_CMO + j, lambda t: hi[:, 2 * t + j, :], lambda k, t: vm[:, k, t * P:t * P + P])
            ffn(4, 11, 1, 8, 0)

        @block.vector
        def _(dve):
            link = Link(dve, dve_chain)
            tt, ts, stt = dve.tensor_tensor, dve.tensor_scalar, dve.scalar_tensor_tensor

            def col(r, n=1, t=0):
                return cols[:, t, r:r + n]

            def rstd_of(r):
                dve.wait_ge(norm_std, r + 1)
                link(dve.reciprocal(rstd[:], std[:]))

            def norm(i, r, src, off, scale, shift=None):
                rstd_of(r)
                for t in range(TT):
                    ts(xn[:, t, :], src[:, t, :], rstd[:, t:t + 1], None, ALU.mult).then_inc(norm_xn, 1)
                for c in range(4):
                    dve.wait_ge(norm_turned, 4 * i + c // 2 + 1)
                    ps = hi[:, c // 2, (c % 2) * T:(c % 2 + 1) * T]
                    if shift is None:
                        ins = ts(ht[:, c, off:off + T], ps, scale[:, c:c + 1], None, ALU.mult)
                    else:
                        ins = ts(ht[:, c, off:off + T], ps, scale[:, c:c + 1], shift[:, c:c + 1], ALU.mult, ALU.add)
                    ins.then_inc(norm_ready, 1)

            def residual(n, dst, signal, gated=False):
                last = None
                for j in range(2):
                    if len(n) > j:
                        wait_used(dve, n[j])
                    for t in range(TT):
                        ps, xs = hi[:, 2 * t + j, :], dst[:, t, j * 512:j * 512 + 512]
                        if gated:
                            link(tt(tmp[:], ps, gate_b[:, j * 512:j * 512 + 512], ALU.mult))
                            ps = tmp[:]
                        last = tt(xs, ps, xs, ALU.add)
                        if gated and (j, t) != (1, 1):
                            link(last)
                if gated:
                    link(last)
                    tt(tmp[:, 0:1], eps[:], eps[:], ALU.add).then_inc(gain_used, 1)
                    tt(tmp[:, 1:2], eps[:], eps[:], ALU.add).then_inc(signal, 1)
                else:
                    last.then_inc(signal, 1)


            dve.memset(eps[:], EPS).then_inc(set_up, 1)
            dve.memset(means[:, 0, :], 1.0 / CW).then_inc(set_up, 1)
            dve.memset(means[:, 1, :], 1.0 / P).then_inc(set_up, 1)
            dve.memset(silu_c[:], 0.0).then_inc(set_up, 1)
            dve.memset(upad[:, :, 0:TAPS - 1], 0.0).then_inc(set_up, 1)
            link(dve.memset(reset, 1.0))
            link(dve.memset(gate_b[:, 0::CHUNK], 0.0))
            link(dve.memset(zero[:], 0.0))

            dve.wait_ge(cols_turned, 1)
            for t, n in enumerate((R_END, R2_END, R3_END, R4_END)):
                dve.tensor_copy(cols[:, t, 0:n], lo[:, 0, t * P:t * P + n]).then_inc(cols_ready, 1)
            dve.wait_ge(cols_ready, 4)
            tt(small[:, 0:CC], col(R_LB, CC), col(R_LB + CC, CC), ALU.subtract).then_inc(cols_ready, 1)
            link(ts(subln[:], col(R_SUBLN), 1.0 - LAM_INIT, None, ALU.mult))
            norm(0, 0, x, 0, col(R_MIX, KC))
            dve.wait_ge(col_math, 3)
            link(ts(lbc[:, 1, :], lbc[:, 0, :], -1.0, 1.0, ALU.mult, ALU.add))

            dve.wait_ge(mix_cg, 1)
            wait_used(dve, U_IN)
            tt(upad[:, :, TAPS - 1:TAPS - 1 + T], lo[:, 0:2, :].rearrange("p a (b t) -> p (a b) t", b=2), sg, ALU.mult).then_inc(mix_u, 1)
            dve.wait_ge(mix_f, 1)
            for c in range(CC):
                link(ts(qk[0][:, c, :], cum[:, c, :], lbc[:, 1, c:c + 1], lbc[:, 0, c:c + 1], ALU.mult, ALU.add))
            ts(kT, qk[0], -1.0, 1.0, ALU.mult, ALU.add).then_inc(mix_fk, 1)
            wait_used(dve, U_IN + 4)
            dve.tensor_copy(vtok, lo[:, 0:2, :]).then_inc(mix_v, 1)
            dve.wait_ge(mix_ln_f, 1)
            dve.wait_ge(mix_fk, 1)
            dve.tensor_tensor_scan(cum.rearrange("p a b -> p (a b)"), reset, eb[0].rearrange("p a b -> p (a b)"), 0.0, ALU.mult, ALU.add
                                   ).then_inc(mix_scan, 1)
            dve.wait_ge(mix_u, 1)
            for c in range(CC):
                ts(acc[:, c, :], upad[:, c, 0:T], col(R2_TAPS + c, 1, 1), col(R_CONVB + c), ALU.mult, ALU.add).then_inc(conv_step, 1)
            with dve.Fori(1, TAPS) as j:
                for c in range(CC):
                    dve.wait_ge(conv_step, j * CC + (c + 1 - CC))
                    stt(acc[:, c, :], upad[:, c, bass.ds(j, T)], cols[:, 1, bass.ds(j * CC + c, 1)], acc[:, c, :], ALU.mult, ALU.add
                        ).then_inc(conv_step, 1)
            dve.wait_ge(mix_scan, 1)
            wait_used(dve, U_IN + 9)
            link(dve.memset(ST, 0.0))

            def halves(a, v):
                return a.rearrange("p h t -> p (h t)").rearrange("p (n a l) -> p n a l", a=2, l=1 << (v - 1))

            def diff(v):
                e = eb[v % 2]
                if v <= LEVELS:
                    c, o, half = halves(cum, v), halves(e, v), 1 << (v - 1)
                    edge = c[:, :, 0, half - 1:half].broadcast_to([P, CC * T // (2 * half), half])
                    link(tt(o[:, :, 0, :], edge, c[:, :, 0, :], ALU.subtract))
                    if v < LEVELS:
                        ins = tt(o[:, :, 1, :], c[:, :, 1, :], edge, ALU.subtract)
                    else:
                        ins = dve.tensor_copy(o[:, :, 1, :], c[:, :, 1, :])
                else:
                    def chunk(a, k):
                        return a[:, :, CHUNK * k:CHUNK * k + CHUNK]

                    def last(k):
                        return cum[:, :, CHUNK * k + CHUNK - 1:CHUNK * k + CHUNK]

                    both = small[:, 60:64].unsqueeze(2)
                    link(tt(both, last(0), last(1), ALU.add))
                    link(tt(chunk(e, 0), both.broadcast_to([P, CC, CHUNK]), chunk(cum, 0), ALU.subtract))
                    link(tt(chunk(e, 1), last(1).broadcast_to([P, CC, CHUNK]), chunk(cum, 1), ALU.subtract))
                    link(dve.tensor_copy(chunk(e, 2), chunk(cum, 2)))
                    ins = tt(chunk(e, 3), chunk(cum, 3), last(2).broadcast_to([P, CC, CHUNK]), ALU.add)
                ins.then_inc(lev_diff, 1)
                dve.wait_ge(lev_diff, v)

            def keep(v):
                dve.wait_ge(lev_s, v + 1)
                ps = lo[:, 2 * (v % 2):2 * (v % 2) + 2, :].rearrange("p a (b t s) -> p (a b) t s", b=2, t=TT)
                dve.copy_predicated(ST, masks[:, v, :].bitcast(U32).unsqueeze(1).unsqueeze(1).broadcast_to([P, CC, TT, P]), ps).then_inc(lev_kept, 1)
                dve.wait_ge(lev_kept, v + 1)

            diff(1)
            keep(0)
            for v in range(1, LEVELS + 2):
                if v <= LEVELS:
                    if v >= 2:
                        dve.wait_ge(lev_qk, v - 1)
                    diff(v + 1)
                dve.wait_ge(lev_exp, v)
                z, e = qk[v % 2], eb[v % 2]
                if v >= 3:
                    dve.wait_ge(lev_s, v - 1)
                if v <= LEVELS:
                    z4, e4, q4, k4 = (halves(a, v) for a in (z, e, qT, kT))
                    link(tt(z4[:, :, 0, :], k4[:, :, 0, :], e4[:, :, 0, :], ALU.mult))
                    tt(z4[:, :, 1, :], q4[:, :, 1, :], e4[:, :, 1, :], ALU.mult).then_inc(lev_qk, 1)
                    keep(v)
                else:
                    link(tt(z[:, :, 0:P], kT[:, :, 0:P], e[:, :, 0:P], ALU.mult))
                    tt(z[:, :, P:T], qT[:, :, P:T], e[:, :, P:T], ALU.mult).then_inc(lev_qk, 1)
            dve.wait_ge(lev_s, LEVELS + 2)
            dve.tensor_copy(S01, lo[:, 0, :].rearrange("p (a b s) -> p a b s", a=2, b=2)).then_inc(lev_kept, 1)
            dve.wait_ge(cn_mean, 1)
            tt(acc, acc, hi[:, 0, 0:T].unsqueeze(1).broadcast_to([P, CC, T]), ALU.subtract).then_inc(cn_d, 1)
            dve.wait_ge(cn_std, 1)
            link(dve.reciprocal(eb[1][:, 1, :], eb[1][:, 0, :]))
            dve.wait_ge(cn_sq, 1)
            tt(acc, acc, eb[1][:, 1, :].unsqueeze(1).broadcast_to([P, CC, T]), ALU.mult).then_inc(cn_y, 1)
            dve.wait_ge(ho_std, 1)
            link(dve.reciprocal(eb[1], eb[0]))
            link(tt(oN, hi[:, 2:4, :].rearrange("p a (b t) -> p (a b) t", b=2), eb[1], ALU.mult))
            dve.wait_ge(mix_g, 1)
            stt(oN, oN, col(R_ONORM), grT, ALU.mult, ALU.mult).then_inc(ho_n, 1)
            wait_used(dve, U_CONV)
            dve.wait_ge(mix_gate, 4)
            tt(merged, gcT, lo[:, :, :].rearrange("p a (b t) -> p (a b) t", b=2), ALU.mult).then_inc(mg_conv, 1)
            wait_used(dve, U_HGRN)
            link(tt(grT2, grT2, hi[:, :, :].rearrange("p a (b t) -> p (a b) t", b=2), ALU.mult))
            dve.wait_ge(mg_conv, 1)
            tt(merged, merged, grT2, ALU.add).then_inc(mg_all, 1)
            residual((U_MIX, U_MIX + 1), x, x_ready)

            norm(1, 1, x, 0, col(R_XA, KC))
            norm(2, 2, cx, T, col(R_MEM, KC))
            for j in range(2):
                wait_used(dve, U_XK + j)
                dve.tensor_copy(xk[:, 4 * j:4 * j + 4, :], hi[:, 2 * j:2 * j + 2, :].rearrange("p a (b t) -> p (a b) t", b=2)).then_inc(xa_k, 1)
            wait_used(dve, U_XV + 1)
            dve.tensor_copy(xv[:, :, 512:1024], lo[:, 2:4, :]).then_inc(xa_v1, 1)
            for h in range(XH):
                dve.wait_ge(xa_s, h + 1)
                mx, nm = small[:, 8 + 2 * h:10 + 2 * h], small[:, 16 + 2 * h:18 + 2 * h]
                link(dve.tensor_reduce(mx, hi[:, h, :].rearrange("p (t m) -> p t m", t=TT), AX.X, ALU.max))
                ts(nm, mx, -XD ** -0.5, None, ALU.mult).then_inc(xa_nm, 1)

            def xa_out(h):
                dve.wait_ge(xa_pv, h + 1)
                dve.tensor_copy(xo[:, 2 * h:2 * h + 2, :], lo[:, 2 + h % 2, :].rearrange("p (d t) -> p d t", d=2)).then_inc(xa_o, 1)

            for h in range(XH):
                dve.wait_ge(xa_e, TT * (h + 1))
                r = small[:, 8 + 2 * h:10 + 2 * h]
                link(dve.reciprocal(r, small[:, 24 + 2 * h:26 + 2 * h]))
                for t in range(TT):
                    ts(xp[:, h, t, :], xp[:, h, t, :], r[:, t:t + 1], None, ALU.mult).then_inc(xa_p, 1)
                if h:
                    xa_out(h - 1)
            xa_out(XH - 1)
            residual((U_XO, U_XO + 1), x, x_ready)

            norm(3, 3, x, 0, col(R_FFN, KC))
            dve.wait_ge(rt_logits, 1)
            lgs = lo[:, 0, 0:128].rearrange("p (t n) -> p t n", t=TT)[:, :, 0:GROUPS + EXPERTS]
            link(tt(lg, lgs, router_b[:].unsqueeze(1).broadcast_to([P, TT, GROUPS + EXPERTS]), ALU.add))
            groups, experts = lg[:, :, 0:GROUPS], lg[:, :, GROUPS:].rearrange("p t (g j) -> p t g j", g=GROUPS)
            gmax, gsum, gp = small[:, 64:66].unsqueeze(2), small[:, 66:68].unsqueeze(2), small[:, 68:70].unsqueeze(2)
            m1, m2 = small[:, 70:72].unsqueeze(2), small[:, 72:74].unsqueeze(2)
            pick = small[:, 74:76].unsqueeze(2)
            ghot, shifted, gexp = part(4184, TT, GROUPS), part(4192, TT, GROUPS), part(4200, TT, GROUPS)
            inside, hot1, hot2, rest = (part(4208 + 16 * k, TT, PER_GROUP) for k in range(4))
            both, prod = part(4272, TT, PER_GROUP), part(4288, TT, PER_GROUP * GROUPS)

            def first_best(dst, v, best, n):
                link(tt(dst, v, best.broadcast_to([P, TT, n]), ALU.is_equal))
                link(tt(dst, dst, desc[:, PER_GROUP - n:].unsqueeze(1).broadcast_to([P, TT, n]), ALU.mult))
                link(dve.tensor_reduce(pick, dst, AX.X, ALU.max))
                link(tt(dst, dst, pick.broadcast_to([P, TT, n]), ALU.is_equal))

            link(dve.tensor_reduce(gmax, groups, AX.X, ALU.max))
            tt(shifted, groups, gmax.broadcast_to([P, TT, GROUPS]), ALU.subtract).then_inc(rt_d, 1)
            first_best(ghot, groups, gmax, GROUPS)
            prod4 = prod.rearrange("p t (g j) -> p t g j", g=GROUPS)
            for t in range(TT):
                link(tt(prod4[:, t], experts[:, t], ghot[:, t].unsqueeze(2).broadcast_to([P, GROUPS, PER_GROUP]), ALU.mult))
                link(dve.tensor_reduce(inside[:, t], prod4[:, t].rearrange("p g j -> p j g"), AX.X, ALU.add))
            link(dve.tensor_reduce(m1, inside, AX.X, ALU.max))
            first_best(hot1, inside, m1, PER_GROUP)
            link(stt(rest, hot1, -3.0e38, inside, ALU.mult, ALU.add))
            link(dve.tensor_reduce(m2, rest, AX.X, ALU.max))
            first_best(hot2, rest, m2, PER_GROUP)
            tt(small[:, 32:34].unsqueeze(2), m2, m1, ALU.subtract).then_inc(rt_d2, 1)
            dve.wait_ge(rt_e, 1)
            link(dve.tensor_reduce(gsum, gexp, AX.X, ALU.add))
            link(dve.reciprocal(gp, gsum))
            dve.wait_ge(rt_e2, 1)
            link(ts(small[:, 36:38], small[:, 34:36], 1.0, None, ALU.add))
            link(dve.reciprocal(small[:, 38:40], small[:, 36:38]))
            w1, w2 = small[:, 38:40].unsqueeze(2), small[:, 34:36].unsqueeze(2)
            link(tt(w1, w1, gp, ALU.mult))
            link(tt(w2, w2, w1, ALU.mult))
            link(tt(hot1, hot1, w1.broadcast_to([P, TT, PER_GROUP]), ALU.mult))
            link(tt(hot2, hot2, w2.broadcast_to([P, TT, PER_GROUP]), ALU.mult))
            link(tt(both, hot1, hot2, ALU.add))
            comb4 = comb[:, :, :].rearrange("p t (g j) -> p t g j", g=GROUPS)
            for t in range(TT):
                ins = tt(comb4[:, t], ghot[:, t].unsqueeze(2).broadcast_to([P, GROUPS, PER_GROUP]),
                         both[:, t].unsqueeze(1).broadcast_to([P, GROUPS, PER_GROUP]), ALU.mult)
                if t == 0:
                    link(ins)
            link(ins)
            ts(chosen, comb[:, :, :], 0.0, float(CW), ALU.is_gt, ALU.mult).then_inc(rt_comb, 1)
            link(dve.memset(place, -1.0))
            dve.wait_ge(rt_rank, 1)
            ranks = lo[:, 1, 0:TT * EXPERTS].rearrange("p (t n) -> p t n", t=TT)
            link(stt(count, ranks, 1.0, chosen, ALU.add, ALU.mult))
            link(ts(place[:, :, 0:EXPERTS], count, 1.0 / CW, -1.0, ALU.mult, ALU.add))
            link(dve.tensor_reduce(small[:, 80:81], lo[:, 1, TT * EXPERTS:(TT + 1) * EXPERTS], AX.X, ALU.max))
            ts(small[:, 81:82], small[:, 80:81], float(PLACES), None, ALU.is_gt).then_inc(rt_flag, 1)
            dve.wait_ge(rt_flag, 1)
            dve.tensor_copy(overflow[:], small[:, 81:82]).then_inc(rt_flag, 1)
            numbers4 = numbers.unsqueeze(1).unsqueeze(1).broadcast_to([P, TT, 2, PLACES])

            def one_hots(at):
                tt(onehot, numbers4, place[:, :, at].unsqueeze(3).broadcast_to([P, TT, 2, PLACES]), ALU.is_equal).then_inc(ex_onehot, 1)

            def gathered(i=None):
                for j in range(2):
                    dve.wait_ge(ex_gathered, j + 1 if i is None else i * 2 + (j + 3))
                    tt(hg[:, 4 * j:4 * j + 4, :], lo[:, 2 + j, :].rearrange("p (c s) -> p c s", c=4),
                       col(R_FFN + 4 * j, 4).unsqueeze(2).broadcast_to([P, 4, 2 * PLACES]), ALU.mult).then_inc(ex_hg, 1)

            one_hots(slice(0, 2))
            gathered()
            with dve.Fori(0, EXPERTS // 2) as i:
                dve.wait_ge(ex_onehot, i + 1)
                dve.wait_ge(ex_back_turned, i + 1)
                tt(weighted, onehot, comb[:, :, bass.ds(i * 2, 2)].unsqueeze(3).broadcast_to([P, TT, 2, PLACES]), ALU.mult).then_inc(ex_weighted, 1)
                dve.wait_ge(ex_weighted, i + 1)
                one_hots(bass.ds(i * 2 + 2, 2))
                for e in range(2):
                    wait_used(dve, U_MOE + 2 + e, i)
                dve.wait_ge(ex_sgd, i + 1)
                tt(ex_h, ex_sg, lo[:, 1, :], ALU.mult).then_inc(ex_hd, 1)
                gathered(i)
            dve.wait_ge(ex_done, 1)
            x2 = x[:, :, :].rearrange("p t (h n) -> p (t h) n", h=2)
            tt(x2, x2, hi[:, :, :], ALU.add).then_inc(moe_done, 1)
            dve.wait_ge(moe_done, 1)
            with dve.If(dve.value_load(overflow[0:1, 0:1], min_val=0, max_val=1)):
                ts(chosen, place[:, :, 0:EXPERTS], float(PLACES), None, ALU.is_ge).then_inc(rt_flag, 1)
                dve.wait_ge(rt_flag, 3)
                tt(comb[:, :, :], comb[:, :, :], chosen, ALU.mult).then_inc(dn_added, 1)
                with dve.Fori(0, EXPERTS) as e:
                    for f in range(4):
                        dve.wait_ge(dn_sgd, e * 4 + (f + 1))
                        tt(dn_h[:, f, :], dn_sg[:, f, :], lo[:, f, T:2 * T], ALU.mult).then_inc(dn_hd, 1)
                    dve.wait_ge(dn_down, e + 1)
                    dve.wait_ge(dn_added, e + 1)
                    for t in range(TT):
                        for h in range(2):
                            xs = x[:, t, h * 512:h * 512 + 512]
                            ins = stt(xs, hi[:, 2 * t + h, :], comb[:, t, bass.ds(e, 1)], xs, ALU.mult, ALU.add)
                    ins.then_inc(dn_added, 1)
                dve.wait_ge(dn_added, EXPERTS + 1)
            tt(tmp[:, 0:1], eps[:], eps[:], ALU.add).then_inc(x_ready, 1)

            rstd_of(4)
            dve.wait_ge(gain_loaded, 16)
            for t in range(TT):
                ins = stt(x[:, t, :], x[:, t, :], rstd[:, t:t + 1], gate_b[:], ALU.mult, ALU.mult)
            link(ins)
            tt(tmp[:, 0:1], eps[:], eps[:], ALU.add).then_inc(gain_used, 1)
            tt(tmp[:, 1:2], eps[:], eps[:], ALU.add).then_inc(x_ready, 1)

            for l in range(2):
                with dve.Fori(0, NMOD // 3) as i:
                    for b in range(3):
                        wait_used(dve, U_MOD + 18 * l + 2 * b + 1, i)
                        dve.tensor_copy(mrow[:, b, :], lo[:, b, 0:T]).then_inc(md_copied, 1)
                        dve.wait_ge(md_turned, i * 3 + (9 * l + b + 1))
                        ps = hi[:, b, 0:T].rearrange("p (b g w) -> p g b w", b=2, w=32)
                        for v in range(2):
                            tt(mod[:, l, bass.ds(i * 3 + b, 1), v, :].rearrange("p a (g b) -> p (a g) b", b=2), ps[:, :, :, v],
                               cols[:, 2 + l, bass.ds(i * 24 + 8 * b, 8)].rearrange("p (g b) -> p g b", b=2), ALU.add).then_inc(md_done, 1)
            dve.wait_ge(md_done, 4 * NMOD)
            uses = [(0, 0, 1, 1), (0, 0, 1, 0), (0, 1, 4, 0), (0, 1, 4, 1), (0, 2, 7, 0), (1, 0, 1, 0), (1, 1, 4, 0), (1, 2, 7, 0)]
            for k, (l, j, m, v) in enumerate(uses):
                ins = stt(mod_scale[:, k, :], mod[:, l, m, v, :], 1.0, col(R_NG2 + (3 * l + j) * KC, KC), ALU.add, ALU.mult)
            ins.then_inc(md_scales, 1)

            def ffn(f, i, src, scale, shift, signal):
                norm(i, i + 1, src, 0, scale, shift)
                with dve.Fori(0, NCHUNK) as c:
                    for b in range(2):
                        dve.wait_ge(ffn_sgd, c * 2 + (2 * NCHUNK * f + b + 1))
                        tt(ffn_h[:, b, :], ffn_sg[:, b, :], lo[:, b, T:2 * T], ALU.mult).then_inc(ffn_hd, 1)
                g = (0, 1, 3, 4, 6)[f]
                dve.wait_ge(gate_ready, g + 1)
                residual((U_FFN[f] + 16,), src, signal, True)

            ffn(0, 4, cx, mod_scale[:, 0], mod[:, 0, 0, 1], ctx_ready)
            ffn(1, 5, x, mod_scale[:, 1], mod[:, 0, 0, 0], x_ready)

            norm(6, 7, x, 0, mod_scale[:, 2], mod[:, 0, 3, 0])
            for z, a in ((qe, HD), (qo, 0), (qbe, HD), (qbo, 0)):
                dve.memset(z[a:a + HD], 0.0).then_inc(at_zero, 1)
            norm(7, 8, cx, T, mod_scale[:, 3], mod[:, 0, 3, 1])
            wait_used(dve, U_ATT + 2)
            dve.tensor_copy(va, lo[:, :, :]).then_inc(at_va, 1)
            dve.wait_ge(bias_loaded, 16 * 16)
            dve.wait_ge(rope_loaded, 64)
            tt(bias, bias, window.unsqueeze(1).broadcast_to([P, 2 * NAH, T]), ALU.add).then_inc(na_bias, 1)
            cosb, sinb = (a.unsqueeze(1).broadcast_to([P, CC, T]) for a in (cos, sin))
            dve.wait_ge(at_rot, 1)
            link(tt(rawq, rawq, cosb, ALU.mult))
            link(tt(rtmp, lo[:, 0:2, :].rearrange("p a (b t) -> p (a b) t", b=2), sinb, ALU.mult))
            tt(qbe[0:HD], rawq[0:HD], rtmp[0:HD], ALU.add).then_inc(at_rope, 1)
            tt(qbo[HD:P], rawq[HD:P], rtmp[HD:P], ALU.add).then_inc(at_rope, 1)
            dve.wait_ge(at_rot, 2)
            link(tt(rawk, rawk, cosb, ALU.mult))
            dve.wait_ge(at_rope, 2)
            link(tt(rtmp, lo[:, 2:4, :].rearrange("p a (b t) -> p (a b) t", b=2), sinb, ALU.mult))
            tt(kbT[:, :, 0:T], rawk, rtmp, ALU.add).then_inc(at_rope, 1)
            link(tt(lam_in[:, 0, :], lam_in[:, 0, :], lam_in[:, 1, :], ALU.mult))
            link(tt(lam_in[:, 2, :], lam_in[:, 2, :], lam_in[:, 3, :], ALU.mult))
            dve.tensor_reduce(small[:, 40:42], lam_in[:, 0::2, :], AX.X, ALU.add).then_inc(lam_d, 1)
            dve.wait_ge(lam_e, 1)
            lam = small[:, 44:45]
            link(tt(lam, small[:, 42:43], small[:, 43:44], ALU.subtract))
            link(ts(lam, lam, LAM_INIT, None, ALU.add))

            def na_max(h):
                dve.wait_ge(na_s, h + 1)
                b = 2 * (h % 2)
                link(dve.tensor_reduce(small[:, 56 + b:58 + b], hi[:, b:b + 2, :], AX.X, ALU.max))
                ts(small[:, 48 + b:50 + b], small[:, 56 + b:58 + b], -HD ** -0.5, None, ALU.mult).then_inc(na_nm, 1)

            na_max(0)
            for h in range(NAH):
                b = 2 * (h % 2)
                if h + 1 < NAH:
                    na_max(h + 1)
                dve.wait_ge(na_e, TT * (h + 1))
                link(dve.reciprocal(small[:, 76 + b:78 + b], small[:, 52 + b:54 + b]))
                for t in range(TT):
                    ts(ap_[:, b + t, :], ap_[:, b + t, :], small[:, 76 + b + t:77 + b + t], None, ALU.mult).then_inc(na_p, 1)
                if h % 2:
                    dve.wait_ge(na_pv, h + 1)
                    dve.tensor_copy(mergeT[:, h // 2, :], lo[:, 2 + (h // 2) % 2, 0:T]).then_inc(na_o, 1)
            for h in range(DH):
                dve.wait_ge(df_s, h + 1)
                link(dve.tensor_reduce(small[:, 56:60], hi[:, :, :], AX.X, ALU.max))
                ts(small[:, 48:52], small[:, 56:60], -HD ** -0.5, None, ALU.mult).then_inc(df_nm, 1)
                dve.wait_ge(df_e, 4 * (h + 1))
                r = small[:, 76:80]
                link(dve.reciprocal(r, small[:, 52:56]))
                link(ts(r[:, 2:4], r[:, 2:4], lam, None, ALU.mult))
                for t in range(TT):
                    link(ts(ap_[:, 2 + t, :], ap_[:, 2 + t, :], r[:, 2 + t:3 + t], None, ALU.mult))
                    stt(ap_[:, t, :], ap_[:, t, :], r[:, t:t + 1], ap_[:, 2 + t, :], ALU.mult, ALU.subtract).then_inc(df_p, 1)
                dve.wait_ge(df_pv, h + 1)
                dve.tensor_copy(dO[:, h, :], lo[:, 2 + h % 2, 0:T]).then_inc(df_o, 1)
            dve.wait_ge(df_std, 1)
            link(dve.reciprocal(dsq, dsq))
            dve.wait_ge(df_o, DH)
            stt(mergeT[:, CC:KC, :], dO, subln[:], dsq, ALU.mult, ALU.mult).then_inc(df_n, 1)
            dve.wait_ge(gate_ready, 3)
            residual((U_ATTO, U_ATTO + 1), x, x_ready, True)

            ffn(2, 8, x, mod_scale[:, 4], mod[:, 0, 6, 0], x_ready)
            ffn(3, 9, x, mod_scale[:, 5], mod[:, 1, 0, 0], x_ready)

            norm(10, 11, x, 0, mod_scale[:, 6], mod[:, 1, 3, 0])
            link(dve.memset(up2[:, :, 0:T + 2:T + 1], 0.0))
            for j in range(2):
                wait_used(dve, U_CM + 2 * j + 1)
                dve.wait_ge(cm_cg, j + 1)
                ins = tt(up2[:, 4 * j:4 * j + 4, 1:T + 1], (hi if j else lo)[:, 2:4, :].rearrange("p a (b t) -> p (a b) t", b=2),
                         cgs[:, 4 * j:4 * j + 4, :], ALU.mult)
                ins.then_inc(cm_u, 1)
            dve.wait_ge(cm_u, 2)
            for c in range(KC):
                taps = [col(R3_CONV2 + j * KC + c, 1, 2) for j in range(3)]
                link(ts(vm[:, c, :], up2[:, c, 0:T], taps[0], None, ALU.mult))
                for j in (1, 2):
                    link(stt(vm[:, c, :], up2[:, c, j:j + T], taps[j], vm[:, c, :], ALU.mult, ALU.add))
            for j in range(2):
                wait_used(dve, U_CM + 4 + j)
                v = vm[:, 4 * j:4 * j + 4, :]
                tt(v, v, lo[:, 2 * j:2 * j + 2, :].rearrange("p a (b t) -> p (a b) t", b=2), ALU.mult).then_inc(cm_bg, 1)
            dve.wait_ge(gate_ready, 6)
            residual((U_CMO, U_CMO + 1), x, x_ready, True)
            ffn(4, 11, x, mod_scale[:, 7], mod[:, 1, 6, 0], x_ready)

            rstd_of(13)
            dve.wait_ge(gain_loaded, 32)
            dve.wait_ge(norm_turned, 48)
            for t in range(TT):
                ins = stt(xn[:, t, :], x[:, t, :], rstd[:, t:t + 1], gate_b[:], ALU.mult, ALU.mult)
            ins.then_inc(x_ready, 1)


_INS = ['x', 'mem', 'norm_mix_g', 'w_in', 'conv_w', 'conv_b', 'conv_ln_g', 'conv_ln_b', 'conv_w_out', 'hgrn_lb_logits',
        'hgrn_onorm_g', 'hgrn_w_out', 'w_mix_out', 'norm_xa_g', 'norm_mem_g', 'xa_w_q', 'xa_w_k', 'xa_w_v', 'xa_w_o',
        'norm_ffn_g', 'router_group_w', 'router_group_b', 'router_expert_w', 'router_expert_b', 'moe_w_gate', 'moe_w_up',
        'moe_w_down', 'final_norm_g', 'c_2', 'ctx_2', 'c_ctx_2', 'mod_w_2', 'mod_b_2', 'norm_g_2', 'ffn_w_gate_2',
        'ffn_w_up_2', 'ffn_w_down_2', 'attn_w_in_2', 'attn_w_out_2', 'rpb_pad', 'diff_lambda_2', 'diff_subln_g_2',
        'conv_w_in_2', 'conv_w_out_2', 'conv_w_2', 'final_g_2']


def constants():
    import numpy as np

    f = np.float32
    mats = np.zeros((P, 3, P), f)
    mats[:, 0] = np.eye(P)
    for a in range(0, P, GRID):
        mats[a:a + GRID, 1, a:a + GRID] = 8.0 * np.eye(GRID)[::-1]
    for i in range(0, P, 2):
        mats[i + 1, 2, i], mats[i, 2, i + 1] = -1.0, 1.0
    s, t = np.arange(P)[:, None], np.arange(P)[None, :]
    masks = np.zeros((P, 8, P), f)
    masks[:, 0] = np.eye(P)
    for v in range(1, 8):
        half = 1 << (v - 1)
        masks[:, v] = (s // (2 * half) == t // (2 * half)) & (s // half % 2 == 0) & (t // half % 2 == 1)
    n_freq = HD // 4
    inv = f(10000.0) ** (-np.arange(n_freq, dtype=f) / f(n_freq))
    tok = np.arange(T)
    ang = np.concatenate([(tok // GRID).astype(f)[:, None] * inv, (tok % GRID).astype(f)[:, None] * inv], axis=-1)
    rope = np.zeros((P, 2, T), f)
    pair = np.arange(P) % HD // 2
    rope[:, 0], rope[:, 1] = np.cos(ang).T[pair], np.sin(ang).T[pair]
    qc = GRID - 1 - np.arange(P) % GRID
    start = np.clip(qc - 8, 0, GRID - 16)
    kc = np.arange(T) % GRID
    window = np.where((kc >= start[:, None]) & (kc < start[:, None] + 16), f(0), f(-1e30)).astype(f)
    desc = np.tile(np.arange(PER_GROUP, 0, -1, dtype=f), (P, 1))
    rank = np.zeros((P, P + PLACES), f)
    rank[:, 0:P] = (s < t) / f(CW)
    rank[:, P:] = np.arange(PLACES)
    return {"k_mats": mats, "k_masks": masks, "k_rope": rope, "k_window": window, "k_desc": desc, "k_rank": rank}


def kernel(**inputs):
    import numpy as _np
    import concourse.bacc as _bacc
    from concourse import mybir as _mybir
    from concourse.bass_utils import run_bass_kernel_spmd as _run

    nc = _bacc.Bacc("TRN2", target_bir_lowering=False, num_devices=1)
    tables = constants()
    rpb = _np.asarray(inputs["na_rpb_2"])[0]
    pad = GRID - 16
    tables["rpb_pad"] = _np.pad(rpb, ((0, 0), (0, 0), (pad, P - pad - rpb.shape[-1])))
    arrays, args = {}, []
    for name in _INS + ["k_mats", "k_masks", "k_rope", "k_window", "k_desc", "k_rank"]:
        a = _np.ascontiguousarray(tables[name] if name in tables else inputs[name])
        arrays[f"in_{name}_dram"] = a
        args.append(nc.dram_tensor(f"in_{name}_dram", a.shape, _mybir.dt.from_np(a.dtype), kind="ExternalInput").ap())
    args.append(nc.dram_tensor("out_0_dram", (1, T, D), F32, kind="ExternalOutput").ap())
    program(nc, *args)
    r = _run(nc, [arrays], core_ids=[0])
    return r.results[0]["out_0_dram"]
```

```python
from contextlib import ExitStack

import concourse.bass as bass
from concourse import mybir

F32 = mybir.dt.float32
U32 = mybir.dt.uint32
I32 = mybir.dt.int32
F32R = mybir.dt.float32r
ALU = mybir.AluOpType
ACT = mybir.ActivationFunctionType
AX = mybir.AxisListType

P = 128
T = 256
TT = T // P
D = 1024
KC = D // P
CW = 512
CC = CW // P
TAPS = 31
CHUNK = 64
XH = 4
XD = D // XH
GROUPS, PER_GROUP = 4, 8
EXPERTS = GROUPS * PER_GROUP
FF = 512
PLACES = 64
FF2 = 2816
FCHUNK = 256
NCHUNK = FF2 // FCHUNK
NMOD = 9
NAH, HD = 8, 64
DH = 4
GRID = 64
KEYS = 2 * T
EPS = 1e-6
LAM_INIT = 0.2

RING = 6
UNIT = 4096

VECTORS = 2 * NMOD


def u_in(j):
    return 3 * min(j, NMOD) + max(j - NMOD, 0)


def u_mod(m):
    return 3 * m + 1 if m < NMOD else u_in(10) + 2 * (m - NMOD)


U_CONV = u_mod(VECTORS)
U_HGRN, U_MIX = U_CONV + 1, U_CONV + 2
U_XQ, U_XK, U_XV, U_XO = (U_MIX + 2 * k for k in range(1, 5))
U_MOE = U_XO + 2
FFN_UNITS = NCHUNK + (NCHUNK + 1) // 2
U_FFN = [0] * 5
U_FFN[0] = U_MOE + 3 * EXPERTS
U_FFN[1] = U_FFN[0] + FFN_UNITS
U_ATT = U_FFN[1] + FFN_UNITS
U_ATTO = U_ATT + 6
U_FFN[2] = U_ATTO + 2
U_FFN[3] = U_FFN[2] + FFN_UNITS
U_CM = U_FFN[3] + FFN_UNITS
U_CMO = U_CM + 6
U_FFN[4] = U_CMO + 2

R_MIX, R_XA, R_MEM, R_FFN = 0, 8, 16, 24
R_CONVB, R_LNG, R_LNB, R_LB, R_ONORM, R_SUBLN, R_NG2, R_C, R_CCTX, R_END = 32, 36, 40, 44, 52, 53, 54, 102, 110, 118
R2_TAPS, R2_END = 0, TAPS * CC
R3_MODB, R3_CONV2, R3_END = 0, 72, 96
R4_END = 72

SCRATCH = 14336


def program(nc, x_in, mem, norm_mix_g, w_in, conv_w, conv_b, conv_ln_g, conv_ln_b, conv_w_out, hgrn_lb_logits,
            hgrn_onorm_g, hgrn_w_out, w_mix_out, norm_xa_g, norm_mem_g, xa_w_q, xa_w_k, xa_w_v, xa_w_o, norm_ffn_g,
            router_group_w, router_group_b, router_expert_w, router_expert_b, moe_w_gate, moe_w_up, moe_w_down,
            final_norm_g, c_2, ctx_2, c_ctx_2, mod_w_2, mod_b_2, norm_g_2, ffn_w_gate_2, ffn_w_up_2, ffn_w_down_2,
            attn_w_in_2, attn_w_out_2, rpb_pad, diff_lambda_2, diff_subln_g_2, conv_w_in_2, conv_w_out_2, conv_w_2,
            final_g_2, k_mats, k_masks, k_rope, k_window, k_desc, k_rank, out):
    ctx = ExitStack()
    with ctx:
        def sb(name, shape, dt=F32):
            return ctx.enter_context(nc.sbuf_tensor(name, shape, dt))

        def sem(name):
            return ctx.enter_context(nc.semaphore(name))

        with ExitStack() as between:
            x_split, w_split, d_split, h_split = (
                between.enter_context(nc.sbuf_tensor(name, shape, F32R))
                for name, shape in (("x_split", [P, 2, KC, T]), ("w_split", [P, 2, 2, 2, KC, P]), ("d_split", [P, 2, 2, D]),
                                    ("h_split", [P, 2, 2, T])))
        ht = sb("ht", [P, KC, KEYS])
        scratch = sb("scratch", [P, SCRATCH])
        ring = sb("ring", [P, RING, UNIT])
        x = sb("x", [P, TT, D])
        side = sb("side", [P, 2, TT * D])
        cx = side[:, 0, :].rearrange("p (t d) -> p t d", t=TT)
        xn = side[:, 1, :].rearrange("p (t d) -> p t d", t=TT)
        gate_b = sb("gate_b", [P, D])
        mats = sb("mats", [P, 3, P])
        desc = sb("desc", [P, PER_GROUP])
        cols = sb("cols", [P, 4, P])
        means = sb("means", [P, 2, P])
        tmp = sb("tmp", [P, 512])
        eps = sb("eps", [P, 1])
        overflow = sb("overflow", [P, 1], I32)
        ss = sb("ss", [P, TT])
        std = sb("std", [P, TT])
        rstd = sb("rstd", [P, TT])
        router_w = sb("router_w", [P, KC, GROUPS + EXPERTS])
        router_b = sb("router_b", [P, GROUPS + EXPERTS])
        comb = sb("comb", [P, TT, EXPERTS])
        mod = sb("mod", [P, 2, NMOD, 2, KC])
        mod_scale = sb("mod_scale", [P, 8, KC])
        silu_c = sb("silu_c", [P, KC, 32])
        small = sb("small", [P, 96])
        lbc = sb("lbc", [P, 2, CC])
        subln = sb("subln", [P, 1])
        zero = sb("zero", [P, 1])
        zero_r = sb("zero_r", [P, 1], F32R)
        masks = ht[:, :, T:T + P]
        rows = tmp[:].rearrange("p (a b) -> p a b", b=P)
        cos, sin = silu_c[:].rearrange("p a b -> p (a b)"), router_w[:].rearrange("p a b -> p (a b)")[:, 0:T]
        window, lam_in = tmp[:, 0:T], tmp[:, T:2 * T].rearrange("p (a b) -> p a b", a=4)

        lo = ctx.enter_context(nc.psum_tensor("lo", [P, 4, 512], F32))
        hi = ctx.enter_context(nc.psum_tensor("hi", [P, 4, 512], F32))

        ident, flip8, rot = mats[:, 0, :], mats[:, 1, :], mats[:, 2, :]

        def part(at, *shape):
            n = 1
            for s in shape:
                n *= s
            v = scratch[:, at:at + n]
            if len(shape) == 1:
                return v
            if len(shape) == 2:
                return v.rearrange("p (a b) -> p a b", a=shape[0])
            return v.rearrange("p (a b c) -> p a b c", a=shape[0], b=shape[1])

        def htpart(at, *shape):
            v = ht[:, :, :].rearrange("p a b -> p (a b)")
            n = 1
            for s in shape:
                n *= s
            v = v[:, at:at + n]
            return v if len(shape) == 1 else v.rearrange("p (a b) -> p a b", a=shape[0])

        unit_loaded = [sem(f"unit_loaded{s}") for s in range(RING)]
        unit_used = [sem(f"unit_used{s}") for s in range(RING)]
        x_loaded, mem_loaded, ctx_loaded = sem("x_loaded"), sem("mem_loaded"), sem("ctx_loaded")
        mats_loaded, rows_loaded, consts_loaded, bias_loaded = (sem(n + "_loaded") for n in ("mats", "rows", "consts", "bias"))
        gain_loaded, out_stored = sem("gain_loaded"), sem("out_stored")
        dve_chain, act_chain = sem("dve_chain"), sem("act_chain")
        set_up = sem("set_up")
        cols_turned, cols_ready = sem("cols_turned"), sem("cols_ready")
        col_math = sem("col_math")
        norm_sq, norm_std, norm_xn = sem("norm_sq"), sem("norm_std"), sem("norm_xn")
        norm_turned, norm_ready = sem("norm_turned"), sem("norm_ready")
        x_ready, ctx_ready = sem("x_ready"), sem("ctx_ready")
        gate_turned, gate_ready = sem("gate_turned"), sem("gate_ready")

        def unit_of(n):
            return ring[:, n % RING, :]

        def as_cols(n):
            return unit_of(n).rearrange("p (k n) -> p k n", k=KC)

        def as_rows(n):
            return unit_of(n).rearrange("p (k n) -> p k n", k=4)

        def wait_unit(pe, n, i=None):
            v = n // RING + 1
            pe.wait_ge(unit_loaded[n % RING], 32 * v if i is None else (i + v) * 32)

        def wait_used(eng, n, i=None):
            v = n // RING + 1
            eng.wait_ge(unit_used[n % RING], v if i is None else i + v)

        def up_unit(n, c, b):
            n += 6 * (c // 4) + (0, 2, 3, 5)[c % 4]
            return n, unit_of(n).rearrange("p (a k n) -> p a k n", a=2, k=KC)[:, :, :, b * P:b * P + P]

        def down_unit(n, c, b):
            n += 6 * (c // 4) + (1, 1, 4, 4)[c % 4]
            return n, as_rows(n)[:, 2 * (c % 2) + b, :]

        def nth(f, c, b, it=None):
            v = 2 * NCHUNK * f + 2 * c + b + 1
            return v if it is None else it * 8 + v

        class Link:

            def __init__(self, eng, chain):
                self.eng, self.chain, self.n = eng, chain, 0

            def __call__(self, ins):
                self.n += 1
                ins.then_inc(self.chain, 1)
                self.eng.wait_ge(self.chain, self.n)

        block = ctx.enter_context(nc.Block())

        sg, upad, acc = part(0, CC, T), part(1024, CC, 286), part(2168, CC, T)
        qT, kT, cum = part(3192, CC, T), part(4216, CC, T), part(5240, CC, T)
        eb = [part(6264, CC, T), part(0, CC, T)]
        qk = [part(7288, CC, T), part(1024, CC, T)]
        grT = part(8312, CC, T)
        vtok = side[:, 1, 0:TT * CW].rearrange("p (t n) -> p t n", t=TT)
        gcT, grT2 = part(9336, KC, T), part(11384, KC, T)
        ST = ht[:, 0:CC, 0:T].rearrange("p h (t s) -> p h t s", t=TT)
        S01 = ht[:, CC:CC + 2, 0:T].rearrange("p a (b s) -> p a b s", b=2)
        oN = part(4216, CC, T)
        reset = gate_b[:]
        merged = side[:, 1, :].rearrange("p (c t) -> p c t", c=KC)
        LEVELS = 7
        xq, xk, xv = part(0, KC, T), part(2048, KC, T), part(4096, TT, D)
        xp, xpt, xo = part(6144, XH, TT, T), part(8192, 2, 2, T), part(9216, KC, T)
        ffn_sg, ffn_h = part(13 * D, 2, T), part(13 * D + 2 * T, 2, T)
        lg = part(4096, TT, GROUPS + EXPERTS)
        hg, onehot, weighted, back = part(0, KC, 2 * PLACES), part(1024, TT, 2, PLACES), part(1280, TT, 2, PLACES), part(1536, T)
        ex_sg, ex_h, ex_hT, ex_y = part(2048, FF), part(2560, FF), part(3072, 4, 2 * PLACES), part(5120, D)
        place, chosen, count = part(4608, TT, EXPERTS + 2), part(4736, TT, EXPERTS), part(4800, TT, EXPERTS)
        before_me, numbers = part(13440, P), part(13440 + P, PLACES)
        dn_w = part(0, 3, UNIT)
        dn_sg, dn_h = part(3 * UNIT, 4, T), part(3 * UNIT + 4 * T, 4, T)
        mrow = part(13440 + P + PLACES, 2, T)
        qe, qo, kaT, va = part(0, CC, T), part(1024, CC, T), part(2048, CC, KEYS), part(4096, 4, CW)
        qbe, qbo, kbT, vb = part(6144, CC, T), part(7168, CC, T), part(8192, CC, KEYS), part(10240, 4, CW)
        ap_, apt = part(12288, 4, KEYS), htpart(3072, 4, T)
        rawq, rawk = part(12288, CC, T), part(13312, CC, T)
        rtmp = htpart(2048, CC, T)
        dO, dsq = part(0, CC, T), part(1024, CC, T)
        bias = side[:, :, :].rearrange("p a (h n) -> p (a h) n", n=T)
        mergeT = htpart(0, KC, T)
        cgs, up2, vm = part(0, KC, T), part(2048, KC, T + 2), part(4112, KC, T)

        mix_u = sem("mix_u")
        mix_cg, mix_q, mix_f, mix_v, mix_g, mix_gate = (sem("mix_" + n) for n in ("cg", "q", "f", "v", "g", "gate"))
        mix_fk, mix_ln_f, mix_scan, conv_step = (sem(n) for n in ("mix_fk", "mix_ln_f", "mix_scan", "conv_step"))
        at_zero, rope_loaded = sem("at_zero"), sem("rope_loaded")
        lev_diff, lev_exp, lev_qk, lev_s, lev_kept = (sem("lev_" + n) for n in ("diff", "exp", "qk", "s", "kept"))
        cn_mean, cn_d, cn_sq, cn_var, cn_std, cn_y, cn_act = (sem("cn_" + n) for n in ("mean", "d", "sq", "var", "std", "y", "act"))
        ho_o, ho_sq, ho_ms, ho_std, ho_n = (sem("ho_" + n) for n in ("o", "sq", "ms", "std", "n"))
        mg_conv, mg_all = sem("mg_conv"), sem("mg_all")
        xa_q, xa_k, xa_v, xa_v1, xa_s, xa_nm, xa_e, xa_p, xa_t, xa_pt, xa_pv, xa_o = (
            sem("xa_" + n) for n in ("q", "k", "v", "v1", "s", "nm", "e", "p", "t", "pt", "pv", "o"))
        rt_logits, rt_d, rt_e = (sem("rt_" + n) for n in ("logits", "d", "e"))
        rt_comb, rt_rank, rt_flag = (sem("rt_" + n) for n in ("comb", "rank", "flag"))
        ex_onehot, ex_weighted, ex_gathered, ex_hg, ex_sgd, ex_hd, ex_turned, ex_hTd, ex_back_turned, ex_back, ex_yd, ex_done = (
            sem("ex_" + n) for n in ("onehot", "weighted", "gathered", "hg", "sg", "h", "turned", "hT", "back_turned", "back", "y", "done"))
        dn_loaded, dn_gu, dn_sgd, dn_hd, dn_down, dn_added = (sem("dn_" + n) for n in ("loaded", "gu", "sg", "h", "down", "added"))
        moe_done = sem("moe_done")
        md_copied, md_turned, md_cols, md_scales = (sem("md_" + n) for n in ("copied", "turned", "cols", "scales"))
        ffn_gu, ffn_sgd, ffn_h32, ffn_hd, ffn_dn = (sem("ffn_" + n) for n in ("gu", "sg", "h32", "h", "dn"))
        xs_hi, xs_lo, gs_hi, gs_lo, ds_hi, ds_lo = (sem(n) for n in ("xs_hi", "xs_lo", "gs_hi", "gs_lo", "ds_hi", "ds_lo"))
        at_qa, at_ka, at_va, at_qb, at_kb, at_vb, at_rot, at_rope = (
            sem("at_" + n) for n in ("qa", "ka", "va", "qb", "kb", "vb", "rot", "rope"))
        na_bias, na_s, na_nm, na_e, na_p, na_t, na_pt, na_pv, na_o = (
            sem("na_" + n) for n in ("bias", "s", "nm", "e", "p", "t", "pt", "pv", "o"))
        df_s, df_nm, df_e, df_p, df_t, df_pt, df_pv, df_o, df_sq, df_ms, df_std, df_n = (
            sem("df_" + n) for n in ("s", "nm", "e", "p", "t", "pt", "pv", "o", "sq", "ms", "std", "n"))
        lam_d, lam_e = sem("lam_d"), sem("lam_e")
        cm_cg, cm_u, cm_bg = sem("cm_cg"), sem("cm_u"), sem("cm_bg")
        gain_used = sem("gain_used")

        @block.sync
        def _(sp):
            sp.dma_start(x[:], x_in[0].rearrange("(t p) d -> p t d", p=P)).then_inc(x_loaded, 16)

            def load(n, halves, i=None):
                if i is not None:
                    sp.wait_ge(unit_used[n % RING], i + n // RING)
                elif n >= RING:
                    sp.wait_ge(unit_used[n % RING], n // RING)
                for dst, src in halves():
                    sp.dma_start(dst, src).then_inc(unit_loaded[n % RING], 16)

            def split(v, s, half):
                return (v[:, 0:half], s[:, 0:half]), (v[:, half:2 * half], s[:, half:2 * half])

            def cols_unit(n, w, at, i=None, step=0):
                def halves():
                    cut = slice(at, at + 512) if i is None else bass.ds(i * step + at, 512)
                    return split(as_cols(n), w[:, cut].rearrange("(k p) n -> p k n", p=P), 4)
                load(n, halves, i)

            def rows_unit(n, w):
                load(n, lambda: split(as_rows(n), w.rearrange("(k p) n -> p k n", p=P), 2))

            def mod_units(m):
                for j in range(2):
                    cols_unit(u_mod(m) + j, mod_w_2[m // NMOD], D * (m % NMOD) + 512 * j)

            for j in range(10):
                cols_unit(u_in(j), w_in[0], 512 * j)
                if j == 0:
                    sp.wait_ge(rows_loaded, 16 * 17)
                if j < NMOD:
                    mod_units(j)
            for m in range(NMOD, VECTORS):
                mod_units(m)
            rows_unit(U_CONV, conv_w_out[0])
            rows_unit(U_HGRN, hgrn_w_out[0])
            for u, w in ((U_MIX, w_mix_out), (U_XQ, xa_w_q), (U_XK, xa_w_k), (U_XV, xa_w_v), (U_XO, xa_w_o)):
                for j in range(2):
                    cols_unit(u + j, w[0], 512 * j)

            def expert_of(w, at):
                return w[0, at].rearrange("e (k p) n -> p (e k) n", p=P)

            with sp.Fori(0, EXPERTS // 2) as i:
                for j, w, view, half in ((0, moe_w_gate, as_cols, 4), (2, moe_w_up, as_cols, 4), (4, moe_w_down, as_rows, 2)):
                    for e in range(2):
                        n = U_MOE + j + e
                        load(n, lambda: split(view(n), expert_of(w, bass.ds(i * 2 + e, 1)), half), i)
            sp.wait_ge(rt_flag, 2)
            with sp.If(sp.value_load(overflow[0:1, 0:1], min_val=0, max_val=1)):
                with sp.Fori(0, EXPERTS) as e:
                    sp.wait_ge(dn_added, e + 1)
                    for j, w, k in ((0, moe_w_gate, KC), (1, moe_w_up, KC), (2, moe_w_down, 4)):
                        sp.dma_start(dn_w[:, j, :].rearrange("p (k n) -> p k n", k=k), expert_of(w, bass.ds(e, 1))).then_inc(dn_loaded, 16)

            def ffn_units(f, l, j):
                wg, wu, wd = ffn_w_gate_2[l, j], ffn_w_up_2[l, j], ffn_w_down_2[l, j]

                def gate_up(n, c, i=None):
                    def halves():
                        v = unit_of(n).rearrange("p (a k n) -> p a k n", a=2, k=KC)
                        cut = bass.ds(c * FCHUNK if i is None else i * (4 * FCHUNK) + c * FCHUNK, FCHUNK)
                        return tuple((v[:, a], w[:, cut].rearrange("(k p) n -> p k n", p=P)) for a, w in ((0, wg), (1, wu)))
                    load(n, halves, i)

                def down(n, c, chunks, i=None):
                    def halves():
                        size = chunks * FCHUNK
                        cut = bass.ds(c * FCHUNK if i is None else i * (4 * FCHUNK) + c * FCHUNK, size)
                        return split(as_rows(n), wd[cut, :].rearrange("(k p) n -> p k n", p=P), chunks)
                    load(n, halves, i)

                n = U_FFN[f]
                with sp.Fori(0, 2) as i:
                    for h in range(2):
                        gate_up(n + 3 * h, 2 * h, i)
                        down(n + 3 * h + 1, 2 * h, 2, i)
                        gate_up(n + 3 * h + 2, 2 * h + 1, i)
                gate_up(n + 12, 8)
                down(n + 13, 8, 2)
                gate_up(n + 14, 9)
                gate_up(n + 15, 10)
                down(n + 16, 10, 1)

            ffn_units(0, 0, 0)
            ffn_units(1, 0, 0)
            for j in range(6):
                cols_unit(U_ATT + j, attn_w_in_2[0], 512 * j)
            for j in range(2):
                cols_unit(U_ATTO + j, attn_w_out_2[0], 512 * j)
            ffn_units(2, 0, 1)
            ffn_units(3, 1, 0)
            for j, c in enumerate((2, 4, 3, 5, 0, 1)):
                cols_unit(U_CM + j, conv_w_in_2[0], 512 * c)
            for j in range(2):
                cols_unit(U_CMO + j, conv_w_out_2[0], 512 * j)
            ffn_units(4, 1, 1)
            for t in range(TT):
                sp.wait_ge(x_ready, TT * 10 + t + 1)
                sp.dma_start(out[0, t * P:t * P + P, :], xn[:, t, :]).then_inc(out_stored, 16)
            sp.wait_ge(out_stored, 16 * TT)

        @block.gpsimd
        def _(pool):
            for dst, src in ((masks, k_masks), (desc[:], k_desc), (scratch[:, 13440:13440 + P + PLACES], k_rank)):
                pool.dma_start(dst, src).then_inc(consts_loaded, 16)
            pool.dma_start(cx, mem[0].rearrange("(t p) d -> p t d", p=P)).then_inc(mem_loaded, 16)
            pool.dma_start(router_w[:, :, 0:GROUPS], router_group_w[0].rearrange("(k p) n -> p k n", p=P)).then_inc(consts_loaded, 16)
            pool.dma_start(router_w[:, :, GROUPS:], router_expert_w[0].rearrange("(k p) n -> p k n", p=P)).then_inc(consts_loaded, 16)
            pool.dma_start(router_b[:, 0:GROUPS], router_group_b[0].partition_broadcast(P)).then_inc(consts_loaded, 16)
            pool.dma_start(router_b[:, GROUPS:], router_expert_b[0].partition_broadcast(P)).then_inc(consts_loaded, 16)
            pool.wait_ge(mix_scan, 1)
            pool.dma_start(gate_b[:], final_norm_g.partition_broadcast(P)).then_inc(gain_loaded, 16)
            pool.wait_ge(norm_xn, 6)
            pool.dma_start(cx, ctx_2[0].rearrange("(t p) d -> p t d", p=P)).then_inc(ctx_loaded, 16)
            pool.wait_ge(x_ready, TT * 5)
            for dst, src in ((cos, k_rope[:, 0, :]), (sin, k_rope[:, 1, :]), (window, k_window), (lam_in, diff_lambda_2[0].partition_broadcast(P))):
                pool.dma_start(dst, src).then_inc(rope_loaded, 16)
            pool.wait_ge(norm_turned, 4 * 8)
            for t in range(TT):
                for r in range(2):
                    for a in range(T // GRID):
                        src = bass.AP(rpb_pad.tensor, (7 + a - 2 * t - r) * P, [[1, GRID], [15 * P, NAH], [1, GRID]])
                        pool.dma_start(bias[GRID * r:GRID * r + GRID, t::2, GRID * a:GRID * a + GRID], src).then_inc(bias_loaded, 16)
            pool.wait_ge(x_ready, TT * 10)
            pool.dma_start(gate_b[:], final_g_2.partition_broadcast(P)).then_inc(gain_loaded, 16)
        @block.scalar
        def _(act):
            link = Link(act, act_chain)

            def col(r, n=1, t=0):
                return cols[:, t, r:r + n]

            def norm_stats(r, src, turned=0, ready=None, squares=xn):
                if turned:
                    act.wait_ge(norm_turned, turned)
                for t in range(TT):
                    if ready:
                        act.wait_ge(ready[0], TT * ready[1] - TT + t + 1)
                    act.activation(squares[:, t, :], src[:, t, :], ACT.Square, accum_out=ss[:, t:t + 1]).then_inc(norm_sq, 1)
                    act.wait_ge(norm_sq, TT * r + t + 1)
                    act.activation(std[:, t:t + 1], ss[:, t:t + 1], ACT.Sqrt, bias=eps[:], scale=1.0 / D).then_inc(norm_std, 1)

            def norm_out(i, off, scale, shift=None):
                for c in range(4, KC):
                    act.wait_ge(norm_turned, 4 * i + (c // 2 + 1 if off is not None else 4))
                    act.activation(ht[:, c, off:off + T] if off is not None else merged[:, c, :], hi[:, c // 2, (c % 2) * T:(c % 2 + 1) * T], ACT.Identity,
                                   scale=scale[:, c:c + 1], bias=shift[:, c:c + 1] if shift is not None else 0.0
                                   ).then_inc(norm_ready, 1)

            vec = [(R_MIX, norm_mix_g), (R_XA, norm_xa_g), (R_MEM, norm_mem_g), (R_FFN, norm_ffn_g), (R_CONVB, conv_b),
                   (R_LNG, conv_ln_g), (R_LNB, conv_ln_b), (R_LB, hgrn_lb_logits), (R_ONORM, hgrn_onorm_g),
                   (R_SUBLN, diff_subln_g_2), (R_C, c_2)]
            act.dma_start(mats[:], k_mats).then_inc(mats_loaded, 16)
            for at, v in vec:
                s = v.rearrange("a (c p) -> (a c) p", p=P)
                act.dma_start(rows[at:at + s.shape[0], 0, :], s).then_inc(rows_loaded, 16)
            act.dma_start(rows[R_NG2:R_C, 0, :], norm_g_2.rearrange("l j (c p) -> (l j c) p", p=P)).then_inc(rows_loaded, 16)
            act.dma_start(rows[R_CCTX:R_END, 0, :], c_ctx_2.rearrange("(c p) -> c p", p=P)).then_inc(rows_loaded, 16)
            act.dma_start(rows[0:R2_END, 1, :], conv_w[0].rearrange("j (c p) -> (j c) p", p=P)).then_inc(rows_loaded, 16)
            act.dma_start(rows[0:R3_CONV2, 2, :], mod_b_2[0].rearrange("(c p) -> c p", p=P)).then_inc(rows_loaded, 16)
            act.dma_start(rows[R3_CONV2:R3_END, 2, :], conv_w_2[0].rearrange("j (c p) -> (j c) p", p=P)).then_inc(rows_loaded, 16)
            act.dma_start(rows[0:R4_END, 3, :], mod_b_2[1].rearrange("(c p) -> c p", p=P)).then_inc(rows_loaded, 16)
            act.wait_ge(set_up, 5)
            act.wait_ge(x_loaded, 16)
            norm_stats(0, x, 0)
            act.wait_ge(cols_ready, 5)
            act.activation(silu_c[:, :, 0], col(R_C, KC), ACT.Silu).then_inc(col_math, 1)
            act.activation(silu_c[:, :, 1], col(R_CCTX, KC), ACT.Silu).then_inc(col_math, 1)
            act.activation(lbc[:, 0, :], small[:, 0:CC], ACT.Sigmoid).then_inc(col_math, 1)

            norm_out(0, 0, col(R_MIX, KC))

            def mod_copied(m):
                wait_used(act, u_mod(m) + 1)
                act.activation(mrow[:, m % 2, :], hi[:, m % 4, 0:T], ACT.Copy).then_inc(md_copied, 1)

            def mod_cols(m):
                act.wait_ge(md_turned, m + 1)
                ps = hi[:, m % 4, T:2 * T].rearrange("p (b g w) -> p w g b", b=2, w=32)[:, 0:2]
                act.activation(mod[:, m // NMOD, m % NMOD].rearrange("p v (g b) -> p v g b", b=2), ps, ACT.Copy).then_inc(md_cols, 1)

            for j in range(10):
                if j in (1, 2, 3, 5):
                    src, dst, fun, done = {1: (lo[:, 2:4, :], sg, ACT.Sigmoid, mix_cg), 2: (lo[:, 0:2, :], qT, ACT.Silu, mix_q),
                                           3: (lo[:, 2:4, :], cum, ACT.Sigmoid, mix_f), 5: (lo[:, 2:4, :], grT, ACT.Silu, mix_g)}[j]
                    wait_used(act, u_in(j))
                    act.activation(dst, src, fun).then_inc(done, 1)
                elif j == 4:
                    act.wait_ge(mix_fk, 1)
                    act.activation(eb[0], qk[0], ACT.Ln).then_inc(mix_ln_f, 1)
                elif j >= 6:
                    wait_used(act, u_in(j))
                    dst = (gcT if j < 8 else grT2)[:, 4 * (j % 2):4 * (j % 2) + 4, :]
                    act.activation(dst, lo[:, 2 * (j % 2):2 * (j % 2) + 2, :], ACT.Sigmoid).then_inc(mix_gate, 1)
                if j < NMOD:
                    mod_copied(j)
                if j:
                    mod_cols(j - 1)
            for v in range(1, LEVELS + 4):
                if v <= LEVELS + 1:
                    act.wait_ge(lev_diff, v)
                    act.activation(eb[v % 2], eb[v % 2], ACT.Exp).then_inc(lev_exp, 1)
                if 2 <= v:
                    mod_copied(NMOD - 2 + v)
                if v >= 3:
                    mod_cols(NMOD - 3 + v)
            mod_cols(VECTORS - 1)
            act.wait_ge(cn_d, 1)
            act.activation(eb[0], acc, ACT.Square).then_inc(cn_sq, 1)
            act.wait_ge(cn_var, 1)
            act.activation(eb[1][:, 0, :], hi[:, 1, 0:T], ACT.Sqrt, bias=eps[:], scale=1.0).then_inc(cn_std, 1)
            act.wait_ge(cn_y, 1)
            for c in range(CC):
                act.activation(acc[:, c, :], acc[:, c, :], ACT.Silu, scale=col(R_LNG + c), bias=col(R_LNB + c)).then_inc(cn_act, 1)
            act.wait_ge(ho_o, 1)
            act.activation(eb[0], hi[:, 2:4, :], ACT.Square).then_inc(ho_sq, 1)
            act.wait_ge(ho_ms, 1)
            act.activation(eb[0], hi[:, 0:2, :], ACT.Sqrt, bias=eps[:], scale=1.0).then_inc(ho_std, 1)

            norm_stats(1, x, 4, (x_ready, 1))
            norm_out(1, 0, col(R_XA, KC))
            act.wait_ge(mem_loaded, 16)
            norm_stats(2, cx, 8)
            norm_out(2, T, col(R_MEM, KC))
            for j in range(2):
                wait_used(act, U_XQ + j)
                act.activation(xq[:, 4 * j:4 * j + 4, :], lo[:, 2 * j:2 * j + 2, :], ACT.Copy).then_inc(xa_q, 1)
            wait_used(act, U_XV)
            act.activation(xv[:, :, 0:512], lo[:, 0:2, :], ACT.Copy).then_inc(xa_v, 1)
            for h in range(XH):
                act.wait_ge(xa_nm, h + 1)
                for t in range(TT):
                    act.activation(xp[:, h, t, :], hi[:, h, t * T:t * T + T], ACT.Exp, scale=XD ** -0.5,
                                   bias=small[:, 16 + 2 * h + t:17 + 2 * h + t],
                                   accum_out=small[:, 24 + 2 * h + t:25 + 2 * h + t]).then_inc(xa_e, 1)
            for h in range(XH):
                act.wait_ge(xa_t, h + 1)
                act.activation(xpt[:, h % 2], lo[:, h % 2, :], ACT.Copy).then_inc(xa_pt, 1)

            norm_stats(3, x, 12, (x_ready, 2))
            norm_out(3, 0, col(R_FFN, KC))
            act.wait_ge(rt_d, 1)
            act.activation(part(4200, TT, GROUPS), part(4192, TT, GROUPS), ACT.Exp).then_inc(rt_e, 1)
            act.wait_ge(rt_d, 2)
            act.activation(small[:, 34:36], small[:, 32:34], ACT.Exp).then_inc(rt_e, 1)
            act.wait_ge(ctx_loaded, 16)
            norm_stats(4, cx, squares=part(8192, TT, D))
            for h in range(2):
                act.activation(ex_y[:, h * 512:h * 512 + 512], zero[:].broadcast_to([P, 512]), ACT.Copy).then_inc(ex_yd, 1)
            act.activation(back, zero[:].broadcast_to([P, T]), ACT.Copy).then_inc(ex_back, 1)
            with act.Fori(0, EXPERTS // 2) as i:
                for e in range(2):
                    wait_used(act, U_MOE + e, i)
                act.activation(ex_sg, lo[:, 0, :], ACT.Silu).then_inc(ex_sgd, 1)
                act.wait_ge(ex_turned, i + 1)
                act.activation(ex_hT, lo[:, 0, :], ACT.Copy).then_inc(ex_hTd, 1)
                act.wait_ge(ex_back_turned, i + 2)
                act.activation(back, lo[:, 1, 0:T], ACT.Copy).then_inc(ex_back, 1)
                for e in range(2):
                    wait_used(act, U_MOE + 4 + e, i)
                for h in range(2):
                    act.activation(ex_y[:, h * 512:h * 512 + 512], lo[:, 2 + h, :], ACT.Copy).then_inc(ex_yd, 1)
            act.wait_ge(rt_flag, 2)
            with act.If(act.value_load(overflow[0:1, 0:1], min_val=0, max_val=1)):
                with act.Fori(0, EXPERTS) as e:
                    for f in range(4):
                        act.wait_ge(dn_gu, e * 4 + (f + 1))
                        act.activation(dn_sg[:, f, :], lo[:, f, 0:T], ACT.Silu).then_inc(dn_sgd, 1)

            def split_up(f, c, b, it=None):
                n, w = up_unit(U_FFN[f], c, b)
                wait_unit(act, n, it)
                if nth(f, c, b) > 2:
                    act.wait_ge(ffn_gu, nth(f, c, b, it) - 2)
                act.activation(w_split[:, b, 0], w, ACT.Copy).then_inc(gs_hi, 1)

            def split_down(f, c, b, it=None):
                n, w = down_unit(U_FFN[f], c, b)
                wait_unit(act, n, it)
                if nth(f, c, b) > 2:
                    act.wait_ge(ffn_dn, nth(f, c, b, it) - 2)
                act.activation(d_split[:, b, 0], w, ACT.Copy).then_inc(ds_hi, 1)

            def ffn(f, i, r, src, ready, at, scale, shift, half_gate):
                if f == 0:
                    act.wait_ge(x_ready, TT * 3)
                else:
                    norm_stats(r, src, 4 * i, ready)
                if f % 2 == 0:
                    split_up(f, 0, 0)
                    split_up(f, 0, 1)
                norm_out(i, None, scale, shift)
                act.wait_ge(norm_ready, KC * (i + 1))
                for h in range(2):
                    act.activation(x_split[:, 0, 4 * h:4 * h + 4], merged[:, 4 * h:4 * h + 4], ACT.Copy).then_inc(xs_hi, 1)
                if f % 2 == 0:
                    split_down(f, 0, 0)
                    split_down(f, 0, 1)
                if f == 0:
                    act.wait_ge(xs_lo, 2)
                    norm_stats(5, x)
                gate(half_gate, 0.5)

                def chunk(c, it=None):
                    nf, nc_ = (f, c + 1) if c + 1 < NCHUNK else (f + 1, 0)
                    more = nc_ or nf in (1, 3)
                    for b in range(2):
                        act.wait_ge(ffn_gu, nth(f, c, b, it))
                        act.activation(ffn_sg[:, b, :], lo[:, b, 0:T], ACT.Silu).then_inc(ffn_sgd, 1)
                        if more:
                            split_up(nf, nc_, b, it)
                    for b in range(2):
                        if more:
                            split_down(nf, nc_, b, it)

                with act.Fori(0, 2) as it:
                    for c in range(4):
                        chunk(c, it)
                for c in range(8, NCHUNK):
                    chunk(c)

            def gate(g, scale):
                act.wait_ge(gate_turned, g + 1)
                act.wait_ge(gain_used, g + 1)
                act.activation(gate_b[:], lo[:, 2:4, :], ACT.Copy, scale=scale).then_inc(gate_ready, 1)

            act.wait_ge(md_scales, 1)
            ffn(0, 4, 4, cx, None, 0, mod_scale[:, 0], mod[:, 0, 0, 1], 0)
            ffn(1, 5, 6, x, (x_ready, 4), 1, mod_scale[:, 1], mod[:, 0, 0, 0], 1)

            norm_stats(7, x, 24, (x_ready, 5))
            norm_out(6, 0, mod_scale[:, 2], mod[:, 0, 3, 0])
            norm_stats(8, cx, 28, (ctx_ready, 1))
            norm_out(7, T, mod_scale[:, 3], mod[:, 0, 3, 1])
            wait_used(act, U_ATT)
            act.activation(qe[0:HD], lo[0:HD, 0:2, :], ACT.Copy).then_inc(at_qa, 1)
            act.activation(qo[HD:P], lo[HD:P, 0:2, :], ACT.Copy).then_inc(at_qa, 1)
            wait_used(act, U_ATT + 1)
            act.activation(kaT, hi[:, :, :], ACT.Copy).then_inc(at_ka, 1)
            wait_used(act, U_ATT + 3)
            act.activation(rawq, hi[:, 0:2, :], ACT.Copy).then_inc(at_qb, 1)
            wait_used(act, U_ATT + 4)
            act.activation(rawk, lo[:, :, 0:T], ACT.Copy).then_inc(at_kb, 1)
            act.activation(kbT[:, :, T:KEYS], lo[:, :, T:KEYS], ACT.Copy).then_inc(at_kb, 1)
            wait_used(act, U_ATT + 5)
            act.activation(vb, hi[:, :, :], ACT.Copy).then_inc(at_vb, 1)
            gate(2, 1.0)
            act.wait_ge(lam_d, 1)
            act.activation(small[:, 42:44], small[:, 40:42], ACT.Exp).then_inc(lam_e, 1)
            act.wait_ge(at_rope, 3)

            def na_exp(h):
                b = 2 * (h % 2)
                act.wait_ge(na_nm, h + 1)
                for t in range(TT):
                    act.activation(ap_[:, b + t, :], hi[:, b + t, :], ACT.Exp, scale=HD ** -0.5,
                                   bias=small[:, 48 + b + t:49 + b + t],
                                   accum_out=small[:, 52 + b + t:53 + b + t]).then_inc(na_e, 1)

            def na_copy(h):
                act.wait_ge(na_t, h + 1)
                act.activation(apt, lo[:, 0:2, :], ACT.Copy).then_inc(na_pt, 1)

            na_exp(0)
            na_exp(1)
            for h in range(NAH):
                na_copy(h)
                if h + 2 < NAH:
                    na_exp(h + 2)
            for h in range(DH):
                act.wait_ge(df_nm, h + 1)
                for m in range(4):
                    act.activation(ap_[:, m, :], hi[:, m, :], ACT.Exp, scale=HD ** -0.5, bias=small[:, 48 + m:49 + m],
                                   accum_out=small[:, 52 + m:53 + m]).then_inc(df_e, 1)
                act.wait_ge(df_t, h + 1)
                act.activation(apt, lo[:, 0:2, :], ACT.Copy).then_inc(df_pt, 1)
            act.wait_ge(df_o, DH)
            act.activation(dsq, dO, ACT.Square).then_inc(df_sq, 1)
            act.wait_ge(df_ms, 1)
            act.activation(dsq, hi[:, 0:2, :], ACT.Sqrt, bias=eps[:], scale=1.0).then_inc(df_std, 1)

            ffn(2, 8, 9, x, (x_ready, 6), 2, mod_scale[:, 4], mod[:, 0, 6, 0], 3)
            ffn(3, 9, 10, x, (x_ready, 7), 3, mod_scale[:, 5], mod[:, 1, 0, 0], 4)

            norm_stats(11, x, 40, (x_ready, 8))
            norm_out(10, 0, mod_scale[:, 6], mod[:, 1, 3, 0])
            for j in range(2):
                wait_used(act, U_CM + 2 * j)
                act.activation(cgs[:, 4 * j:4 * j + 4, :], (hi if j else lo)[:, 0:2, :], ACT.Copy).then_inc(cm_cg, 1)
            gate(5, 1.0)
            ffn(4, 11, 12, x, (x_ready, 9), 4, mod_scale[:, 7], mod[:, 1, 6, 0], 6)

            norm_stats(13, x, 48, (x_ready, 10))

        @block.tensor
        def _(pe):
            def mm(dst, lhsT, rhs, start=True, stop=True, **kw):
                return pe.matmul(dst, lhsT, rhs, start=start, stop=stop, **kw)

            def to_features(n, dst, rhs, chunks, last=True):
                for f in range(4):
                    for k in range(chunks):
                        ins = mm(dst(f), as_cols(n)[:, k, f * P:f * P + P], rhs(k), k == 0, k == chunks - 1)
                ins.then_inc(unit_used[n % RING], 1)

            def to_rows(n, dst, lhsT, tiles=TT):
                for t in range(tiles):
                    for k in range(KC):
                        ins = mm(dst(t), lhsT(k, t), as_cols(n)[:, k, :], k == 0, k == KC - 1)
                ins.then_inc(unit_used[n % RING], 1)

            def pair(ps, b):
                return lambda f: ps[:, b + f // 2, (f % 2) * T:(f % 2 + 1) * T]

            def norm(i):
                for t in range(TT):
                    pe.wait_ge(norm_xn, TT * i + t + 1)
                    for c in range(KC):
                        ins = pe.transpose(hi[:, c // 2, (c % 2) * T + t * P:(c % 2) * T + t * P + P], xn[:, t, c * P:c * P + P], ident)
                        if t == TT - 1 and c % 2:
                            ins.then_inc(norm_turned, 1)

            def normed(i):
                pe.wait_ge(norm_ready, KC * (i + 1))

            def ht_all(k):
                return ht[:, k, 0:T]

            def ht_tile(k, t):
                return ht[:, k, t * P:t * P + P]

            pe.wait_ge(mats_loaded, 16)
            pe.wait_ge(rows_loaded, 16 * 17)
            for t, n in enumerate((R_END, R2_END, R3_END, R4_END)):
                ins = pe.transpose(lo[:, 0, t * P:t * P + n], rows[0:n, t, :], ident[0:n, 0:n])
            ins.then_inc(cols_turned, 1)
            norm(0)
            normed(0)
            pe.wait_ge(cols_ready, 4)

            before = [None, None, (mix_u, 1), (mix_cg, 1), (mix_q, 1), (mix_f, 1), (mix_v, 1), (mix_g, 1), (mix_gate, 1), (mix_gate, 2)]
            def mod_product(m):
                if m >= 4:
                    pe.wait_ge(md_cols, m - 3)
                for j in range(2):
                    n = u_mod(m) + j
                    wait_unit(pe, n)
                    for k in range(KC):
                        for h in range(2):
                            g = 2 * j + h
                            ins = mm(hi[32 * g:32 * g + 32, m % 4, 0:T], silu_c[:, k, :], as_cols(n)[:, k, h * T:h * T + T],
                                     k == 0, k == KC - 1, tile_position=(0, 32 * g))
                    ins.then_inc(unit_used[n % RING], 1)

            def mod_turn(m):
                pe.wait_ge(md_copied, m + 1)
                for h in range(2):
                    ins = pe.transpose(hi[:, m % 4, T + h * P:T + h * P + P], mrow[:, m % 2, h * P:h * P + P], ident)
                ins.then_inc(md_turned, 1)

            pe.wait_ge(col_math, 2)
            for j in range(10):
                n = u_in(j)
                wait_unit(pe, n)
                if before[j]:
                    pe.wait_ge(*before[j])
                if j == 4:
                    to_rows(n, lambda t: lo[:, t, :], ht_tile)
                else:
                    to_features(n, pair(lo, 2 * (j % 2)), ht_all, KC)
                if j < NMOD:
                    mod_product(j)
                if j:
                    mod_turn(j - 1)

            def blocks(b):
                return lambda h, t: lo[:, b + h // 2, (h % 2) * T + t * P:(h % 2) * T + t * P + P]

            pe.wait_ge(consts_loaded, 16 * 7)
            pe.wait_ge(mix_fk, 1)
            pe.wait_ge(mix_gate, 3)
            for h in range(CC):
                for t in range(TT):
                    ins = mm(blocks(0)(h, t), kT[:, h, t * P:t * P + P], qT[:, h, t * P:t * P + P])
            ins.then_inc(lev_s, 1)
            mod_product(NMOD)
            for v in range(1, LEVELS + 1):
                pe.wait_ge(lev_qk, v)
                if v == 1:
                    pe.wait_ge(mix_gate, 4)
                else:
                    pe.wait_ge(lev_kept, v - 1)
                for h in range(CC):
                    for t in range(TT):
                        z = qk[v % 2][:, h, t * P:t * P + P]
                        ins = mm(blocks(2 * (v % 2))(h, t), z, z)
                ins.then_inc(lev_s, 1)
                mod_product(NMOD + v)
                mod_turn(NMOD + v - 1)
            pe.wait_ge(lev_qk, LEVELS + 1)
            pe.wait_ge(lev_kept, LEVELS)
            for h in range(CC):
                ins = mm(lo[:, 0, h * P:h * P + P], qk[0][:, h, 0:P], qk[0][:, h, P:T])
            ins.then_inc(lev_s, 1)
            mod_product(VECTORS - 1)
            for m in (VECTORS - 2, VECTORS - 1):
                mod_turn(m)
            for c in range(CC):
                if c == 0:
                    pe.wait_ge(conv_step, TAPS * CC)
                    pe.wait_ge(md_cols, VECTORS)
                ins = mm(hi[:, 0, 0:T], means[:, 0, :], acc[:, c, :], c == 0, c == CC - 1)
            ins.then_inc(cn_mean, 1)
            pe.wait_ge(cn_sq, 1)
            for c in range(CC):
                ins = mm(hi[:, 1, 0:T], means[:, 0, :], eb[0][:, c, :], c == 0, c == CC - 1)
            ins.then_inc(cn_var, 1)
            pe.wait_ge(lev_kept, LEVELS + 2)
            pe.wait_ge(mix_v, 1)
            for h in range(CC):
                o = hi[:, 2 + h // 2, (h % 2) * T:(h % 2 + 1) * T]
                v0, v1 = vtok[:, 0, h * P:h * P + P], vtok[:, 1, h * P:h * P + P]
                mm(o[:, 0:P], v0, ST[:, h, 0, :])
                mm(o[:, P:T], v0, S01[:, h // 2, h % 2, :], True, False)
                ins = mm(o[:, P:T], v1, ST[:, h, 1, :], False, True)
            ins.then_inc(ho_o, 1)
            wait_unit(pe, U_CONV)
            pe.wait_ge(cn_act, CC)

            def wide(n, dst, rhs):
                for f in range(KC):
                    for k in range(CC):
                        ins = mm(dst[:, f // 2, (f % 2) * T:(f % 2 + 1) * T], as_rows(n)[:, k, f * P:f * P + P], rhs[:, k, :], k == 0, k == CC - 1)
                ins.then_inc(unit_used[n % RING], 1)

            wide(U_CONV, lo, acc)
            pe.wait_ge(ho_sq, 1)
            pe.wait_ge(cn_std, 1)
            for b in range(2):
                ins = mm(hi[:, b, :], means[:, 1, :], eb[0][:, 2 * b:2 * b + 2, :])
            ins.then_inc(ho_ms, 1)
            wait_unit(pe, U_HGRN)
            pe.wait_ge(ho_n, 1)
            wide(U_HGRN, hi, oN)
            pe.wait_ge(mg_all, 1)
            for j in range(2):
                wait_unit(pe, U_MIX + j)
                to_rows(U_MIX + j, lambda t: hi[:, 2 * t + j, :], lambda k, t: merged[:, k, t * P:t * P + P])

            norm(1)
            normed(1)
            norm(2)
            for j in range(2):
                wait_unit(pe, U_XQ + j)
                if j == 0:
                    pe.wait_ge(mg_conv, 1)
                to_features(U_XQ + j, pair(lo, 2 * j), ht_all, KC)
            normed(2)
            for j in range(2):
                wait_unit(pe, U_XK + j)
                to_features(U_XK + j, pair(hi, 2 * j), lambda k: ht[:, k, T:KEYS], KC)
            for j in range(2):
                wait_unit(pe, U_XV + j)
                pe.wait_ge(xa_q, j + 1)
                to_rows(U_XV + j, lambda t: lo[:, 2 * j + t, :], lambda k, t: ht[:, k, T + t * P:T + t * P + P])
            pe.wait_ge(xa_k, 2)
            for h in range(XH):
                for t in range(TT):
                    for d in range(2):
                        ins = mm(hi[:, h, t * T:t * T + T], xq[:, 2 * h + d, t * P:t * P + P], xk[:, 2 * h + d, :], d == 0, d == 1)
                ins.then_inc(xa_s, 1)

            def xa_turn(h):
                pe.wait_ge(xa_p, TT * (h + 1))
                for t in range(TT):
                    for m in range(2):
                        ins = pe.transpose(lo[:, h % 2, m * T + t * P:m * T + t * P + P], xp[:, h, t, m * P:m * P + P], ident)
                ins.then_inc(xa_t, 1)

            def xa_value(h):
                pe.wait_ge(xa_pt, h + 1)
                if h >= 2:
                    pe.wait_ge(xa_o, h - 1)
                for d in range(2):
                    for m in range(2):
                        c = h * XD + d * P
                        ins = mm(lo[:, 2 + h % 2, d * T:d * T + T], xv[:, m, c:c + P], xpt[:, h % 2, m, :], m == 0, m == 1)
                ins.then_inc(xa_pv, 1)

            pe.wait_ge(xa_v, 1)
            pe.wait_ge(xa_v1, 1)
            xa_turn(0)
            for h in range(XH):
                if h + 1 < XH:
                    xa_turn(h + 1)
                xa_value(h)
            pe.wait_ge(xa_o, XH)
            for j in range(2):
                wait_unit(pe, U_XO + j)
                to_rows(U_XO + j, lambda t: hi[:, 2 * t + j, :], lambda k, t: xo[:, k, t * P:t * P + P])

            norm(3)
            normed(3)
            for t in range(TT):
                for k in range(KC):
                    ins = mm(lo[:, 0, t * 64:t * 64 + GROUPS + EXPERTS], ht_tile(k, t), router_w[:, k, :], k == 0, k == KC - 1)
            ins.then_inc(rt_logits, 1)
            pe.wait_ge(rt_comb, 1)
            ranks, counts = lo[:, 1, 0:TT * EXPERTS].rearrange("p (t n) -> p t n", t=TT), lo[:, 1, TT * EXPERTS:(TT + 1) * EXPERTS]
            mm(ranks[:, 0, :], before_me, chosen[:, 0, :])
            mm(ranks[:, 1, :], before_me, chosen[:, 1, :], True, False)
            mm(ranks[:, 1, :], means[:, 0, :], chosen[:, 0, :], False, True)
            for t in range(TT):
                ins = mm(counts, means[:, 0, :], chosen[:, t, :], t == 0, t == 1)
            ins.then_inc(rt_rank, 1)
            for t in range(TT):
                for h in range(2):
                    ins = mm(hi[:, 2 * t + h, :], zero[:].broadcast_to([P, P]), x[:, 0, 0:512], True, False, skip_group_check=True)
            ins.then_inc(ex_back_turned, 1)

            def gather():
                for c in range(KC):
                    for t in range(TT):
                        ins = mm(lo[:, 2 + c // 4, (c % 4) * P:(c % 4 + 1) * P], xn[:, t, c * P:c * P + P], onehot[:, t], t == 0, t == 1)
                    if c % 4 == 3:
                        ins.then_inc(ex_gathered, 1)

            def scatter(last):
                for t in range(TT):
                    for h in range(2):
                        ins = mm(hi[:, 2 * t + h, :], back[:, t * P:t * P + P], ex_y[:, h * 512:h * 512 + 512], False, last, skip_group_check=True)
                return ins

            pe.wait_ge(ex_onehot, 1)
            gather()
            with pe.Fori(0, EXPERTS // 2) as i:
                def places(e, n, bank, lhsT, k, rhs, chunks):
                    ins = mm(lo[PLACES * e:PLACES * e + PLACES, bank, :], lhsT[:, k, PLACES * e:PLACES * e + PLACES], rhs,
                             k == 0, k == chunks - 1, tile_position=(0, PLACES * e))
                    return ins

                pe.wait_ge(ex_hg, i * 2 + 2)
                for bank in range(2):
                    n = U_MOE + 2 * bank
                    if bank == 1:
                        pe.wait_ge(ex_back, i + 1)
                    for e in range(2):
                        wait_unit(pe, n + e, i)
                    for k in range(KC):
                        for e in range(2):
                            ins = places(e, n + e, bank, hg, k, as_cols(n + e)[:, k, :], KC)
                            if k == KC - 1:
                                ins.then_inc(unit_used[(n + e) % RING], 1)
                pe.wait_ge(ex_yd, i * 2 + 2)
                scatter(False)
                pe.wait_ge(ex_onehot, i + 2)
                gather()
                pe.wait_ge(ex_hd, i + 1)
                for f in range(4):
                    ins = pe.transpose(lo[:, 0, f * P:f * P + P], ex_h[:, f * P:f * P + P], ident)
                ins.then_inc(ex_turned, 1)
                pe.wait_ge(ex_weighted, i + 1)
                for t in range(TT):
                    ins = pe.transpose(lo[:, 1, t * P:t * P + P], weighted[:, t].rearrange("p e s -> p (e s)"), ident)
                ins.then_inc(ex_back_turned, 1)
                pe.wait_ge(ex_hTd, i + 1)
                pe.wait_ge(ex_hg, i * 2 + 4)
                n = U_MOE + 4
                for e in range(2):
                    wait_unit(pe, n + e, i)
                for h in range(2):
                    for k in range(4):
                        for e in range(2):
                            ins = places(e, n + e, 2 + h, ex_hT, k, as_rows(n + e)[:, k, h * 512:h * 512 + 512], 4)
                            if h == 1 and k == 3:
                                ins.then_inc(unit_used[(n + e) % RING], 1)
            pe.wait_ge(ex_yd, EXPERTS + 2)
            pe.wait_ge(ex_back, EXPERTS // 2 + 1)
            scatter(True).then_inc(ex_done, 1)
            pe.wait_ge(rt_flag, 2)
            with pe.If(pe.value_load(overflow[0:1, 0:1], min_val=0, max_val=1)):
                with pe.Fori(0, EXPERTS) as e:
                    pe.wait_ge(dn_loaded, e * 48 + 48)
                    for f in range(4):
                        for j in range(2):
                            w = dn_w[:, j, :].rearrange("p (k n) -> p k n", k=KC)
                            for k in range(KC):
                                ins = mm(lo[:, f, j * T:j * T + T], w[:, k, f * P:f * P + P], ht_all(k), k == 0, k == KC - 1)
                        ins.then_inc(dn_gu, 1)
                    w = dn_w[:, 2, :].rearrange("p (k n) -> p k n", k=4)
                    for f in range(4):
                        pe.wait_ge(dn_hd, e * 4 + (f + 1))
                        for t in range(TT):
                            for h in range(2):
                                ins = mm(hi[:, 2 * t + h, :], dn_h[:, f, t * P:t * P + P], w[:, f, h * 512:h * 512 + 512], f == 0, f == 3)
                    ins.then_inc(dn_down, 1)

            pe.wait_ge(x_ready, TT * 3)
            pe.wait_ge(md_scales, 1)

            def gate(l, i, v):
                for c in range(KC):
                    ins = mm(lo[:, 2 + c // 4, (c % 4) * P:(c % 4 + 1) * P], mod[:, l, i, v, c:c + 1].broadcast_to([P, P]), ident)
                ins.then_inc(gate_turned, 1)

            def ffn(f, i, l, m, v):
                norm(i)
                gate(l, m, v)
                pe.wait_ge(xs_lo, 2 * (f + 1))
                for t in range(TT):
                    for h in range(2):
                        mm(hi[:, 2 * t + h, :], zero_r[:].broadcast_to([P, P]), x_split[:, 0, 0:2, :], True, False, skip_group_check=True)
                halves = ((0, 0), (1, 0), (0, 1))

                def chunk(c, it=None):
                    n, last = U_FFN[f], c == NCHUNK - 1
                    for b in range(2):
                        pe.wait_ge(gs_lo, nth(f, c, b, it))
                        for a in range(2):
                            for k in range(KC):
                                for xh, wh in halves:
                                    ins = mm(lo[:, b, a * T:a * T + T], w_split[:, b, wh, a, k, :], x_split[:, xh, k, :],
                                             k == 0 and not xh + wh, k == KC - 1 and wh == 1)
                                    if b == 1 and a + k + xh + wh == 0:
                                        ins.then_inc(unit_used[up_unit(n, c, b)[0] % RING], 1)
                        ins.then_inc(ffn_gu, 1)
                    for b in range(2):
                        pe.wait_ge(ds_lo, nth(f, c, b, it))
                        pe.wait_ge(ffn_hd, nth(f, c, b, it))
                        for h in range(2):
                            for t in range(TT):
                                for xh, wh in halves:
                                    ins = mm(hi[:, 2 * t + h, :], h_split[:, b, xh, t * P:t * P + P], d_split[:, b, wh, h * 512:h * 512 + 512],
                                             False, last and b == 1 and wh == 1, skip_group_check=True)
                                    if b == 1 and h + t + xh + wh == 0 and (c % 2 or last):
                                        ins.then_inc(unit_used[down_unit(n, c, b)[0] % RING], 1)
                        ins.then_inc(ffn_dn, 1)

                with pe.Fori(0, 2) as it:
                    for c in range(4):
                        chunk(c, it)
                for c in range(8, NCHUNK):
                    chunk(c)

            ffn(0, 4, 0, 2, 1)
            ffn(1, 5, 0, 2, 0)

            norm(6)
            normed(6)
            norm(7)
            wait_unit(pe, U_ATT)
            to_features(U_ATT, pair(lo, 0), ht_all, KC)
            normed(7)
            both = lambda k: ht[:, k, :]
            keys = lambda k, t: ht[:, k, t * P:t * P + P]
            wait_unit(pe, U_ATT + 1)
            to_features(U_ATT + 1, lambda f: hi[:, f, :], both, KC)
            wait_unit(pe, U_ATT + 2)
            pe.wait_ge(at_qa, 2)
            to_rows(U_ATT + 2, lambda t: lo[:, t, :], keys, 4)
            wait_unit(pe, U_ATT + 3)
            pe.wait_ge(at_ka, 1)
            to_features(U_ATT + 3, pair(hi, 0), ht_all, KC)
            wait_unit(pe, U_ATT + 4)
            pe.wait_ge(at_va, 1)
            to_features(U_ATT + 4, lambda f: lo[:, f, :], both, KC)
            wait_unit(pe, U_ATT + 5)
            pe.wait_ge(at_qb, 1)
            to_rows(U_ATT + 5, lambda t: hi[:, t, :], keys, 4)
            pe.wait_ge(at_kb, 2)
            for b in range(2):
                ins = mm(lo[:, b, :], rot, rawq[:, 2 * b:2 * b + 2, :])
            ins.then_inc(at_rot, 1)
            for b in range(2):
                ins = mm(lo[:, 2 + b, :], rot, rawk[:, 2 * b:2 * b + 2, :])
            ins.then_inc(at_rot, 1)
            pe.wait_ge(at_rope, 3)
            gate(0, 5, 0)

            pe.wait_ge(at_zero, 4)
            pe.wait_ge(na_bias, 1)
            pe.wait_ge(at_vb, 1)

            def na_score(h):
                if h >= 2:
                    pe.wait_ge(na_e, TT * (h - 1))
                b = 2 * (h % 2)
                for t in range(TT):
                    mm(hi[:, b + t, :], (qo if h % 2 else qe)[:, h // 2, t * P:t * P + P], kaT[:, h // 2, :], True, False)
                    ins = mm(hi[:, b + t, 0:T], flip8, bias[:, 2 * h + t, :], False, True)
                ins.then_inc(na_s, 1)

            def turn(h, rows_of, ready, done):
                pe.wait_ge(*ready)
                for t in range(TT):
                    for c in range(4):
                        at = c * T + t * P
                        ins = pe.transpose(lo[:, at // 512, at % 512:at % 512 + P], rows_of(t)[:, c * P:c * P + P], ident)
                ins.then_inc(done, 1)

            def df_score(h):
                pe.wait_ge(na_e, TT * NAH)
                if h:
                    pe.wait_ge(df_e, 4 * h)
                for m in range(2):
                    for t in range(TT):
                        ins = mm(hi[:, 2 * m + t, :], (qbo if m else qbe)[:, h, t * P:t * P + P], kbT[:, h, :])
                ins.then_inc(df_s, 1)

            na_score(0)
            na_score(1)
            for h in range(NAH):
                turn(h, lambda t: ap_[:, 2 * (h % 2) + t, :], (na_p, TT * (h + 1)), na_t)
                if h + 2 < NAH:
                    na_score(h + 2)
                elif h == NAH - 1:
                    df_score(0)
                pe.wait_ge(na_pt, h + 1)
                if h == 0:
                    pe.wait_ge(gate_ready, 3)
                if h >= 4 and h % 2 == 0:
                    pe.wait_ge(na_o, h // 2 - 1)
                at = HD * (h % 2)
                for c in range(4):
                    ins = mm(lo[at:at + HD, 2 + (h // 2) % 2, 0:T], va[:, c, h * HD:h * HD + HD], apt[:, c, :], c == 0, c == 3,
                             tile_position=(0, at))
                ins.then_inc(na_pv, 1)

            for h in range(DH):
                if h + 1 < DH:
                    df_score(h + 1)
                turn(h, lambda t: ap_[:, t, :], (df_p, TT * (h + 1)), df_t)
                pe.wait_ge(df_pt, h + 1)
                pe.wait_ge(na_o, 4)
                if h >= 2:
                    pe.wait_ge(df_o, h - 1)
                for c in range(4):
                    ins = mm(lo[:, 2 + h % 2, 0:T], vb[:, c, h * P:h * P + P], apt[:, c, :], c == 0, c == 3)
                ins.then_inc(df_pv, 1)
            pe.wait_ge(df_sq, 1)
            for b in range(2):
                ins = mm(hi[:, b, :], means[:, 1, :], dsq[:, 2 * b:2 * b + 2, :])
            ins.then_inc(df_ms, 1)
            pe.wait_ge(df_n, 1)
            for j in range(2):
                wait_unit(pe, U_ATTO + j)
                to_rows(U_ATTO + j, lambda t: hi[:, 2 * t + j, :], lambda k, t: mergeT[:, k, t * P:t * P + P])

            ffn(2, 8, 0, 8, 0)
            ffn(3, 9, 1, 2, 0)

            norm(10)
            normed(10)
            for j, b in enumerate((lo[:, 0:2], lo[:, 2:4], hi[:, 0:2], hi[:, 2:4], lo[:, 0:2], lo[:, 2:4])):
                wait_unit(pe, U_CM + j)
                if j >= 4:
                    pe.wait_ge(cm_u, 1)
                to_features(U_CM + j, pair(b, 0), ht_all, KC)
            pe.wait_ge(cm_bg, 2)
            gate(1, 5, 0)
            for j in range(2):
                wait_unit(pe, U_CMO + j)
                to_rows(U_CMO + j, lambda t: hi[:, 2 * t + j, :], lambda k, t: vm[:, k, t * P:t * P + P])
            ffn(4, 11, 1, 8, 0)

        @block.vector
        def _(dve):
            link = Link(dve, dve_chain)
            tt, ts, stt = dve.tensor_tensor, dve.tensor_scalar, dve.scalar_tensor_tensor

            def col(r, n=1, t=0):
                return cols[:, t, r:r + n]

            def rstd_of(r, t):
                dve.wait_ge(norm_std, TT * r + t + 1)
                link(dve.reciprocal(rstd[:, t:t + 1], std[:, t:t + 1]))

            def norm_rows(r, src):
                for t in range(TT):
                    rstd_of(r, t)
                    ts(xn[:, t, :], src[:, t, :], rstd[:, t:t + 1], None, ALU.mult).then_inc(norm_xn, 1)

            def norm(i, r, src, off, scale, shift=None):
                if i != 4:
                    norm_rows(r, src)
                for c in range(4):
                    dve.wait_ge(norm_turned, 4 * i + (c // 2 + 1 if off is not None else 4))
                    ps = hi[:, c // 2, (c % 2) * T:(c % 2 + 1) * T]
                    dst = ht[:, c, off:off + T] if off is not None else merged[:, c, :]
                    if shift is None:
                        ins = ts(dst, ps, scale[:, c:c + 1], None, ALU.mult)
                    else:
                        ins = ts(dst, ps, scale[:, c:c + 1], shift[:, c:c + 1], ALU.mult, ALU.add)
                    ins.then_inc(norm_ready, 1)

            gates_used = [0]

            def gate_used(ins):
                gates_used[0] += 1
                ins.then_inc(gain_used, 1)
                dve.wait_ge(gain_used, gates_used[0])

            def residual(n, dst, signal, gated=False):
                for k in n:
                    wait_used(dve, k)
                for t in range(TT):
                    ps = hi[:, 2 * t:2 * t + 2, :].rearrange("p a n -> p (a n)")
                    if gated:
                        (gate_used if t == TT - 1 else link)(tt(ps, ps, gate_b[:], ALU.mult))
                    tt(dst[:, t, :], ps, dst[:, t, :], ALU.add).then_inc(signal, 1)


            dve.memset(eps[:], EPS).then_inc(set_up, 1)
            dve.memset(means[:, 0, :], 1.0 / CW).then_inc(set_up, 1)
            dve.memset(means[:, 1, :], 1.0 / P).then_inc(set_up, 1)
            dve.memset(silu_c[:], 0.0).then_inc(set_up, 1)
            dve.memset(upad[:, :, 0:TAPS - 1], 0.0).then_inc(set_up, 1)
            link(dve.memset(reset, 1.0))
            link(dve.memset(gate_b[:, 0::CHUNK], 0.0))
            link(dve.memset(zero[:], 0.0))
            link(dve.tensor_copy(zero_r[:], zero[:]))

            dve.wait_ge(cols_turned, 1)
            for t, n in enumerate((R_END, R2_END, R3_END, R4_END)):
                dve.tensor_copy(cols[:, t, 0:n], lo[:, 0, t * P:t * P + n]).then_inc(cols_ready, 1)
            dve.wait_ge(cols_ready, 4)
            tt(small[:, 0:CC], col(R_LB, CC), col(R_LB + CC, CC), ALU.subtract).then_inc(cols_ready, 1)
            link(ts(subln[:], col(R_SUBLN), 1.0 - LAM_INIT, None, ALU.mult))
            norm(0, 0, x, 0, col(R_MIX, KC))
            dve.wait_ge(col_math, 3)
            link(ts(lbc[:, 1, :], lbc[:, 0, :], -1.0, 1.0, ALU.mult, ALU.add))

            dve.wait_ge(mix_cg, 1)
            wait_used(dve, u_in(0))
            tt(upad[:, :, TAPS - 1:TAPS - 1 + T], lo[:, 0:2, :].rearrange("p a (b t) -> p (a b) t", b=2), sg, ALU.mult).then_inc(mix_u, 1)
            dve.wait_ge(mix_f, 1)
            for c in range(CC):
                link(ts(qk[0][:, c, :], cum[:, c, :], lbc[:, 1, c:c + 1], lbc[:, 0, c:c + 1], ALU.mult, ALU.add))
            ts(kT, qk[0], -1.0, 1.0, ALU.mult, ALU.add).then_inc(mix_fk, 1)
            wait_used(dve, u_in(4))
            dve.tensor_copy(vtok, lo[:, 0:2, :]).then_inc(mix_v, 1)
            dve.wait_ge(mix_ln_f, 1)
            dve.wait_ge(mix_fk, 1)
            dve.tensor_tensor_scan(cum.rearrange("p a b -> p (a b)"), reset, eb[0].rearrange("p a b -> p (a b)"), 0.0, ALU.mult, ALU.add
                                   ).then_inc(mix_scan, 1)
            dve.wait_ge(mix_u, 1)
            for c in range(CC):
                ts(acc[:, c, :], upad[:, c, 0:T], col(R2_TAPS + c, 1, 1), col(R_CONVB + c), ALU.mult, ALU.add).then_inc(conv_step, 1)
            with dve.Fori(1, TAPS) as j:
                for c in range(CC):
                    dve.wait_ge(conv_step, j * CC + (c + 1 - CC))
                    stt(acc[:, c, :], upad[:, c, bass.ds(j, T)], cols[:, 1, bass.ds(j * CC + c, 1)], acc[:, c, :], ALU.mult, ALU.add
                        ).then_inc(conv_step, 1)
            dve.wait_ge(mix_scan, 1)
            wait_used(dve, u_in(9))
            link(dve.memset(ST, 0.0))

            def halves(a, v):
                return a.rearrange("p h t -> p (h t)").rearrange("p (n a l) -> p n a l", a=2, l=1 << (v - 1))

            def diff(v):
                e = eb[v % 2]
                if v <= LEVELS:
                    c, o, half = halves(cum, v), halves(e, v), 1 << (v - 1)
                    edge = c[:, :, 0, half - 1:half].broadcast_to([P, CC * T // (2 * half), half])
                    link(tt(o[:, :, 0, :], edge, c[:, :, 0, :], ALU.subtract))
                    if v < LEVELS:
                        ins = tt(o[:, :, 1, :], c[:, :, 1, :], edge, ALU.subtract)
                    else:
                        ins = dve.tensor_copy(o[:, :, 1, :], c[:, :, 1, :])
                else:
                    def chunk(a, k):
                        return a[:, :, CHUNK * k:CHUNK * k + CHUNK]

                    def last(k):
                        return cum[:, :, CHUNK * k + CHUNK - 1:CHUNK * k + CHUNK]

                    both = small[:, 60:64].unsqueeze(2)
                    link(tt(both, last(0), last(1), ALU.add))
                    link(tt(chunk(e, 0), both.broadcast_to([P, CC, CHUNK]), chunk(cum, 0), ALU.subtract))
                    link(tt(chunk(e, 1), last(1).broadcast_to([P, CC, CHUNK]), chunk(cum, 1), ALU.subtract))
                    link(dve.tensor_copy(chunk(e, 2), chunk(cum, 2)))
                    ins = tt(chunk(e, 3), chunk(cum, 3), last(2).broadcast_to([P, CC, CHUNK]), ALU.add)
                ins.then_inc(lev_diff, 1)
                dve.wait_ge(lev_diff, v)

            def keep(v):
                dve.wait_ge(lev_s, v + 1)
                ps = lo[:, 2 * (v % 2):2 * (v % 2) + 2, :].rearrange("p a (b t s) -> p (a b) t s", b=2, t=TT)
                dve.copy_predicated(ST, masks[:, v, :].bitcast(U32).unsqueeze(1).unsqueeze(1).broadcast_to([P, CC, TT, P]), ps).then_inc(lev_kept, 1)
                dve.wait_ge(lev_kept, v + 1)

            diff(1)
            keep(0)
            for v in range(1, LEVELS + 2):
                if v <= LEVELS:
                    if v >= 2:
                        dve.wait_ge(lev_qk, v - 1)
                    diff(v + 1)
                dve.wait_ge(lev_exp, v)
                z, e = qk[v % 2], eb[v % 2]
                if v >= 3:
                    dve.wait_ge(lev_s, v - 1)
                if v <= LEVELS:
                    z4, e4, q4, k4 = (halves(a, v) for a in (z, e, qT, kT))
                    link(tt(z4[:, :, 0, :], k4[:, :, 0, :], e4[:, :, 0, :], ALU.mult))
                    tt(z4[:, :, 1, :], q4[:, :, 1, :], e4[:, :, 1, :], ALU.mult).then_inc(lev_qk, 1)
                    keep(v)
                else:
                    link(tt(z[:, :, 0:P], kT[:, :, 0:P], e[:, :, 0:P], ALU.mult))
                    tt(z[:, :, P:T], qT[:, :, P:T], e[:, :, P:T], ALU.mult).then_inc(lev_qk, 1)
            dve.wait_ge(lev_s, LEVELS + 2)
            dve.tensor_copy(S01, lo[:, 0, :].rearrange("p (a b s) -> p a b s", a=2, b=2)).then_inc(lev_kept, 1)
            dve.wait_ge(cn_mean, 1)
            tt(acc, acc, hi[:, 0, 0:T].unsqueeze(1).broadcast_to([P, CC, T]), ALU.subtract).then_inc(cn_d, 1)
            dve.wait_ge(cn_std, 1)
            link(dve.reciprocal(eb[1][:, 1, :], eb[1][:, 0, :]))
            dve.wait_ge(cn_sq, 1)
            tt(acc, acc, eb[1][:, 1, :].unsqueeze(1).broadcast_to([P, CC, T]), ALU.mult).then_inc(cn_y, 1)
            dve.wait_ge(ho_std, 1)
            link(dve.reciprocal(eb[1], eb[0]))
            link(tt(oN, hi[:, 2:4, :].rearrange("p a (b t) -> p (a b) t", b=2), eb[1], ALU.mult))
            dve.wait_ge(mix_g, 1)
            stt(oN, oN, col(R_ONORM), grT, ALU.mult, ALU.mult).then_inc(ho_n, 1)
            wait_used(dve, U_CONV)
            dve.wait_ge(mix_gate, 4)
            tt(merged, gcT, lo[:, :, :].rearrange("p a (b t) -> p (a b) t", b=2), ALU.mult).then_inc(mg_conv, 1)
            wait_used(dve, U_HGRN)
            link(tt(grT2, grT2, hi[:, :, :].rearrange("p a (b t) -> p (a b) t", b=2), ALU.mult))
            dve.wait_ge(mg_conv, 1)
            tt(merged, merged, grT2, ALU.add).then_inc(mg_all, 1)
            residual((U_MIX, U_MIX + 1), x, x_ready)

            norm(1, 1, x, 0, col(R_XA, KC))
            norm(2, 2, cx, T, col(R_MEM, KC))
            dve.wait_ge(md_cols, VECTORS)
            for l in range(2):
                for v in range(2):
                    m = mod[:, l, :, v, :]
                    ins = tt(m, m, cols[:, 2 + l, 0:NMOD * KC].rearrange("p (m c) -> p m c", c=KC), ALU.add)
                    link(ins)
            uses = [(0, 0, 1, 1), (0, 0, 1, 0), (0, 1, 4, 0), (0, 1, 4, 1), (0, 2, 7, 0), (1, 0, 1, 0), (1, 1, 4, 0), (1, 2, 7, 0)]
            for k, (l, j, m, v) in enumerate(uses):
                ins = stt(mod_scale[:, k, :], mod[:, l, m, v, :], 1.0, col(R_NG2 + (3 * l + j) * KC, KC), ALU.add, ALU.mult)
            ins.then_inc(md_scales, 1)
            for j in range(2):
                wait_used(dve, U_XK + j)
                dve.tensor_copy(xk[:, 4 * j:4 * j + 4, :], hi[:, 2 * j:2 * j + 2, :].rearrange("p a (b t) -> p (a b) t", b=2)).then_inc(xa_k, 1)
            wait_used(dve, U_XV + 1)
            dve.tensor_copy(xv[:, :, 512:1024], lo[:, 2:4, :]).then_inc(xa_v1, 1)
            for h in range(XH):
                dve.wait_ge(xa_s, h + 1)
                mx, nm = small[:, 8 + 2 * h:10 + 2 * h], small[:, 16 + 2 * h:18 + 2 * h]
                link(dve.tensor_reduce(mx, hi[:, h, :].rearrange("p (t m) -> p t m", t=TT), AX.X, ALU.max))
                ts(nm, mx, -XD ** -0.5, None, ALU.mult).then_inc(xa_nm, 1)

            def xa_out(h):
                dve.wait_ge(xa_pv, h + 1)
                dve.tensor_copy(xo[:, 2 * h:2 * h + 2, :], lo[:, 2 + h % 2, :].rearrange("p (d t) -> p d t", d=2)).then_inc(xa_o, 1)

            for h in range(XH):
                dve.wait_ge(xa_e, TT * (h + 1))
                r = small[:, 8 + 2 * h:10 + 2 * h]
                link(dve.reciprocal(r, small[:, 24 + 2 * h:26 + 2 * h]))
                for t in range(TT):
                    ts(xp[:, h, t, :], xp[:, h, t, :], r[:, t:t + 1], None, ALU.mult).then_inc(xa_p, 1)
                if h:
                    xa_out(h - 1)
            xa_out(XH - 1)
            residual((U_XO, U_XO + 1), x, x_ready)

            norm(3, 3, x, 0, col(R_FFN, KC))
            dve.wait_ge(rt_logits, 1)
            lgs = lo[:, 0, 0:128].rearrange("p (t n) -> p t n", t=TT)[:, :, 0:GROUPS + EXPERTS]
            link(tt(lg, lgs, router_b[:].unsqueeze(1).broadcast_to([P, TT, GROUPS + EXPERTS]), ALU.add))
            groups, experts = lg[:, :, 0:GROUPS], lg[:, :, GROUPS:].rearrange("p t (g j) -> p t g j", g=GROUPS)
            gmax, gsum, gp = small[:, 64:66].unsqueeze(2), small[:, 66:68].unsqueeze(2), small[:, 68:70].unsqueeze(2)
            m1, m2 = small[:, 70:72].unsqueeze(2), small[:, 72:74].unsqueeze(2)
            pick = small[:, 74:76].unsqueeze(2)
            ghot, shifted, gexp = part(4184, TT, GROUPS), part(4192, TT, GROUPS), part(4200, TT, GROUPS)
            inside, hot1, hot2, rest = (part(4208 + 16 * k, TT, PER_GROUP) for k in range(4))
            both, prod = part(4272, TT, PER_GROUP), part(4288, TT, PER_GROUP * GROUPS)

            def first_best(dst, v, best, n):
                link(tt(dst, v, best.broadcast_to([P, TT, n]), ALU.is_equal))
                link(tt(dst, dst, desc[:, PER_GROUP - n:].unsqueeze(1).broadcast_to([P, TT, n]), ALU.mult))
                link(dve.tensor_reduce(pick, dst, AX.X, ALU.max))
                link(tt(dst, dst, pick.broadcast_to([P, TT, n]), ALU.is_equal))

            link(dve.tensor_reduce(gmax, groups, AX.X, ALU.max))
            tt(shifted, groups, gmax.broadcast_to([P, TT, GROUPS]), ALU.subtract).then_inc(rt_d, 1)
            first_best(ghot, groups, gmax, GROUPS)
            prod4 = prod.rearrange("p t (g j) -> p t g j", g=GROUPS)
            for t in range(TT):
                link(tt(prod4[:, t], experts[:, t], ghot[:, t].unsqueeze(2).broadcast_to([P, GROUPS, PER_GROUP]), ALU.mult))
                link(dve.tensor_reduce(inside[:, t], prod4[:, t].rearrange("p g j -> p j g"), AX.X, ALU.add))
            link(dve.tensor_reduce(m1, inside, AX.X, ALU.max))
            first_best(hot1, inside, m1, PER_GROUP)
            link(stt(rest, hot1, -3.0e38, inside, ALU.mult, ALU.add))
            link(dve.tensor_reduce(m2, rest, AX.X, ALU.max))
            first_best(hot2, rest, m2, PER_GROUP)
            tt(small[:, 32:34].unsqueeze(2), m2, m1, ALU.subtract).then_inc(rt_d, 1)
            dve.wait_ge(rt_e, 1)
            link(dve.tensor_reduce(gsum, gexp, AX.X, ALU.add))
            link(dve.reciprocal(gp, gsum))
            dve.wait_ge(rt_e, 2)
            link(ts(small[:, 36:38], small[:, 34:36], 1.0, None, ALU.add))
            link(dve.reciprocal(small[:, 38:40], small[:, 36:38]))
            w1, w2 = small[:, 38:40].unsqueeze(2), small[:, 34:36].unsqueeze(2)
            link(tt(w1, w1, gp, ALU.mult))
            link(tt(w2, w2, w1, ALU.mult))
            link(tt(hot1, hot1, w1.broadcast_to([P, TT, PER_GROUP]), ALU.mult))
            link(tt(hot2, hot2, w2.broadcast_to([P, TT, PER_GROUP]), ALU.mult))
            link(tt(both, hot1, hot2, ALU.add))
            comb4 = comb[:, :, :].rearrange("p t (g j) -> p t g j", g=GROUPS)
            for t in range(TT):
                ins = tt(comb4[:, t], ghot[:, t].unsqueeze(2).broadcast_to([P, GROUPS, PER_GROUP]),
                         both[:, t].unsqueeze(1).broadcast_to([P, GROUPS, PER_GROUP]), ALU.mult)
                if t == 0:
                    link(ins)
            link(ins)
            ts(chosen, comb[:, :, :], 0.0, float(CW), ALU.is_gt, ALU.mult).then_inc(rt_comb, 1)
            link(dve.memset(place, -1.0))
            dve.wait_ge(rt_rank, 1)
            ranks = lo[:, 1, 0:TT * EXPERTS].rearrange("p (t n) -> p t n", t=TT)
            link(stt(count, ranks, 1.0, chosen, ALU.add, ALU.mult))
            link(ts(place[:, :, 0:EXPERTS], count, 1.0 / CW, -1.0, ALU.mult, ALU.add))
            link(dve.tensor_reduce(small[:, 80:81], lo[:, 1, TT * EXPERTS:(TT + 1) * EXPERTS], AX.X, ALU.max))
            ts(small[:, 81:82], small[:, 80:81], float(PLACES), None, ALU.is_gt).then_inc(rt_flag, 1)
            dve.wait_ge(rt_flag, 1)
            dve.tensor_copy(overflow[:], small[:, 81:82]).then_inc(rt_flag, 1)
            numbers4 = numbers.unsqueeze(1).unsqueeze(1).broadcast_to([P, TT, 2, PLACES])

            def one_hots(at):
                tt(onehot, numbers4, place[:, :, at].unsqueeze(3).broadcast_to([P, TT, 2, PLACES]), ALU.is_equal).then_inc(ex_onehot, 1)

            def gathered(i=None):
                for j in range(2):
                    dve.wait_ge(ex_gathered, j + 1 if i is None else i * 2 + (j + 3))
                    tt(hg[:, 4 * j:4 * j + 4, :], lo[:, 2 + j, :].rearrange("p (c s) -> p c s", c=4),
                       col(R_FFN + 4 * j, 4).unsqueeze(2).broadcast_to([P, 4, 2 * PLACES]), ALU.mult).then_inc(ex_hg, 1)

            one_hots(slice(0, 2))
            gathered()
            with dve.Fori(0, EXPERTS // 2) as i:
                dve.wait_ge(ex_onehot, i + 1)
                dve.wait_ge(ex_back_turned, i + 1)
                tt(weighted, onehot, comb[:, :, bass.ds(i * 2, 2)].unsqueeze(3).broadcast_to([P, TT, 2, PLACES]), ALU.mult).then_inc(ex_weighted, 1)
                dve.wait_ge(ex_weighted, i + 1)
                one_hots(bass.ds(i * 2 + 2, 2))
                for e in range(2):
                    wait_used(dve, U_MOE + 2 + e, i)
                dve.wait_ge(ex_sgd, i + 1)
                tt(ex_h, ex_sg, lo[:, 1, :], ALU.mult).then_inc(ex_hd, 1)
                gathered(i)
            norm_rows(4, cx)
            dve.wait_ge(ex_done, 1)
            x2 = x[:, :, :].rearrange("p t (h n) -> p (t h) n", h=2)
            tt(x2, x2, hi[:, :, :], ALU.add).then_inc(moe_done, 1)
            dve.wait_ge(moe_done, 1)
            with dve.If(dve.value_load(overflow[0:1, 0:1], min_val=0, max_val=1)):
                ts(chosen, place[:, :, 0:EXPERTS], float(PLACES), None, ALU.is_ge).then_inc(rt_flag, 1)
                dve.wait_ge(rt_flag, 3)
                tt(comb[:, :, :], comb[:, :, :], chosen, ALU.mult).then_inc(dn_added, 1)
                with dve.Fori(0, EXPERTS) as e:
                    for f in range(4):
                        dve.wait_ge(dn_sgd, e * 4 + (f + 1))
                        tt(dn_h[:, f, :], dn_sg[:, f, :], lo[:, f, T:2 * T], ALU.mult).then_inc(dn_hd, 1)
                    dve.wait_ge(dn_down, e + 1)
                    dve.wait_ge(dn_added, e + 1)
                    for t in range(TT):
                        for h in range(2):
                            xs = x[:, t, h * 512:h * 512 + 512]
                            ins = stt(xs, hi[:, 2 * t + h, :], comb[:, t, bass.ds(e, 1)], xs, ALU.mult, ALU.add)
                    ins.then_inc(dn_added, 1)
                dve.wait_ge(dn_added, EXPERTS + 1)
            tt(tmp[:, 0:1], eps[:], eps[:], ALU.add).then_inc(x_ready, TT)

            def split_up(f, c, b, it=None):
                dve.wait_ge(gs_hi, nth(f, c, b, it))
                tt(w_split[:, b, 1], up_unit(U_FFN[f], c, b)[1], w_split[:, b, 0].bitcast(F32), ALU.subtract).then_inc(gs_lo, 1)

            def split_down(f, c, b, it=None):
                dve.wait_ge(ds_hi, nth(f, c, b, it))
                tt(d_split[:, b, 1], down_unit(U_FFN[f], c, b)[1], d_split[:, b, 0].bitcast(F32), ALU.subtract).then_inc(ds_lo, 1)

            def ffn(f, i, src, scale, shift, signal):
                norm(i, i + 1 if i > 4 else 4, src, None, scale, shift)
                for h in range(2):
                    dve.wait_ge(xs_hi, 2 * f + h + 1)
                    half = slice(4 * h, 4 * h + 4)
                    tt(x_split[:, 1, half], merged[:, half], x_split[:, 0, half].bitcast(F32), ALU.subtract).then_inc(xs_lo, 1)
                if f % 2 == 0:
                    for split in (split_up, split_down):
                        for b in range(2):
                            split(f, 0, b)
                if f == 0:
                    dve.wait_ge(gain_loaded, 16)
                    dve.wait_ge(norm_std, TT * 6)
                    link(dve.reciprocal(rstd[:], std[:]))
                    for t in range(TT):
                        ins = stt(x[:, t, :], x[:, t, :], rstd[:, t:t + 1], gate_b[:], ALU.mult, ALU.mult)
                    gate_used(ins)
                    tt(tmp[:, 0:1], eps[:], eps[:], ALU.add).then_inc(x_ready, TT)

                def chunk(c, it=None):
                    nf, nc_ = (f, c + 1) if c + 1 < NCHUNK else (f + 1, 0)
                    more = nc_ or nf in (1, 3)
                    for b in range(2):
                        h32 = ffn_h[:, b, :]
                        dve.wait_ge(ffn_sgd, nth(f, c, b, it))
                        tt(h32, ffn_sg[:, b, :], lo[:, b, T:2 * T], ALU.mult).then_inc(ffn_h32, 1)
                        dve.wait_ge(ffn_h32, nth(f, c, b, it) * 2 - 1)
                        dve.tensor_copy(h_split[:, b, 0], h32).then_inc(ffn_h32, 1)
                        dve.wait_ge(ffn_h32, nth(f, c, b, it) * 2)
                        tt(h_split[:, b, 1], h32, h_split[:, b, 0].bitcast(F32), ALU.subtract).then_inc(ffn_hd, 1)
                        if more:
                            split_up(nf, nc_, b, it)
                    for b in range(2):
                        if more:
                            split_down(nf, nc_, b, it)

                with dve.Fori(0, 2) as it:
                    for c in range(4):
                        chunk(c, it)
                for c in range(8, NCHUNK):
                    chunk(c)
                g = (0, 1, 3, 4, 6)[f]
                dve.wait_ge(gate_ready, g + 1)
                dve.wait_ge(ffn_dn, nth(f, NCHUNK - 1, 1))
                residual((), src, signal, True)

            ffn(0, 4, cx, mod_scale[:, 0], mod[:, 0, 0, 1], ctx_ready)
            ffn(1, 5, x, mod_scale[:, 1], mod[:, 0, 0, 0], x_ready)

            norm(6, 7, x, 0, mod_scale[:, 2], mod[:, 0, 3, 0])
            for z, a in ((qe, HD), (qo, 0), (qbe, HD), (qbo, 0)):
                dve.memset(z[a:a + HD], 0.0).then_inc(at_zero, 1)
            norm(7, 8, cx, T, mod_scale[:, 3], mod[:, 0, 3, 1])
            wait_used(dve, U_ATT + 2)
            dve.tensor_copy(va, lo[:, :, :]).then_inc(at_va, 1)
            dve.wait_ge(bias_loaded, 16 * 16)
            dve.wait_ge(rope_loaded, 64)
            tt(bias, bias, window.unsqueeze(1).broadcast_to([P, 2 * NAH, T]), ALU.add).then_inc(na_bias, 1)
            cosb, sinb = (a.unsqueeze(1).broadcast_to([P, CC, T]) for a in (cos, sin))
            dve.wait_ge(at_rot, 1)
            link(tt(rawq, rawq, cosb, ALU.mult))
            link(tt(rtmp, lo[:, 0:2, :].rearrange("p a (b t) -> p (a b) t", b=2), sinb, ALU.mult))
            tt(qbe[0:HD], rawq[0:HD], rtmp[0:HD], ALU.add).then_inc(at_rope, 1)
            tt(qbo[HD:P], rawq[HD:P], rtmp[HD:P], ALU.add).then_inc(at_rope, 1)
            dve.wait_ge(at_rot, 2)
            link(tt(rawk, rawk, cosb, ALU.mult))
            dve.wait_ge(at_rope, 2)
            link(tt(rtmp, lo[:, 2:4, :].rearrange("p a (b t) -> p (a b) t", b=2), sinb, ALU.mult))
            tt(kbT[:, :, 0:T], rawk, rtmp, ALU.add).then_inc(at_rope, 1)
            link(tt(lam_in[:, 0, :], lam_in[:, 0, :], lam_in[:, 1, :], ALU.mult))
            link(tt(lam_in[:, 2, :], lam_in[:, 2, :], lam_in[:, 3, :], ALU.mult))
            dve.tensor_reduce(small[:, 40:42], lam_in[:, 0::2, :], AX.X, ALU.add).then_inc(lam_d, 1)
            dve.wait_ge(lam_e, 1)
            lam = small[:, 44:45]
            link(tt(lam, small[:, 42:43], small[:, 43:44], ALU.subtract))
            link(ts(lam, lam, LAM_INIT, None, ALU.add))

            def na_max(h):
                dve.wait_ge(na_s, h + 1)
                b = 2 * (h % 2)
                link(dve.tensor_reduce(small[:, 56 + b:58 + b], hi[:, b:b + 2, :], AX.X, ALU.max))
                ts(small[:, 48 + b:50 + b], small[:, 56 + b:58 + b], -HD ** -0.5, None, ALU.mult).then_inc(na_nm, 1)

            def na_out(h):
                dve.wait_ge(na_pv, h + 1)
                dve.tensor_copy(mergeT[:, h // 2, :], lo[:, 2 + (h // 2) % 2, 0:T]).then_inc(na_o, 1)

            def df_max(h):
                dve.wait_ge(df_s, h + 1)
                link(dve.tensor_reduce(small[:, 56:60], hi[:, :, :], AX.X, ALU.max))
                ts(small[:, 48:52], small[:, 56:60], -HD ** -0.5, None, ALU.mult).then_inc(df_nm, 1)

            def df_out(h):
                dve.wait_ge(df_pv, h + 1)
                dve.tensor_copy(dO[:, h, :], lo[:, 2 + h % 2, 0:T]).then_inc(df_o, 1)

            na_max(0)
            na_max(1)
            for h in range(NAH):
                b = 2 * (h % 2)
                dve.wait_ge(na_e, TT * (h + 1))
                link(dve.reciprocal(small[:, 76 + b:78 + b], small[:, 52 + b:54 + b]))
                for t in range(TT):
                    ts(ap_[:, b + t, :], ap_[:, b + t, :], small[:, 76 + b + t:77 + b + t], None, ALU.mult).then_inc(na_p, 1)
                if h + 2 < NAH:
                    na_max(h + 2)
                if h and h % 2 == 0:
                    na_out(h - 1)
            df_max(0)
            na_out(NAH - 1)
            for h in range(DH):
                dve.wait_ge(df_e, 4 * (h + 1))
                r = small[:, 76:80]
                link(dve.reciprocal(r, small[:, 52:56]))
                link(ts(r[:, 2:4], r[:, 2:4], lam, None, ALU.mult))
                for t in range(TT):
                    link(ts(ap_[:, 2 + t, :], ap_[:, 2 + t, :], r[:, 2 + t:3 + t], None, ALU.mult))
                    stt(ap_[:, t, :], ap_[:, t, :], r[:, t:t + 1], ap_[:, 2 + t, :], ALU.mult, ALU.subtract).then_inc(df_p, 1)
                if h + 1 < DH:
                    df_max(h + 1)
                if h:
                    df_out(h - 1)
            df_out(DH - 1)
            dve.wait_ge(df_std, 1)
            link(dve.reciprocal(dsq, dsq))
            dve.wait_ge(df_o, DH)
            stt(mergeT[:, CC:KC, :], dO, subln[:], dsq, ALU.mult, ALU.mult).then_inc(df_n, 1)
            dve.wait_ge(gate_ready, 3)
            residual((U_ATTO, U_ATTO + 1), x, x_ready, True)

            ffn(2, 8, x, mod_scale[:, 4], mod[:, 0, 6, 0], x_ready)
            ffn(3, 9, x, mod_scale[:, 5], mod[:, 1, 0, 0], x_ready)

            norm(10, 11, x, 0, mod_scale[:, 6], mod[:, 1, 3, 0])
            link(dve.memset(up2[:, :, 0:T + 2:T + 1], 0.0))
            for j in range(2):
                wait_used(dve, U_CM + 2 * j + 1)
                dve.wait_ge(cm_cg, j + 1)
                ins = tt(up2[:, 4 * j:4 * j + 4, 1:T + 1], (hi if j else lo)[:, 2:4, :].rearrange("p a (b t) -> p (a b) t", b=2),
                         cgs[:, 4 * j:4 * j + 4, :], ALU.mult)
                ins.then_inc(cm_u, 1)
            dve.wait_ge(cm_u, 2)
            for c in range(KC):
                taps = [col(R3_CONV2 + j * KC + c, 1, 2) for j in range(3)]
                link(ts(vm[:, c, :], up2[:, c, 0:T], taps[0], None, ALU.mult))
                for j in (1, 2):
                    link(stt(vm[:, c, :], up2[:, c, j:j + T], taps[j], vm[:, c, :], ALU.mult, ALU.add))
            for j in range(2):
                wait_used(dve, U_CM + 4 + j)
                v = vm[:, 4 * j:4 * j + 4, :]
                tt(v, v, lo[:, 2 * j:2 * j + 2, :].rearrange("p a (b t) -> p (a b) t", b=2), ALU.mult).then_inc(cm_bg, 1)
            dve.wait_ge(gate_ready, 6)
            residual((U_CMO, U_CMO + 1), x, x_ready, True)
            ffn(4, 11, x, mod_scale[:, 7], mod[:, 1, 6, 0], x_ready)

            dve.wait_ge(gain_loaded, 32)
            dve.wait_ge(norm_turned, 48)
            for t in range(TT):
                rstd_of(13, t)
                stt(xn[:, t, :], x[:, t, :], rstd[:, t:t + 1], gate_b[:], ALU.mult, ALU.mult).then_inc(x_ready, 1)


_INS = ['x', 'mem', 'norm_mix_g', 'w_in', 'conv_w', 'conv_b', 'conv_ln_g', 'conv_ln_b', 'conv_w_out', 'hgrn_lb_logits',
        'hgrn_onorm_g', 'hgrn_w_out', 'w_mix_out', 'norm_xa_g', 'norm_mem_g', 'xa_w_q', 'xa_w_k', 'xa_w_v', 'xa_w_o',
        'norm_ffn_g', 'router_group_w', 'router_group_b', 'router_expert_w', 'router_expert_b', 'moe_w_gate', 'moe_w_up',
        'moe_w_down', 'final_norm_g', 'c_2', 'ctx_2', 'c_ctx_2', 'mod_w_2', 'mod_b_2', 'norm_g_2', 'ffn_w_gate_2',
        'ffn_w_up_2', 'ffn_w_down_2', 'attn_w_in_2', 'attn_w_out_2', 'rpb_pad', 'diff_lambda_2', 'diff_subln_g_2',
        'conv_w_in_2', 'conv_w_out_2', 'conv_w_2', 'final_g_2']


def constants():
    import numpy as np

    f = np.float32
    mats = np.zeros((P, 3, P), f)
    mats[:, 0] = np.eye(P)
    for a in range(0, P, GRID):
        mats[a:a + GRID, 1, a:a + GRID] = 8.0 * np.eye(GRID)[::-1]
    for i in range(0, P, 2):
        mats[i + 1, 2, i], mats[i, 2, i + 1] = -1.0, 1.0
    s, t = np.arange(P)[:, None], np.arange(P)[None, :]
    masks = np.zeros((P, 8, P), f)
    masks[:, 0] = np.eye(P)
    for v in range(1, 8):
        half = 1 << (v - 1)
        masks[:, v] = (s // (2 * half) == t // (2 * half)) & (s // half % 2 == 0) & (t // half % 2 == 1)
    n_freq = HD // 4
    inv = f(10000.0) ** (-np.arange(n_freq, dtype=f) / f(n_freq))
    tok = np.arange(T)
    ang = np.concatenate([(tok // GRID).astype(f)[:, None] * inv, (tok % GRID).astype(f)[:, None] * inv], axis=-1)
    rope = np.zeros((P, 2, T), f)
    pair = np.arange(P) % HD // 2
    rope[:, 0], rope[:, 1] = np.cos(ang).T[pair], np.sin(ang).T[pair]
    qc = GRID - 1 - np.arange(P) % GRID
    start = np.clip(qc - 8, 0, GRID - 16)
    kc = np.arange(T) % GRID
    window = np.where((kc >= start[:, None]) & (kc < start[:, None] + 16), f(0), f(-1e30)).astype(f)
    desc = np.tile(np.arange(PER_GROUP, 0, -1, dtype=f), (P, 1))
    rank = np.zeros((P, P + PLACES), f)
    rank[:, 0:P] = (s < t) / f(CW)
    rank[:, P:] = np.arange(PLACES)
    return {"k_mats": mats, "k_masks": masks, "k_rope": rope, "k_window": window, "k_desc": desc, "k_rank": rank}


def kernel(**inputs):
    import numpy as _np
    import concourse.bacc as _bacc
    from concourse import mybir as _mybir
    from concourse.bass_utils import run_bass_kernel_spmd as _run

    nc = _bacc.Bacc("TRN2", target_bir_lowering=False, num_devices=1)
    tables = constants()
    rpb = _np.asarray(inputs["na_rpb_2"])[0]
    pad = GRID - 16
    tables["rpb_pad"] = _np.pad(rpb, ((0, 0), (0, 0), (pad, P - pad - rpb.shape[-1])))
    arrays, args = {}, []
    for name in _INS + ["k_mats", "k_masks", "k_rope", "k_window", "k_desc", "k_rank"]:
        a = _np.ascontiguousarray(tables[name] if name in tables else inputs[name])
        arrays[f"in_{name}_dram"] = a
        args.append(nc.dram_tensor(f"in_{name}_dram", a.shape, _mybir.dt.from_np(a.dtype), kind="ExternalInput").ap())
    args.append(nc.dram_tensor("out_0_dram", (1, T, D), F32, kind="ExternalOutput").ap())
    program(nc, *args)
    r = _run(nc, [arrays], core_ids=[0])
    return r.results[0]["out_0_dram"]
```

```python
from contextlib import ExitStack

import concourse.bass as bass
from concourse import mybir

F32 = mybir.dt.float32
U32 = mybir.dt.uint32
I32 = mybir.dt.int32
F32R = mybir.dt.float32r
ALU = mybir.AluOpType
ACT = mybir.ActivationFunctionType
AX = mybir.AxisListType

P = 128
T = 256
TT = T // P
D = 1024
KC = D // P
CW = 512
CC = CW // P
TAPS = 31
CHUNK = 64
XH = 4
XD = D // XH
GROUPS, PER_GROUP = 4, 8
EXPERTS = GROUPS * PER_GROUP
FF = 512
PLACES = 64
FF2 = 2816
FCHUNK = 256
NCHUNK = FF2 // FCHUNK
NMOD = 9
NAH, HD = 8, 64
DH = 4
GRID = 64
KEYS = 2 * T
EPS = 1e-6
LAM_INIT = 0.2

RING = 6
UNIT = 4096

VECTORS = 2 * NMOD


def u_in(j):
    return 3 * min(j, NMOD) + max(j - NMOD, 0)


def u_mod(m):
    return 3 * m + 1 if m < NMOD else u_in(10) + 2 * (m - NMOD)


U_CONV = u_mod(VECTORS)
U_HGRN, U_MIX = U_CONV + 1, U_CONV + 2
U_XQ, U_XK, U_XV, U_XO = (U_MIX + 2 * k for k in range(1, 5))
U_MOE = U_XO + 2
FFN_UNITS = NCHUNK + (NCHUNK + 1) // 2
U_FFN = [0] * 5
U_FFN[0] = U_MOE + 3 * EXPERTS
U_FFN[1] = U_FFN[0] + FFN_UNITS
U_ATT = U_FFN[1] + FFN_UNITS
U_ATTO = U_ATT + 6
U_FFN[2] = U_ATTO + 2
U_FFN[3] = U_FFN[2] + FFN_UNITS
U_CM = U_FFN[3] + FFN_UNITS
U_CMO = U_CM + 6
U_FFN[4] = U_CMO + 2

R_MIX, R_XA, R_MEM, R_FFN = 0, 8, 16, 24
R_CONVB, R_LNG, R_LNB, R_LB, R_ONORM, R_SUBLN, R_NG2, R_C, R_CCTX, R_END = 32, 36, 40, 44, 52, 53, 54, 102, 110, 118
R2_TAPS, R2_END = 0, TAPS * CC
R3_MODB, R3_CONV2, R3_END = 0, 72, 96
R4_END = 72

SCRATCH = 14336


def program(nc, x_in, mem, norm_mix_g, w_in, conv_w, conv_b, conv_ln_g, conv_ln_b, conv_w_out, hgrn_lb_logits,
            hgrn_onorm_g, hgrn_w_out, w_mix_out, norm_xa_g, norm_mem_g, xa_w_q, xa_w_k, xa_w_v, xa_w_o, norm_ffn_g,
            router_group_w, router_group_b, router_expert_w, router_expert_b, moe_w_gate, moe_w_up, moe_w_down,
            final_norm_g, c_2, ctx_2, c_ctx_2, mod_w_2, mod_b_2, norm_g_2, ffn_w_gate_2, ffn_w_up_2, ffn_w_down_2,
            attn_w_in_2, attn_w_out_2, rpb_pad, diff_lambda_2, diff_subln_g_2, conv_w_in_2, conv_w_out_2, conv_w_2,
            final_g_2, k_mats, k_masks, k_rope, k_window, k_desc, k_rank, out):
    ctx = ExitStack()
    with ctx:
        def sb(name, shape, dt=F32):
            return ctx.enter_context(nc.sbuf_tensor(name, shape, dt))

        def sem(name):
            return ctx.enter_context(nc.semaphore(name))

        with ExitStack() as between:
            x_split, w_split, d_split, h_split = (
                between.enter_context(nc.sbuf_tensor(name, shape, F32R))
                for name, shape in (("x_split", [P, 2, KC, T]), ("w_split", [P, 2, 2, 2, KC, P]), ("d_split", [P, 2, 2, D]),
                                    ("h_split", [P, 2, 2, T])))
        ht = sb("ht", [P, KC, KEYS])
        scratch = sb("scratch", [P, SCRATCH])
        ring = sb("ring", [P, RING, UNIT])
        x = sb("x", [P, TT, D])
        side = sb("side", [P, 2, TT * D])
        cx = side[:, 0, :].rearrange("p (t d) -> p t d", t=TT)
        xn = side[:, 1, :].rearrange("p (t d) -> p t d", t=TT)
        gate_b = sb("gate_b", [P, D])
        mats = sb("mats", [P, 3, P])
        desc = sb("desc", [P, PER_GROUP])
        cols = sb("cols", [P, 4, P])
        means = sb("means", [P, 2, P])
        tmp = sb("tmp", [P, 512])
        eps = sb("eps", [P, 1])
        overflow = sb("overflow", [P, 1], I32)
        ss = sb("ss", [P, TT])
        std = sb("std", [P, TT])
        rstd = sb("rstd", [P, TT])
        router_w = sb("router_w", [P, KC, GROUPS + EXPERTS])
        router_b = sb("router_b", [P, GROUPS + EXPERTS])
        comb = sb("comb", [P, TT, EXPERTS])
        mod = sb("mod", [P, 2, NMOD, 2, KC])
        mod_scale = sb("mod_scale", [P, 8, KC])
        silu_c = sb("silu_c", [P, KC, 32])
        small = sb("small", [P, 96])
        lbc = sb("lbc", [P, 2, CC])
        subln = sb("subln", [P, 1])
        zero = sb("zero", [P, 1])
        zero_r = sb("zero_r", [P, 1], F32R)
        masks = ht[:, :, T:T + P]
        rows = tmp[:].rearrange("p (a b) -> p a b", b=P)
        cos, sin = silu_c[:].rearrange("p a b -> p (a b)"), router_w[:].rearrange("p a b -> p (a b)")[:, 0:T]
        window, lam_in = tmp[:, 0:T], tmp[:, T:2 * T].rearrange("p (a b) -> p a b", a=4)

        lo = ctx.enter_context(nc.psum_tensor("lo", [P, 4, 512], F32))
        hi = ctx.enter_context(nc.psum_tensor("hi", [P, 4, 512], F32))

        ident, flip8, rot = mats[:, 0, :], mats[:, 1, :], mats[:, 2, :]

        def part(at, *shape):
            n = 1
            for s in shape:
                n *= s
            v = scratch[:, at:at + n]
            if len(shape) == 1:
                return v
            if len(shape) == 2:
                return v.rearrange("p (a b) -> p a b", a=shape[0])
            return v.rearrange("p (a b c) -> p a b c", a=shape[0], b=shape[1])

        def htpart(at, *shape):
            v = ht[:, :, :].rearrange("p a b -> p (a b)")
            n = 1
            for s in shape:
                n *= s
            v = v[:, at:at + n]
            return v if len(shape) == 1 else v.rearrange("p (a b) -> p a b", a=shape[0])

        unit_loaded = [sem(f"unit_loaded{s}") for s in range(RING)]
        unit_used = [sem(f"unit_used{s}") for s in range(RING)]
        x_loaded, mem_loaded, ctx_loaded = sem("x_loaded"), sem("mem_loaded"), sem("ctx_loaded")
        mats_loaded, rows_loaded, consts_loaded, bias_loaded = (sem(n + "_loaded") for n in ("mats", "rows", "consts", "bias"))
        gain_loaded, out_stored = sem("gain_loaded"), sem("out_stored")
        dve_chain, act_chain = sem("dve_chain"), sem("act_chain")
        set_up = sem("set_up")
        cols_turned, cols_ready = sem("cols_turned"), sem("cols_ready")
        col_math = sem("col_math")
        norm_sq, norm_std, norm_xn = sem("norm_sq"), sem("norm_std"), sem("norm_xn")
        norm_turned, norm_ready = sem("norm_turned"), sem("norm_ready")
        x_ready, ctx_ready = sem("x_ready"), sem("ctx_ready")
        gate_turned, gate_ready = sem("gate_turned"), sem("gate_ready")

        def unit_of(n):
            return ring[:, n % RING, :]

        def as_cols(n):
            return unit_of(n).rearrange("p (k n) -> p k n", k=KC)

        def as_rows(n):
            return unit_of(n).rearrange("p (k n) -> p k n", k=4)

        def wait_unit(pe, n, i=None):
            v = n // RING + 1
            pe.wait_ge(unit_loaded[n % RING], 32 * v if i is None else (i + v) * 32)

        def wait_used(eng, n, i=None):
            v = n // RING + 1
            eng.wait_ge(unit_used[n % RING], v if i is None else i + v)

        def up_unit(n, c, b):
            n += 6 * (c // 4) + (0, 2, 3, 5)[c % 4]
            return n, unit_of(n).rearrange("p (a k n) -> p a k n", a=2, k=KC)[:, :, :, b * P:b * P + P]

        def down_unit(n, c, b):
            n += 6 * (c // 4) + (1, 1, 4, 4)[c % 4]
            return n, as_rows(n)[:, 2 * (c % 2) + b, :]

        def step_of(n, b):
            return as_cols(n).rearrange("p k (s a n) -> p s a k n", s=2, a=2)[:, b]

        def rows_of(n, i):
            return as_cols(n)[:, 2 * i:2 * i + 2, :].rearrange("p k n -> p (k n)")

        def nth(f, c, b, it=None):
            v = 2 * NCHUNK * f + 2 * c + b + 1
            return v if it is None else it * 8 + v

        XA_COLS, XA_ROWS, XA_XS = 16, 16, 3
        CM_UP, CM_DOWN, CM_XS = XA_COLS + 4 * 2 * NCHUNK, XA_ROWS + 4 * 2 * NCHUNK, XA_XS + 4
        CM_UNITS, CM_ROWS = 6, 8

        def cols_of(p):
            n = U_XQ + p // 4
            return n, as_cols(n)[:, :, (p % 4) * P:(p % 4 + 1) * P]

        def xa_rows(k):
            n = U_XV + k // 4
            return n, rows_of(n, k % 4)

        def nth_up(f, c, b, it=None):
            return nth(f, c, b, it) + XA_COLS + (2 * CM_UNITS if f == 4 else 0)

        def nth_down(f, c, b, it=None):
            return nth(f, c, b, it) + XA_ROWS + (CM_ROWS if f == 4 else 0)

        def nth_xs(f):
            return f + XA_XS + (2 if f == 4 else 0)

        class Link:

            def __init__(self, eng, chain):
                self.eng, self.chain, self.n = eng, chain, 0

            def __call__(self, ins):
                self.n += 1
                ins.then_inc(self.chain, 1)
                self.eng.wait_ge(self.chain, self.n)

        block = ctx.enter_context(nc.Block())

        sg, upad, acc = part(0, CC, T), part(1024, CC, 286), part(2168, CC, T)
        qT, kT, cum = part(3192, CC, T), part(4216, CC, T), part(5240, CC, T)
        eb = [part(6264, CC, T), part(0, CC, T)]
        qk = [part(7288, CC, T), part(1024, CC, T)]
        grT = part(8312, CC, T)
        vtok = side[:, 1, 0:TT * CW].rearrange("p (t n) -> p t n", t=TT)
        gcT, grT2 = part(9336, KC, T), part(11384, KC, T)
        ST = ht[:, 0:CC, 0:T].rearrange("p h (t s) -> p h t s", t=TT)
        S01 = ht[:, CC:CC + 2, 0:T].rearrange("p a (b s) -> p a b s", b=2)
        oN = part(4216, CC, T)
        reset = gate_b[:]
        merged = side[:, 1, :].rearrange("p (c t) -> p c t", c=KC)
        LEVELS = 7
        xq, xk, xv = part(4096, KC, T), part(6144, KC, T), part(0, TT, D)
        xp, xpt, xo = part(2048, XH, TT, T), part(12 * D, 2, 2, T), part(4096, KC, T)
        ffn_sg, ffn_h = part(13 * D, 2, T), part(13 * D + 2 * T, 2, T)
        lg = part(4096, TT, GROUPS + EXPERTS)
        hg, onehot, weighted, back = part(0, KC, 2 * PLACES), part(1024, TT, 2, PLACES), part(1280, TT, 2, PLACES), part(1536, T)
        ex_sg, ex_h, ex_hT, ex_y = part(2048, FF), part(2560, FF), part(3072, 4, 2 * PLACES), part(5120, D)
        place, chosen, count = part(4608, TT, EXPERTS + 2), part(4736, TT, EXPERTS), part(4800, TT, EXPERTS)
        before_me, numbers = part(13440, P), part(13440 + P, PLACES)
        dn_w = part(0, 3, UNIT)
        dn_sg, dn_h = part(3 * UNIT, 4, T), part(3 * UNIT + 4 * T, 4, T)
        mrow = part(13440 + P + PLACES, 2, T)
        qe, qo, kaT, va = part(0, CC, T), part(1024, CC, T), part(2048, CC, KEYS), part(4096, 4, CW)
        qbe, qbo, kbT, vb = part(6144, CC, T), part(7168, CC, T), part(8192, CC, KEYS), part(10240, 4, CW)
        ap_, apt = part(12288, 4, KEYS), htpart(3072, 4, T)
        rawq, rawk = part(12288, CC, T), part(13312, CC, T)
        rtmp = htpart(2048, CC, T)
        dO, dsq = part(0, CC, T), part(1024, CC, T)
        bias = side[:, :, :].rearrange("p a (h n) -> p (a h) n", n=T)
        mergeT = htpart(0, KC, T)
        cgs, u2, vm = side[:, 0, :].rearrange("p (c t) -> p c t", c=KC), part(12 * D, KC, T), merged

        mix_u = sem("mix_u")
        mix_cg, mix_q, mix_f, mix_v, mix_g, mix_gate = (sem("mix_" + n) for n in ("cg", "q", "f", "v", "g", "gate"))
        mix_fk, mix_ln_f, mix_scan, conv_step = (sem(n) for n in ("mix_fk", "mix_ln_f", "mix_scan", "conv_step"))
        at_zero, rope_loaded = sem("at_zero"), sem("rope_loaded")
        lev_diff, lev_exp, lev_qk, lev_s, lev_kept = (sem("lev_" + n) for n in ("diff", "exp", "qk", "s", "kept"))
        cn_mean, cn_d, cn_sq, cn_var, cn_std, cn_y, cn_act = (sem("cn_" + n) for n in ("mean", "d", "sq", "var", "std", "y", "act"))
        ho_o, ho_sq, ho_ms, ho_std, ho_n = (sem("ho_" + n) for n in ("o", "sq", "ms", "std", "n"))
        mg_conv, mg_all = sem("mg_conv"), sem("mg_all")
        xa_q, xa_k, xa_v, xa_v1, xa_s, xa_nm, xa_e, xa_p, xa_t, xa_pt, xa_pv, xa_o = (
            sem("xa_" + n) for n in ("q", "k", "v", "v1", "s", "nm", "e", "p", "t", "pt", "pv", "o"))
        rt_logits, rt_d, rt_e = (sem("rt_" + n) for n in ("logits", "d", "e"))
        rt_comb, rt_rank, rt_flag = (sem("rt_" + n) for n in ("comb", "rank", "flag"))
        ex_onehot, ex_weighted, ex_gathered, ex_hg, ex_sgd, ex_hd, ex_turned, ex_hTd, ex_back_turned, ex_back, ex_yd, ex_done = (
            sem("ex_" + n) for n in ("onehot", "weighted", "gathered", "hg", "sg", "h", "turned", "hT", "back_turned", "back", "y", "done"))
        dn_loaded, dn_gu, dn_sgd, dn_hd, dn_down, dn_added = (sem("dn_" + n) for n in ("loaded", "gu", "sg", "h", "down", "added"))
        moe_done = sem("moe_done")
        md_copied, md_turned, md_cols, md_scales = (sem("md_" + n) for n in ("copied", "turned", "cols", "scales"))
        ffn_gu, ffn_sgd, ffn_h32, ffn_hd, ffn_dn = (sem("ffn_" + n) for n in ("gu", "sg", "h32", "h", "dn"))
        xs_hi, xs_lo, gs_hi, gs_lo, ds_hi, ds_lo = (sem(n) for n in ("xs_hi", "xs_lo", "gs_hi", "gs_lo", "ds_hi", "ds_lo"))
        at_qa, at_ka, at_va, at_qb, at_kb, at_vb, at_rot, at_rope = (
            sem("at_" + n) for n in ("qa", "ka", "va", "qb", "kb", "vb", "rot", "rope"))
        na_bias, na_s, na_nm, na_e, na_p, na_t, na_pt, na_pv, na_o = (
            sem("na_" + n) for n in ("bias", "s", "nm", "e", "p", "t", "pt", "pv", "o"))
        df_s, df_nm, df_e, df_p, df_t, df_pt, df_pv, df_o, df_sq, df_ms, df_std, df_n = (
            sem("df_" + n) for n in ("s", "nm", "e", "p", "t", "pt", "pv", "o", "sq", "ms", "std", "n"))
        lam_d, lam_e = sem("lam_d"), sem("lam_e")
        cm_cg, cm_u, cm_bg = sem("cm_cg"), sem("cm_u"), sem("cm_bg")
        gain_used = sem("gain_used")

        @block.sync
        def _(sp):
            sp.dma_start(x[:], x_in[0].rearrange("(t p) d -> p t d", p=P)).then_inc(x_loaded, 16)

            def load(n, halves, i=None):
                if i is not None:
                    sp.wait_ge(unit_used[n % RING], i + n // RING)
                elif n >= RING:
                    sp.wait_ge(unit_used[n % RING], n // RING)
                for dst, src in halves():
                    sp.dma_start(dst, src).then_inc(unit_loaded[n % RING], 16)

            def split(v, s, half):
                return (v[:, 0:half], s[:, 0:half]), (v[:, half:2 * half], s[:, half:2 * half])

            def cols_unit(n, w, at, i=None, step=0):
                def halves():
                    cut = slice(at, at + 512) if i is None else bass.ds(i * step + at, 512)
                    return split(as_cols(n), w[:, cut].rearrange("(k p) n -> p k n", p=P), 4)
                load(n, halves, i)

            def rows_unit(n, w):
                load(n, lambda: split(as_rows(n), w.rearrange("(k p) n -> p k n", p=P), 2))

            def mod_units(m):
                for j in range(2):
                    cols_unit(u_mod(m) + j, mod_w_2[m // NMOD], D * (m % NMOD) + 512 * j)

            for j in range(10):
                cols_unit(u_in(j), w_in[0], 512 * j)
                if j == 0:
                    sp.wait_ge(rows_loaded, 16 * 17)
                if j < NMOD:
                    mod_units(j)
            for m in range(NMOD, VECTORS):
                mod_units(m)
            rows_unit(U_CONV, conv_w_out[0])
            rows_unit(U_HGRN, hgrn_w_out[0])
            for u, w in ((U_MIX, w_mix_out), (U_XQ, xa_w_q), (U_XK, xa_w_k), (U_XV, xa_w_v), (U_XO, xa_w_o)):
                for j in range(2):
                    cols_unit(u + j, w[0], 512 * j)

            def expert_of(w, at):
                return w[0, at].rearrange("e (k p) n -> p (e k) n", p=P)

            with sp.Fori(0, EXPERTS // 2) as i:
                for j, w, view, half in ((0, moe_w_gate, as_cols, 4), (2, moe_w_up, as_cols, 4), (4, moe_w_down, as_rows, 2)):
                    for e in range(2):
                        n = U_MOE + j + e
                        load(n, lambda: split(view(n), expert_of(w, bass.ds(i * 2 + e, 1)), half), i)
            sp.wait_ge(rt_flag, 2)
            with sp.If(sp.value_load(overflow[0:1, 0:1], min_val=0, max_val=1)):
                with sp.Fori(0, EXPERTS) as e:
                    sp.wait_ge(dn_added, e + 1)
                    for j, w, k in ((0, moe_w_gate, KC), (1, moe_w_up, KC), (2, moe_w_down, 4)):
                        sp.dma_start(dn_w[:, j, :].rearrange("p (k n) -> p k n", k=k), expert_of(w, bass.ds(e, 1))).then_inc(dn_loaded, 16)

            def ffn_units(f, l, j):
                wg, wu, wd = ffn_w_gate_2[l, j], ffn_w_up_2[l, j], ffn_w_down_2[l, j]

                def gate_up(n, c, i=None):
                    def halves():
                        v = unit_of(n).rearrange("p (a k n) -> p a k n", a=2, k=KC)
                        cut = bass.ds(c * FCHUNK if i is None else i * (4 * FCHUNK) + c * FCHUNK, FCHUNK)
                        return tuple((v[:, a], w[:, cut].rearrange("(k p) n -> p k n", p=P)) for a, w in ((0, wg), (1, wu)))
                    load(n, halves, i)

                def down(n, c, chunks, i=None):
                    def halves():
                        size = chunks * FCHUNK
                        cut = bass.ds(c * FCHUNK if i is None else i * (4 * FCHUNK) + c * FCHUNK, size)
                        return split(as_rows(n), wd[cut, :].rearrange("(k p) n -> p k n", p=P), chunks)
                    load(n, halves, i)

                n = U_FFN[f]
                with sp.Fori(0, 2) as i:
                    for h in range(2):
                        gate_up(n + 3 * h, 2 * h, i)
                        down(n + 3 * h + 1, 2 * h, 2, i)
                        gate_up(n + 3 * h + 2, 2 * h + 1, i)
                gate_up(n + 12, 8)
                down(n + 13, 8, 2)
                gate_up(n + 14, 9)
                gate_up(n + 15, 10)
                down(n + 16, 10, 1)

            ffn_units(0, 0, 0)
            ffn_units(1, 0, 0)
            for j in range(6):
                cols_unit(U_ATT + j, attn_w_in_2[0], 512 * j)
            for j in range(2):
                cols_unit(U_ATTO + j, attn_w_out_2[0], 512 * j)
            ffn_units(2, 0, 1)
            ffn_units(3, 1, 0)
            for j, c in enumerate((2, 4, 3, 5, 0, 1)):
                cols_unit(U_CM + j, conv_w_in_2[0], 512 * c)
            for j in range(2):
                cols_unit(U_CMO + j, conv_w_out_2[0], 512 * j)
            ffn_units(4, 1, 1)
            for t in range(TT):
                sp.wait_ge(x_ready, TT * 10 + t + 1)
                sp.dma_start(out[0, t * P:t * P + P, :], xn[:, t, :]).then_inc(out_stored, 16)
            sp.wait_ge(out_stored, 16 * TT)

        @block.gpsimd
        def _(pool):
            for dst, src in ((masks, k_masks), (desc[:], k_desc), (scratch[:, 13440:13440 + P + PLACES], k_rank)):
                pool.dma_start(dst, src).then_inc(consts_loaded, 16)
            pool.dma_start(cx, mem[0].rearrange("(t p) d -> p t d", p=P)).then_inc(mem_loaded, 16)
            pool.dma_start(router_w[:, :, 0:GROUPS], router_group_w[0].rearrange("(k p) n -> p k n", p=P)).then_inc(consts_loaded, 16)
            pool.dma_start(router_w[:, :, GROUPS:], router_expert_w[0].rearrange("(k p) n -> p k n", p=P)).then_inc(consts_loaded, 16)
            pool.dma_start(router_b[:, 0:GROUPS], router_group_b[0].partition_broadcast(P)).then_inc(consts_loaded, 16)
            pool.dma_start(router_b[:, GROUPS:], router_expert_b[0].partition_broadcast(P)).then_inc(consts_loaded, 16)
            pool.wait_ge(mix_scan, 1)
            pool.dma_start(gate_b[:], final_norm_g.partition_broadcast(P)).then_inc(gain_loaded, 16)
            pool.wait_ge(norm_xn, 6)
            pool.dma_start(cx, ctx_2[0].rearrange("(t p) d -> p t d", p=P)).then_inc(ctx_loaded, 16)
            pool.wait_ge(x_ready, TT * 5)
            for dst, src in ((cos, k_rope[:, 0, :]), (sin, k_rope[:, 1, :]), (window, k_window), (lam_in, diff_lambda_2[0].partition_broadcast(P))):
                pool.dma_start(dst, src).then_inc(rope_loaded, 16)
            pool.wait_ge(norm_turned, 4 * 8)
            for t in range(TT):
                for r in range(2):
                    for a in range(T // GRID):
                        src = bass.AP(rpb_pad.tensor, (7 + a - 2 * t - r) * P, [[1, GRID], [15 * P, NAH], [1, GRID]])
                        pool.dma_start(bias[GRID * r:GRID * r + GRID, t::2, GRID * a:GRID * a + GRID], src).then_inc(bias_loaded, 16)
            pool.wait_ge(x_ready, TT * 10)
            pool.dma_start(gate_b[:], final_g_2.partition_broadcast(P)).then_inc(gain_loaded, 16)
        @block.scalar
        def _(act):
            link = Link(act, act_chain)

            def col(r, n=1, t=0):
                return cols[:, t, r:r + n]

            def norm_stats(r, src, turned=0, ready=None, squares=xn):
                link(act.activation(small[:, 82:83], eps[:], ACT.Sqrt))
                if turned:
                    act.wait_ge(norm_turned, turned)
                for t in range(TT):
                    if ready:
                        act.wait_ge(ready[0], TT * ready[1] - TT + t + 1)
                    act.activation(squares[:, t, :], src[:, t, :], ACT.Square, accum_out=ss[:, t:t + 1]).then_inc(norm_sq, 1)
                    act.wait_ge(norm_sq, TT * r + t + 1)
                    act.activation(std[:, t:t + 1], ss[:, t:t + 1], ACT.Sqrt, bias=eps[:], scale=1.0 / D).then_inc(norm_std, 1)

            def norm_out(i, off, scale, shift=None):
                for c in range(4, KC):
                    act.wait_ge(norm_turned, 4 * i + c // 2 + 1)
                    act.activation(ht[:, c, off:off + T] if off is not None else merged[:, c, :], hi[:, c // 2, (c % 2) * T:(c % 2 + 1) * T], ACT.Identity,
                                   scale=scale[:, c:c + 1], bias=shift[:, c:c + 1] if shift is not None else 0.0
                                   ).then_inc(norm_ready, 1)

            vec = [(R_MIX, norm_mix_g), (R_XA, norm_xa_g), (R_MEM, norm_mem_g), (R_FFN, norm_ffn_g), (R_CONVB, conv_b),
                   (R_LNG, conv_ln_g), (R_LNB, conv_ln_b), (R_LB, hgrn_lb_logits), (R_ONORM, hgrn_onorm_g),
                   (R_SUBLN, diff_subln_g_2), (R_C, c_2)]
            act.dma_start(mats[:], k_mats).then_inc(mats_loaded, 16)
            for at, v in vec:
                s = v.rearrange("a (c p) -> (a c) p", p=P)
                act.dma_start(rows[at:at + s.shape[0], 0, :], s).then_inc(rows_loaded, 16)
            act.dma_start(rows[R_NG2:R_C, 0, :], norm_g_2.rearrange("l j (c p) -> (l j c) p", p=P)).then_inc(rows_loaded, 16)
            act.dma_start(rows[R_CCTX:R_END, 0, :], c_ctx_2.rearrange("(c p) -> c p", p=P)).then_inc(rows_loaded, 16)
            act.dma_start(rows[0:R2_END, 1, :], conv_w[0].rearrange("j (c p) -> (j c) p", p=P)).then_inc(rows_loaded, 16)
            act.dma_start(rows[0:R3_CONV2, 2, :], mod_b_2[0].rearrange("(c p) -> c p", p=P)).then_inc(rows_loaded, 16)
            act.dma_start(rows[R3_CONV2:R3_END, 2, :], conv_w_2[0].rearrange("j (c p) -> (j c) p", p=P)).then_inc(rows_loaded, 16)
            act.dma_start(rows[0:R4_END, 3, :], mod_b_2[1].rearrange("(c p) -> c p", p=P)).then_inc(rows_loaded, 16)
            act.wait_ge(set_up, 5)
            act.wait_ge(x_loaded, 16)
            norm_stats(0, x, 0)
            act.wait_ge(cols_ready, 5)
            act.activation(silu_c[:, :, 0], col(R_C, KC), ACT.Silu).then_inc(col_math, 1)
            act.activation(silu_c[:, :, 1], col(R_CCTX, KC), ACT.Silu).then_inc(col_math, 1)
            act.activation(lbc[:, 0, :], small[:, 0:CC], ACT.Sigmoid).then_inc(col_math, 1)

            norm_out(0, 0, col(R_MIX, KC))

            def mod_copied(m):
                wait_used(act, u_mod(m) + 1)
                act.activation(mrow[:, m % 2, :], hi[:, m % 4, 0:T], ACT.Copy).then_inc(md_copied, 1)

            def mod_cols(m):
                act.wait_ge(md_turned, m + 1)
                ps = hi[:, m % 4, T:2 * T].rearrange("p (b g w) -> p w g b", b=2, w=32)[:, 0:2]
                act.activation(mod[:, m // NMOD, m % NMOD].rearrange("p v (g b) -> p v g b", b=2), ps, ACT.Copy).then_inc(md_cols, 1)

            for j in range(10):
                if j in (1, 2, 3, 5):
                    src, dst, fun, done = {1: (lo[:, 2:4, :], sg, ACT.Sigmoid, mix_cg), 2: (lo[:, 0:2, :], qT, ACT.Silu, mix_q),
                                           3: (lo[:, 2:4, :], cum, ACT.Sigmoid, mix_f), 5: (lo[:, 2:4, :], grT, ACT.Silu, mix_g)}[j]
                    wait_used(act, u_in(j))
                    act.activation(dst, src, fun).then_inc(done, 1)
                elif j == 4:
                    act.wait_ge(mix_fk, 1)
                    act.activation(eb[0], qk[0], ACT.Ln).then_inc(mix_ln_f, 1)
                elif j >= 6:
                    wait_used(act, u_in(j))
                    dst = (gcT if j < 8 else grT2)[:, 4 * (j % 2):4 * (j % 2) + 4, :]
                    act.activation(dst, lo[:, 2 * (j % 2):2 * (j % 2) + 2, :], ACT.Sigmoid).then_inc(mix_gate, 1)
                if j < NMOD:
                    mod_copied(j)
                if j:
                    mod_cols(j - 1)
            for v in range(1, LEVELS + 4):
                if v <= LEVELS + 1:
                    act.wait_ge(lev_diff, v)
                    act.activation(eb[v % 2], eb[v % 2], ACT.Exp).then_inc(lev_exp, 1)
                if 2 <= v:
                    mod_copied(NMOD - 2 + v)
                if v >= 3:
                    mod_cols(NMOD - 3 + v)
            mod_cols(VECTORS - 1)
            act.wait_ge(cn_d, 1)
            act.activation(eb[0], acc, ACT.Square).then_inc(cn_sq, 1)
            act.wait_ge(cn_var, 1)
            act.activation(eb[1][:, 0, :], hi[:, 1, 0:T], ACT.Sqrt, bias=eps[:], scale=1.0).then_inc(cn_std, 1)
            act.wait_ge(cn_y, 1)
            for c in range(CC):
                act.activation(acc[:, c, :], acc[:, c, :], ACT.Silu, scale=col(R_LNG + c), bias=col(R_LNB + c)).then_inc(cn_act, 1)
            act.wait_ge(ho_o, 1)
            act.activation(eb[0], hi[:, 2:4, :], ACT.Square).then_inc(ho_sq, 1)
            act.wait_ge(ho_ms, 1)
            link(act.activation(eb[0], hi[:, 0:2, :], ACT.Ln, bias=eps[:], scale=1.0))
            act.activation(eb[0], eb[0], ACT.Exp, scale=-0.5).then_inc(ho_std, 1)

            def round_up(n, w, dst, step, it=None):
                wait_unit(act, n, it)
                if it is not None or step > 2:
                    act.wait_ge(ffn_gu, step - 2)
                act.activation(dst, w, ACT.Copy).then_inc(gs_hi, 1)

            def round_down(n, w, b, step, it=None):
                wait_unit(act, n, it)
                if it is not None or step > 2:
                    act.wait_ge(ffn_dn, step - 2)
                act.activation(d_split[:, b, 0], w, ACT.Copy).then_inc(ds_hi, 1)

            def round_x(rows, ready=None):
                for h in range(2):
                    if ready:
                        act.wait_ge(ready, 2 * h + 2)
                    act.activation(x_split[:, 0, 4 * h:4 * h + 4], rows[:, 4 * h:4 * h + 4], ACT.Copy).then_inc(xs_hi, 1)

            def xa_piece(p):
                round_up(*cols_of(p), w_split[:, 0, 0, p % 2], p + 1)

            def xa_step(k):
                round_down(*xa_rows(k), k % 2, k + 1)

            norm_stats(1, x, 4, (x_ready, 1))
            xa_piece(0)
            xa_piece(1)
            norm_out(1, None, col(R_XA, KC))
            act.wait_ge(norm_ready, KC * 2)
            round_x(merged)
            act.wait_ge(mem_loaded, 16)
            norm_stats(2, cx, squares=part(8192, TT, D))
            for p in range(2, 6):
                xa_piece(p)
            act.activation(xq[:, 0:4, :], lo[:, 0:2, :], ACT.Copy).then_inc(xa_q, 1)
            norm_out(2, None, col(R_MEM, KC))
            for p in range(6, 10):
                xa_piece(p)
            act.wait_ge(norm_ready, KC * 3)
            round_x(merged)
            act.activation(xq[:, 4:8, :], lo[:, 2:4, :], ACT.Copy).then_inc(xa_q, 1)
            for p in range(10, XA_COLS):
                xa_piece(p)
            for k in range(6):
                xa_step(k)
            act.activation(xv[:, :, 0:512], lo[:, 0:2, :], ACT.Copy).then_inc(xa_v, 1)
            for k in range(6, 10):
                xa_step(k)
            for h in range(XH):
                act.wait_ge(xa_nm, h + 1)
                for t in range(TT):
                    act.activation(xp[:, h, t, :], hi[:, h, t * T:t * T + T], ACT.Exp, scale=XD ** -0.5,
                                   bias=small[:, 16 + 2 * h + t:17 + 2 * h + t],
                                   accum_out=small[:, 24 + 2 * h + t:25 + 2 * h + t]).then_inc(xa_e, 1)
            for h in range(XH):
                act.wait_ge(xa_t, h + 1)
                act.activation(xpt[:, h % 2], lo[:, h % 2, :], ACT.Copy).then_inc(xa_pt, 1)

            round_x(xo, xa_o)
            for k in range(10, XA_ROWS):
                xa_step(k)

            norm_stats(3, x, 12, (x_ready, 2))
            norm_out(3, 0, col(R_FFN, KC))
            act.wait_ge(rt_d, 1)
            act.activation(part(4200, TT, GROUPS), part(4192, TT, GROUPS), ACT.Exp).then_inc(rt_e, 1)
            act.wait_ge(rt_d, 2)
            act.activation(small[:, 34:36], small[:, 32:34], ACT.Exp).then_inc(rt_e, 1)
            act.wait_ge(ctx_loaded, 16)
            norm_stats(4, cx, squares=part(8192, TT, D))
            for h in range(2):
                act.activation(ex_y[:, h * 512:h * 512 + 512], zero[:].broadcast_to([P, 512]), ACT.Copy).then_inc(ex_yd, 1)
            act.activation(back, zero[:].broadcast_to([P, T]), ACT.Copy).then_inc(ex_back, 1)
            with act.Fori(0, EXPERTS // 2) as i:
                for e in range(2):
                    wait_used(act, U_MOE + e, i)
                act.activation(ex_sg, lo[:, 0, :], ACT.Silu).then_inc(ex_sgd, 1)
                act.wait_ge(ex_turned, i + 1)
                act.activation(ex_hT, lo[:, 0, :], ACT.Copy).then_inc(ex_hTd, 1)
                act.wait_ge(ex_back_turned, i + 2)
                act.activation(back, lo[:, 1, 0:T], ACT.Copy).then_inc(ex_back, 1)
                for e in range(2):
                    wait_used(act, U_MOE + 4 + e, i)
                for h in range(2):
                    act.activation(ex_y[:, h * 512:h * 512 + 512], lo[:, 2 + h, :], ACT.Copy).then_inc(ex_yd, 1)
            act.wait_ge(rt_flag, 2)
            with act.If(act.value_load(overflow[0:1, 0:1], min_val=0, max_val=1)):
                with act.Fori(0, EXPERTS) as e:
                    for f in range(4):
                        act.wait_ge(dn_gu, e * 4 + (f + 1))
                        act.activation(dn_sg[:, f, :], lo[:, f, 0:T], ACT.Silu).then_inc(dn_sgd, 1)

            def split_up(f, c, b, it=None):
                n, w = up_unit(U_FFN[f], c, b)
                round_up(n, w, w_split[:, b, 0], nth_up(f, c, b, it), it)

            def split_down(f, c, b, it=None):
                n, w = down_unit(U_FFN[f], c, b)
                round_down(n, w, b, nth_down(f, c, b, it), it)

            def cm_up(j, b):
                round_up(U_CM + j, step_of(U_CM + j, b), w_split[:, b, 0], CM_UP + 2 * j + b + 1)

            def cm_down(k):
                n = U_CMO + k // 4
                round_down(n, rows_of(n, k % 4), k % 2, CM_DOWN + k + 1)

            def ffn(f, i, r, src, ready, at, scale, shift, half_gate):
                if f == 0:
                    act.wait_ge(x_ready, TT * 3)
                else:
                    norm_stats(r, src, 4 * i, ready)
                if f in (0, 2):
                    split_up(f, 0, 0)
                    split_up(f, 0, 1)
                norm_out(i, None, scale, shift)
                act.wait_ge(norm_ready, KC * (i + 1))
                round_x(merged)
                if f in (0, 2):
                    split_down(f, 0, 0)
                    split_down(f, 0, 1)
                if f == 0:
                    act.wait_ge(xs_lo, 2 * nth_xs(0) + 2)
                    norm_stats(5, x)
                gate(half_gate, 0.5)

                def chunk(c, it=None):
                    nf, nc_ = (f, c + 1) if c + 1 < NCHUNK else (f + 1, 0)
                    more = nc_ or nf in (1, 3)
                    for b in range(2):
                        act.wait_ge(ffn_gu, nth_up(f, c, b, it))
                        act.activation(ffn_sg[:, b, :], lo[:, b, 0:T], ACT.Silu).then_inc(ffn_sgd, 1)
                        if more:
                            split_up(nf, nc_, b, it)
                        elif f == 3:
                            cm_up(0, b)
                    for b in range(2):
                        if more:
                            split_down(nf, nc_, b, it)

                with act.Fori(0, 2) as it:
                    for c in range(4):
                        chunk(c, it)
                for c in range(8, NCHUNK):
                    chunk(c)

            def gate(g, scale):
                act.wait_ge(gate_turned, g + 1)
                act.wait_ge(gain_used, g + 1)
                act.activation(gate_b[:], lo[:, 2:4, :], ACT.Copy, scale=scale).then_inc(gate_ready, 1)

            act.wait_ge(md_scales, 1)
            ffn(0, 4, 4, cx, None, 0, mod_scale[:, 0], mod[:, 0, 0, 1], 0)
            ffn(1, 5, 6, x, (x_ready, 4), 1, mod_scale[:, 1], mod[:, 0, 0, 0], 1)

            norm_stats(7, x, 24, (x_ready, 5))
            norm_out(6, 0, mod_scale[:, 2], mod[:, 0, 3, 0])
            norm_stats(8, cx, 28, (ctx_ready, 1))
            norm_out(7, T, mod_scale[:, 3], mod[:, 0, 3, 1])
            wait_used(act, U_ATT)
            act.activation(qe[0:HD], lo[0:HD, 0:2, :], ACT.Copy).then_inc(at_qa, 1)
            act.activation(qo[HD:P], lo[HD:P, 0:2, :], ACT.Copy).then_inc(at_qa, 1)
            wait_used(act, U_ATT + 1)
            act.activation(kaT, hi[:, :, :], ACT.Copy).then_inc(at_ka, 1)
            wait_used(act, U_ATT + 3)
            act.activation(rawq, hi[:, 0:2, :], ACT.Copy).then_inc(at_qb, 1)
            wait_used(act, U_ATT + 4)
            act.activation(rawk, lo[:, :, 0:T], ACT.Copy).then_inc(at_kb, 1)
            act.activation(kbT[:, :, T:KEYS], lo[:, :, T:KEYS], ACT.Copy).then_inc(at_kb, 1)
            wait_used(act, U_ATT + 5)
            act.activation(vb, hi[:, :, :], ACT.Copy).then_inc(at_vb, 1)
            gate(2, 1.0)
            act.wait_ge(lam_d, 1)
            act.activation(small[:, 42:44], small[:, 40:42], ACT.Exp).then_inc(lam_e, 1)
            act.wait_ge(at_rope, 3)

            def na_exp(h):
                b = 2 * (h % 2)
                act.wait_ge(na_nm, h + 1)
                for t in range(TT):
                    act.activation(ap_[:, b + t, :], hi[:, b + t, :], ACT.Exp, scale=HD ** -0.5,
                                   bias=small[:, 48 + b + t:49 + b + t],
                                   accum_out=small[:, 52 + b + t:53 + b + t]).then_inc(na_e, 1)

            def na_copy(h):
                act.wait_ge(na_t, h + 1)
                act.activation(apt, lo[:, 0:2, :], ACT.Copy).then_inc(na_pt, 1)

            na_exp(0)
            na_exp(1)
            for h in range(NAH):
                na_copy(h)
                if h + 2 < NAH:
                    na_exp(h + 2)
            for h in range(DH):
                act.wait_ge(df_nm, h + 1)
                for m in range(4):
                    act.activation(ap_[:, m, :], hi[:, m, :], ACT.Exp, scale=HD ** -0.5, bias=small[:, 48 + m:49 + m],
                                   accum_out=small[:, 52 + m:53 + m]).then_inc(df_e, 1)
                act.wait_ge(df_t, h + 1)
                act.activation(apt, lo[:, 0:2, :], ACT.Copy).then_inc(df_pt, 1)
            act.wait_ge(df_o, DH)
            act.activation(dsq, dO, ACT.Square).then_inc(df_sq, 1)
            act.wait_ge(df_ms, 1)
            link(act.activation(dsq, hi[:, 0:2, :], ACT.Ln, bias=eps[:], scale=1.0))
            act.activation(dsq, dsq, ACT.Exp, scale=-0.5).then_inc(df_std, 1)

            ffn(2, 8, 9, x, (x_ready, 6), 2, mod_scale[:, 4], mod[:, 0, 6, 0], 3)
            ffn(3, 9, 10, x, (x_ready, 7), 3, mod_scale[:, 5], mod[:, 1, 0, 0], 4)

            norm_stats(11, x, 40, (x_ready, 8))
            norm_out(10, None, mod_scale[:, 6], mod[:, 1, 3, 0])
            act.wait_ge(norm_ready, KC * 11)
            round_x(merged)
            for j in range(CM_UNITS):
                for b in range(2):
                    if j + 1 < CM_UNITS:
                        cm_up(j + 1, b)
                    else:
                        cm_down(b)
                if j in (0, 2):
                    act.wait_ge(ffn_gu, CM_UP + 2 * (j + 1))
                    act.activation(cgs[:, 2 * j:2 * j + 4, :], (hi if j else lo)[:, 0:2, :], ACT.Copy).then_inc(cm_cg, 1)
            act.wait_ge(cm_bg, 2)
            round_x(vm)
            for b in range(2):
                split_up(4, 0, b)
            gate(5, 1.0)
            for k in range(2, CM_ROWS):
                cm_down(k)
            for b in range(2):
                split_down(4, 0, b)
            ffn(4, 11, 12, x, (x_ready, 9), 4, mod_scale[:, 7], mod[:, 1, 6, 0], 6)

            norm_stats(13, x, 48, (x_ready, 10))

        @block.tensor
        def _(pe):
            def mm(dst, lhsT, rhs, start=True, stop=True, **kw):
                return pe.matmul(dst, lhsT, rhs, start=start, stop=stop, **kw)

            def to_features(n, dst, rhs, chunks, last=True):
                for f in range(4):
                    for k in range(chunks):
                        ins = mm(dst(f), as_cols(n)[:, k, f * P:f * P + P], rhs(k), k == 0, k == chunks - 1)
                ins.then_inc(unit_used[n % RING], 1)

            def to_rows(n, dst, lhsT, tiles=TT):
                for t in range(tiles):
                    for k in range(KC):
                        ins = mm(dst(t), lhsT(k, t), as_cols(n)[:, k, :], k == 0, k == KC - 1)
                ins.then_inc(unit_used[n % RING], 1)

            def pair(ps, b):
                return lambda f: ps[:, b + f // 2, (f % 2) * T:(f % 2 + 1) * T]

            def norm(i):
                for t in range(TT):
                    pe.wait_ge(norm_xn, TT * i + t + 1)
                    for c in range(KC):
                        ins = pe.transpose(hi[:, c // 2, (c % 2) * T + t * P:(c % 2) * T + t * P + P], xn[:, t, c * P:c * P + P], ident)
                        if t == TT - 1 and c % 2:
                            ins.then_inc(norm_turned, 1)

            def normed(i):
                pe.wait_ge(norm_ready, KC * (i + 1))

            def ht_all(k):
                return ht[:, k, 0:T]

            def ht_tile(k, t):
                return ht[:, k, t * P:t * P + P]

            pe.wait_ge(mats_loaded, 16)
            pe.wait_ge(rows_loaded, 16 * 17)
            for t, n in enumerate((R_END, R2_END, R3_END, R4_END)):
                ins = pe.transpose(lo[:, 0, t * P:t * P + n], rows[0:n, t, :], ident[0:n, 0:n])
            ins.then_inc(cols_turned, 1)
            norm(0)
            normed(0)
            pe.wait_ge(cols_ready, 4)

            before = [None, None, (mix_u, 1), (mix_cg, 1), (mix_q, 1), (mix_f, 1), (mix_v, 1), (mix_g, 1), (mix_gate, 1), (mix_gate, 2)]
            def mod_product(m):
                if m >= 4:
                    pe.wait_ge(md_cols, m - 3)
                for j in range(2):
                    n = u_mod(m) + j
                    wait_unit(pe, n)
                    for k in range(KC):
                        for h in range(2):
                            g = 2 * j + h
                            ins = mm(hi[32 * g:32 * g + 32, m % 4, 0:T], silu_c[:, k, :], as_cols(n)[:, k, h * T:h * T + T],
                                     k == 0, k == KC - 1, tile_position=(0, 32 * g))
                    ins.then_inc(unit_used[n % RING], 1)

            def mod_turn(m):
                pe.wait_ge(md_copied, m + 1)
                for h in range(2):
                    ins = pe.transpose(hi[:, m % 4, T + h * P:T + h * P + P], mrow[:, m % 2, h * P:h * P + P], ident)
                ins.then_inc(md_turned, 1)

            pe.wait_ge(col_math, 2)
            for j in range(10):
                n = u_in(j)
                wait_unit(pe, n)
                if before[j]:
                    pe.wait_ge(*before[j])
                if j == 4:
                    to_rows(n, lambda t: lo[:, t, :], ht_tile)
                else:
                    to_features(n, pair(lo, 2 * (j % 2)), ht_all, KC)
                if j < NMOD:
                    mod_product(j)
                if j:
                    mod_turn(j - 1)

            def blocks(b):
                return lambda h, t: lo[:, b + h // 2, (h % 2) * T + t * P:(h % 2) * T + t * P + P]

            pe.wait_ge(consts_loaded, 16 * 7)
            pe.wait_ge(mix_fk, 1)
            pe.wait_ge(mix_gate, 3)
            for h in range(CC):
                for t in range(TT):
                    ins = mm(blocks(0)(h, t), kT[:, h, t * P:t * P + P], qT[:, h, t * P:t * P + P])
            ins.then_inc(lev_s, 1)
            mod_product(NMOD)
            for v in range(1, LEVELS + 1):
                pe.wait_ge(lev_qk, v)
                if v == 1:
                    pe.wait_ge(mix_gate, 4)
                else:
                    pe.wait_ge(lev_kept, v - 1)
                for h in range(CC):
                    for t in range(TT):
                        z = qk[v % 2][:, h, t * P:t * P + P]
                        ins = mm(blocks(2 * (v % 2))(h, t), z, z)
                ins.then_inc(lev_s, 1)
                mod_product(NMOD + v)
                mod_turn(NMOD + v - 1)
            pe.wait_ge(lev_qk, LEVELS + 1)
            pe.wait_ge(lev_kept, LEVELS)
            for h in range(CC):
                ins = mm(lo[:, 0, h * P:h * P + P], qk[0][:, h, 0:P], qk[0][:, h, P:T])
            ins.then_inc(lev_s, 1)
            mod_product(VECTORS - 1)
            for m in (VECTORS - 2, VECTORS - 1):
                mod_turn(m)
            for c in range(CC):
                if c == 0:
                    pe.wait_ge(conv_step, TAPS * CC)
                    pe.wait_ge(md_cols, VECTORS)
                ins = mm(hi[:, 0, 0:T], means[:, 0, :], acc[:, c, :], c == 0, c == CC - 1)
            ins.then_inc(cn_mean, 1)
            pe.wait_ge(cn_sq, 1)
            for c in range(CC):
                ins = mm(hi[:, 1, 0:T], means[:, 0, :], eb[0][:, c, :], c == 0, c == CC - 1)
            ins.then_inc(cn_var, 1)
            pe.wait_ge(lev_kept, LEVELS + 2)
            pe.wait_ge(mix_v, 1)
            for h in range(CC):
                o = hi[:, 2 + h // 2, (h % 2) * T:(h % 2 + 1) * T]
                v0, v1 = vtok[:, 0, h * P:h * P + P], vtok[:, 1, h * P:h * P + P]
                mm(o[:, 0:P], v0, ST[:, h, 0, :])
                mm(o[:, P:T], v0, S01[:, h // 2, h % 2, :], True, False)
                ins = mm(o[:, P:T], v1, ST[:, h, 1, :], False, True)
            ins.then_inc(ho_o, 1)
            wait_unit(pe, U_CONV)
            pe.wait_ge(cn_act, CC)

            def wide(n, dst, rhs):
                for f in range(KC):
                    for k in range(CC):
                        ins = mm(dst[:, f // 2, (f % 2) * T:(f % 2 + 1) * T], as_rows(n)[:, k, f * P:f * P + P], rhs[:, k, :], k == 0, k == CC - 1)
                ins.then_inc(unit_used[n % RING], 1)

            wide(U_CONV, lo, acc)
            pe.wait_ge(ho_sq, 1)
            pe.wait_ge(cn_std, 1)
            for b in range(2):
                ins = mm(hi[:, b, :], means[:, 1, :], eb[0][:, 2 * b:2 * b + 2, :])
            ins.then_inc(ho_ms, 1)
            wait_unit(pe, U_HGRN)
            pe.wait_ge(ho_n, 1)
            wide(U_HGRN, hi, oN)
            pe.wait_ge(mg_all, 1)
            for j in range(2):
                wait_unit(pe, U_MIX + j)
                to_rows(U_MIX + j, lambda t: hi[:, 2 * t + j, :], lambda k, t: merged[:, k, t * P:t * P + P])

            halves = ((0, 0), (1, 0), (0, 1))

            def xa_piece(p, dst):
                pe.wait_ge(gs_lo, p + 1)
                for k in range(KC):
                    for xh, wh in halves:
                        ins = mm(dst, w_split[:, 0, wh, p % 2, k, :], x_split[:, xh, k, :], k == 0 and not xh + wh, k == KC - 1 and wh == 1)
                        if p % 4 == 3 and k + xh + wh == 0:
                            ins.then_inc(unit_used[cols_of(p)[0] % RING], 1)
                ins.then_inc(ffn_gu, 1)

            def down_step(step, total, j, i, n, buf):
                pe.wait_ge(ds_lo, total)
                for k in range(2):
                    for t in range(TT):
                        for xh, wh in halves:
                            ins = mm(buf(t, j), x_split[:, xh, 2 * i + k, t * P:t * P + P], d_split[:, step % 2, wh, k * 512:k * 512 + 512],
                                     i + k + xh + wh == 0, i == 3 and k == 1 and wh == 1, skip_group_check=True)
                            if i == 3 and k + t + xh + wh == 0:
                                ins.then_inc(unit_used[n % RING], 1)
                ins.then_inc(ffn_dn, 1)

            norm(1)
            pe.wait_ge(xs_lo, 2)
            pe.wait_ge(mg_conv, 1)
            for p in range(4):
                xa_piece(p, pair(lo, 0)(p))
            norm(2)
            for p in range(4, 8):
                xa_piece(p, pair(lo, 2)(p % 4))
            pe.wait_ge(xs_lo, 4)
            for p in range(8, XA_COLS):
                xa_piece(p, pair(hi, 2 * (p // 4 % 2))(p % 4))
            for k in range(8):
                if k % 4 == 0:
                    pe.wait_ge(xa_q, k // 4 + 1)
                down_step(k, k + 1, k // 4, k % 4, xa_rows(k)[0], lambda t, j: lo[:, 2 * j + t, :])
            pe.wait_ge(xa_k, 2)
            for h in range(XH):
                for t in range(TT):
                    for d in range(2):
                        ins = mm(hi[:, h, t * T:t * T + T], xq[:, 2 * h + d, t * P:t * P + P], xk[:, 2 * h + d, :], d == 0, d == 1)
                ins.then_inc(xa_s, 1)

            def xa_turn(h):
                pe.wait_ge(xa_p, TT * (h + 1))
                for t in range(TT):
                    for m in range(2):
                        ins = pe.transpose(lo[:, h % 2, m * T + t * P:m * T + t * P + P], xp[:, h, t, m * P:m * P + P], ident)
                ins.then_inc(xa_t, 1)

            def xa_value(h):
                pe.wait_ge(xa_pt, h + 1)
                if h >= 2:
                    pe.wait_ge(xa_o, h - 1)
                for d in range(2):
                    for m in range(2):
                        c = h * XD + d * P
                        ins = mm(lo[:, 2 + h % 2, d * T:d * T + T], xv[:, m, c:c + P], xpt[:, h % 2, m, :], m == 0, m == 1)
                ins.then_inc(xa_pv, 1)

            pe.wait_ge(xa_v, 1)
            pe.wait_ge(xa_v1, 1)
            xa_turn(0)
            for h in range(XH):
                if h + 1 < XH:
                    xa_turn(h + 1)
                xa_value(h)
            pe.wait_ge(xa_o, XH)
            for k in range(8, XA_ROWS):
                if k == 8:
                    pe.wait_ge(xs_lo, 6)
                down_step(k, k + 1, k // 4 % 2, k % 4, xa_rows(k)[0], lambda t, j: hi[:, 2 * t + j, :])

            norm(3)
            normed(3)
            for t in range(TT):
                for k in range(KC):
                    ins = mm(lo[:, 0, t * 64:t * 64 + GROUPS + EXPERTS], ht_tile(k, t), router_w[:, k, :], k == 0, k == KC - 1)
            ins.then_inc(rt_logits, 1)
            pe.wait_ge(rt_comb, 1)
            ranks, counts = lo[:, 1, 0:TT * EXPERTS].rearrange("p (t n) -> p t n", t=TT), lo[:, 1, TT * EXPERTS:(TT + 1) * EXPERTS]
            mm(ranks[:, 0, :], before_me, chosen[:, 0, :])
            mm(ranks[:, 1, :], before_me, chosen[:, 1, :], True, False)
            mm(ranks[:, 1, :], means[:, 0, :], chosen[:, 0, :], False, True)
            for t in range(TT):
                ins = mm(counts, means[:, 0, :], chosen[:, t, :], t == 0, t == 1)
            ins.then_inc(rt_rank, 1)
            for t in range(TT):
                for h in range(2):
                    ins = mm(hi[:, 2 * t + h, :], zero[:].broadcast_to([P, P]), x[:, 0, 0:512], True, False, skip_group_check=True)
            ins.then_inc(ex_back_turned, 1)

            def gather():
                for c in range(KC):
                    for t in range(TT):
                        ins = mm(lo[:, 2 + c // 4, (c % 4) * P:(c % 4 + 1) * P], xn[:, t, c * P:c * P + P], onehot[:, t], t == 0, t == 1)
                    if c % 4 == 3:
                        ins.then_inc(ex_gathered, 1)

            def scatter(last):
                for t in range(TT):
                    for h in range(2):
                        ins = mm(hi[:, 2 * t + h, :], back[:, t * P:t * P + P], ex_y[:, h * 512:h * 512 + 512], False, last, skip_group_check=True)
                return ins

            pe.wait_ge(ex_onehot, 1)
            gather()
            with pe.Fori(0, EXPERTS // 2) as i:
                def places(e, n, bank, lhsT, k, rhs, chunks):
                    ins = mm(lo[PLACES * e:PLACES * e + PLACES, bank, :], lhsT[:, k, PLACES * e:PLACES * e + PLACES], rhs,
                             k == 0, k == chunks - 1, tile_position=(0, PLACES * e))
                    return ins

                pe.wait_ge(ex_hg, i * 2 + 2)
                for bank in range(2):
                    n = U_MOE + 2 * bank
                    if bank == 1:
                        pe.wait_ge(ex_back, i + 1)
                    for e in range(2):
                        wait_unit(pe, n + e, i)
                    for k in range(KC):
                        for e in range(2):
                            ins = places(e, n + e, bank, hg, k, as_cols(n + e)[:, k, :], KC)
                            if k == KC - 1:
                                ins.then_inc(unit_used[(n + e) % RING], 1)
                pe.wait_ge(ex_yd, i * 2 + 2)
                scatter(False)
                pe.wait_ge(ex_onehot, i + 2)
                gather()
                pe.wait_ge(ex_hd, i + 1)
                for f in range(4):
                    ins = pe.transpose(lo[:, 0, f * P:f * P + P], ex_h[:, f * P:f * P + P], ident)
                ins.then_inc(ex_turned, 1)
                pe.wait_ge(ex_weighted, i + 1)
                for t in range(TT):
                    ins = pe.transpose(lo[:, 1, t * P:t * P + P], weighted[:, t].rearrange("p e s -> p (e s)"), ident)
                ins.then_inc(ex_back_turned, 1)
                pe.wait_ge(ex_hTd, i + 1)
                pe.wait_ge(ex_hg, i * 2 + 4)
                n = U_MOE + 4
                for e in range(2):
                    wait_unit(pe, n + e, i)
                for h in range(2):
                    for k in range(4):
                        for e in range(2):
                            ins = places(e, n + e, 2 + h, ex_hT, k, as_rows(n + e)[:, k, h * 512:h * 512 + 512], 4)
                            if h == 1 and k == 3:
                                ins.then_inc(unit_used[(n + e) % RING], 1)
            pe.wait_ge(ex_yd, EXPERTS + 2)
            pe.wait_ge(ex_back, EXPERTS // 2 + 1)
            scatter(True).then_inc(ex_done, 1)
            pe.wait_ge(rt_flag, 2)
            with pe.If(pe.value_load(overflow[0:1, 0:1], min_val=0, max_val=1)):
                with pe.Fori(0, EXPERTS) as e:
                    pe.wait_ge(dn_loaded, e * 48 + 48)
                    for f in range(4):
                        for j in range(2):
                            w = dn_w[:, j, :].rearrange("p (k n) -> p k n", k=KC)
                            for k in range(KC):
                                ins = mm(lo[:, f, j * T:j * T + T], w[:, k, f * P:f * P + P], ht_all(k), k == 0, k == KC - 1)
                        ins.then_inc(dn_gu, 1)
                    w = dn_w[:, 2, :].rearrange("p (k n) -> p k n", k=4)
                    for f in range(4):
                        pe.wait_ge(dn_hd, e * 4 + (f + 1))
                        for t in range(TT):
                            for h in range(2):
                                ins = mm(hi[:, 2 * t + h, :], dn_h[:, f, t * P:t * P + P], w[:, f, h * 512:h * 512 + 512], f == 0, f == 3)
                    ins.then_inc(dn_down, 1)

            pe.wait_ge(x_ready, TT * 3)
            pe.wait_ge(md_scales, 1)

            def gate(l, i, v):
                for c in range(KC):
                    ins = mm(lo[:, 2 + c // 4, (c % 4) * P:(c % 4 + 1) * P], mod[:, l, i, v, c:c + 1].broadcast_to([P, P]), ident)
                ins.then_inc(gate_turned, 1)

            def ffn(f, i, l, m, v):
                norm(i)
                gate(l, m, v)
                pe.wait_ge(xs_lo, 2 * nth_xs(f) + 1)
                for t in range(TT):
                    for h in range(2):
                        mm(hi[:, 2 * t + h, :], zero_r[:].broadcast_to([P, P]), x_split[:, 0, 0:2, :], True, False, skip_group_check=True)
                def chunk(c, it=None):
                    n, last = U_FFN[f], c == NCHUNK - 1
                    for b in range(2):
                        pe.wait_ge(gs_lo, nth_up(f, c, b, it))
                        for a in range(2):
                            for k in range(KC):
                                if c + b + a == 0 and k == KC // 2:
                                    pe.wait_ge(xs_lo, 2 * nth_xs(f) + 2)
                                for xh, wh in halves:
                                    ins = mm(lo[:, b, a * T:a * T + T], w_split[:, b, wh, a, k, :], x_split[:, xh, k, :],
                                             k == 0 and not xh + wh, k == KC - 1 and wh == 1)
                                    if b == 1 and a + k + xh + wh == 0:
                                        ins.then_inc(unit_used[up_unit(n, c, b)[0] % RING], 1)
                        ins.then_inc(ffn_gu, 1)
                    for b in range(2):
                        pe.wait_ge(ds_lo, nth_down(f, c, b, it))
                        pe.wait_ge(ffn_hd, nth(f, c, b, it))
                        for h in range(2):
                            for t in range(TT):
                                for xh, wh in halves:
                                    ins = mm(hi[:, 2 * t + h, :], h_split[:, b, xh, t * P:t * P + P], d_split[:, b, wh, h * 512:h * 512 + 512],
                                             False, last and b == 1 and wh == 1, skip_group_check=True)
                                    if b == 1 and h + t + xh + wh == 0 and (c % 2 or last):
                                        ins.then_inc(unit_used[down_unit(n, c, b)[0] % RING], 1)
                        ins.then_inc(ffn_dn, 1)

                with pe.Fori(0, 2) as it:
                    for c in range(4):
                        chunk(c, it)
                for c in range(8, NCHUNK):
                    chunk(c)

            ffn(0, 4, 0, 2, 1)
            ffn(1, 5, 0, 2, 0)

            norm(6)
            normed(6)
            norm(7)
            wait_unit(pe, U_ATT)
            to_features(U_ATT, pair(lo, 0), ht_all, KC)
            normed(7)
            both = lambda k: ht[:, k, :]
            keys = lambda k, t: ht[:, k, t * P:t * P + P]
            wait_unit(pe, U_ATT + 1)
            to_features(U_ATT + 1, lambda f: hi[:, f, :], both, KC)
            wait_unit(pe, U_ATT + 2)
            pe.wait_ge(at_qa, 2)
            to_rows(U_ATT + 2, lambda t: lo[:, t, :], keys, 4)
            wait_unit(pe, U_ATT + 3)
            pe.wait_ge(at_ka, 1)
            to_features(U_ATT + 3, pair(hi, 0), ht_all, KC)
            wait_unit(pe, U_ATT + 4)
            pe.wait_ge(at_va, 1)
            to_features(U_ATT + 4, lambda f: lo[:, f, :], both, KC)
            wait_unit(pe, U_ATT + 5)
            pe.wait_ge(at_qb, 1)
            to_rows(U_ATT + 5, lambda t: hi[:, t, :], keys, 4)
            pe.wait_ge(at_kb, 2)
            for b in range(2):
                ins = mm(lo[:, b, :], rot, rawq[:, 2 * b:2 * b + 2, :])
            ins.then_inc(at_rot, 1)
            for b in range(2):
                ins = mm(lo[:, 2 + b, :], rot, rawk[:, 2 * b:2 * b + 2, :])
            ins.then_inc(at_rot, 1)
            pe.wait_ge(at_rope, 3)
            gate(0, 5, 0)

            pe.wait_ge(at_zero, 4)
            pe.wait_ge(na_bias, 1)
            pe.wait_ge(at_vb, 1)

            def na_score(h):
                if h >= 2:
                    pe.wait_ge(na_e, TT * (h - 1))
                b = 2 * (h % 2)
                for t in range(TT):
                    mm(hi[:, b + t, :], (qo if h % 2 else qe)[:, h // 2, t * P:t * P + P], kaT[:, h // 2, :], True, False)
                    ins = mm(hi[:, b + t, 0:T], flip8, bias[:, 2 * h + t, :], False, True)
                ins.then_inc(na_s, 1)

            def turn(h, rows_of, ready, done):
                pe.wait_ge(*ready)
                for t in range(TT):
                    for c in range(4):
                        at = c * T + t * P
                        ins = pe.transpose(lo[:, at // 512, at % 512:at % 512 + P], rows_of(t)[:, c * P:c * P + P], ident)
                ins.then_inc(done, 1)

            def df_score(h):
                pe.wait_ge(na_e, TT * NAH)
                if h:
                    pe.wait_ge(df_e, 4 * h)
                for m in range(2):
                    for t in range(TT):
                        ins = mm(hi[:, 2 * m + t, :], (qbo if m else qbe)[:, h, t * P:t * P + P], kbT[:, h, :])
                ins.then_inc(df_s, 1)

            na_score(0)
            na_score(1)
            for h in range(NAH):
                turn(h, lambda t: ap_[:, 2 * (h % 2) + t, :], (na_p, TT * (h + 1)), na_t)
                if h + 2 < NAH:
                    na_score(h + 2)
                elif h == NAH - 1:
                    df_score(0)
                pe.wait_ge(na_pt, h + 1)
                if h == 0:
                    pe.wait_ge(gate_ready, 3)
                if h >= 4 and h % 2 == 0:
                    pe.wait_ge(na_o, h // 2 - 1)
                at = HD * (h % 2)
                for c in range(4):
                    ins = mm(lo[at:at + HD, 2 + (h // 2) % 2, 0:T], va[:, c, h * HD:h * HD + HD], apt[:, c, :], c == 0, c == 3,
                             tile_position=(0, at))
                ins.then_inc(na_pv, 1)

            for h in range(DH):
                if h + 1 < DH:
                    df_score(h + 1)
                turn(h, lambda t: ap_[:, t, :], (df_p, TT * (h + 1)), df_t)
                pe.wait_ge(df_pt, h + 1)
                pe.wait_ge(na_o, 4)
                if h >= 2:
                    pe.wait_ge(df_o, h - 1)
                for c in range(4):
                    ins = mm(lo[:, 2 + h % 2, 0:T], vb[:, c, h * P:h * P + P], apt[:, c, :], c == 0, c == 3)
                ins.then_inc(df_pv, 1)
            pe.wait_ge(df_sq, 1)
            for b in range(2):
                ins = mm(hi[:, b, :], means[:, 1, :], dsq[:, 2 * b:2 * b + 2, :])
            ins.then_inc(df_ms, 1)
            pe.wait_ge(df_n, 1)
            for j in range(2):
                wait_unit(pe, U_ATTO + j)
                to_rows(U_ATTO + j, lambda t: hi[:, 2 * t + j, :], lambda k, t: mergeT[:, k, t * P:t * P + P])

            ffn(2, 8, 0, 8, 0)
            ffn(3, 9, 1, 2, 0)

            norm(10)
            for j, ps in enumerate((lo[:, 0:2], lo[:, 2:4], hi[:, 0:2], hi[:, 2:4], lo[:, 0:2], lo[:, 2:4])):
                if j == 0:
                    pe.wait_ge(xs_lo, 2 * CM_XS + 2)
                if j >= 4:
                    pe.wait_ge(cm_u, 1)
                for b in range(2):
                    pe.wait_ge(gs_lo, CM_UP + 2 * j + b + 1)
                    for a in range(2):
                        for k in range(KC):
                            for xh, wh in halves:
                                ins = mm(pair(ps, 0)(2 * b + a), w_split[:, b, wh, a, k, :], x_split[:, xh, k, :],
                                         k == 0 and not xh + wh, k == KC - 1 and wh == 1)
                                if b == 1 and a + k + xh + wh == 0:
                                    ins.then_inc(unit_used[(U_CM + j) % RING], 1)
                    ins.then_inc(ffn_gu, 1)
            pe.wait_ge(cm_bg, 2)
            gate(1, 5, 0)
            pe.wait_ge(xs_lo, 2 * CM_XS + 4)
            for step in range(CM_ROWS):
                j = step // 4
                down_step(step, CM_DOWN + step + 1, j, step % 4, U_CMO + j, lambda t, j: hi[:, 2 * t + j, :])
            ffn(4, 11, 1, 8, 0)

        @block.vector
        def _(dve):
            link = Link(dve, dve_chain)
            tt, ts, stt = dve.tensor_tensor, dve.tensor_scalar, dve.scalar_tensor_tensor

            def col(r, n=1, t=0):
                return cols[:, t, r:r + n]

            def rstd_of(r, t):
                dve.wait_ge(norm_std, TT * r + t + 1)
                link(dve.reciprocal(rstd[:, t:t + 1], std[:, t:t + 1]))

            def norm_rows(r, src):
                for t in range(TT):
                    rstd_of(r, t)
                    ts(xn[:, t, :], src[:, t, :], rstd[:, t:t + 1], None, ALU.mult).then_inc(norm_xn, 1)

            def norm(i, r, src, off, scale, shift=None, meanwhile=None):
                if i != 4:
                    norm_rows(r, src)
                if meanwhile:
                    meanwhile()
                for c in range(4):
                    dve.wait_ge(norm_turned, 4 * i + c // 2 + 1)
                    ps = hi[:, c // 2, (c % 2) * T:(c % 2 + 1) * T]
                    dst = ht[:, c, off:off + T] if off is not None else merged[:, c, :]
                    if shift is None:
                        ins = ts(dst, ps, scale[:, c:c + 1], None, ALU.mult)
                    else:
                        ins = ts(dst, ps, scale[:, c:c + 1], shift[:, c:c + 1], ALU.mult, ALU.add)
                    ins.then_inc(norm_ready, 1)

            gates_used = [0]

            def gate_used(ins):
                gates_used[0] += 1
                ins.then_inc(gain_used, 1)
                dve.wait_ge(gain_used, gates_used[0])

            def residual(n, dst, signal, gated=False):
                for k in n:
                    wait_used(dve, k)
                for t in range(TT):
                    ps = hi[:, 2 * t:2 * t + 2, :].rearrange("p a n -> p (a n)")
                    if gated:
                        (gate_used if t == TT - 1 else link)(tt(ps, ps, gate_b[:], ALU.mult))
                    tt(dst[:, t, :], ps, dst[:, t, :], ALU.add).then_inc(signal, 1)


            dve.memset(eps[:], EPS).then_inc(set_up, 1)
            dve.memset(means[:, 0, :], 1.0 / CW).then_inc(set_up, 1)
            dve.memset(means[:, 1, :], 1.0 / P).then_inc(set_up, 1)
            dve.memset(silu_c[:], 0.0).then_inc(set_up, 1)
            dve.memset(upad[:, :, 0:TAPS - 1], 0.0).then_inc(set_up, 1)
            link(dve.memset(reset, 1.0))
            link(dve.memset(gate_b[:, 0::CHUNK], 0.0))
            link(dve.memset(zero[:], 0.0))
            link(dve.tensor_copy(zero_r[:], zero[:]))

            dve.wait_ge(cols_turned, 1)
            for t, n in enumerate((R_END, R2_END, R3_END, R4_END)):
                dve.tensor_copy(cols[:, t, 0:n], lo[:, 0, t * P:t * P + n]).then_inc(cols_ready, 1)
            dve.wait_ge(cols_ready, 4)
            tt(small[:, 0:CC], col(R_LB, CC), col(R_LB + CC, CC), ALU.subtract).then_inc(cols_ready, 1)
            link(ts(subln[:], col(R_SUBLN), 1.0 - LAM_INIT, None, ALU.mult))
            norm(0, 0, x, 0, col(R_MIX, KC))
            dve.wait_ge(col_math, 3)
            link(ts(lbc[:, 1, :], lbc[:, 0, :], -1.0, 1.0, ALU.mult, ALU.add))

            dve.wait_ge(mix_cg, 1)
            wait_used(dve, u_in(0))
            tt(upad[:, :, TAPS - 1:TAPS - 1 + T], lo[:, 0:2, :].rearrange("p a (b t) -> p (a b) t", b=2), sg, ALU.mult).then_inc(mix_u, 1)
            dve.wait_ge(mix_f, 1)
            for c in range(CC):
                link(ts(qk[0][:, c, :], cum[:, c, :], lbc[:, 1, c:c + 1], lbc[:, 0, c:c + 1], ALU.mult, ALU.add))
            ts(kT, qk[0], -1.0, 1.0, ALU.mult, ALU.add).then_inc(mix_fk, 1)
            wait_used(dve, u_in(4))
            dve.tensor_copy(vtok, lo[:, 0:2, :]).then_inc(mix_v, 1)
            dve.wait_ge(mix_ln_f, 1)
            dve.wait_ge(mix_fk, 1)
            dve.tensor_tensor_scan(cum.rearrange("p a b -> p (a b)"), reset, eb[0].rearrange("p a b -> p (a b)"), 0.0, ALU.mult, ALU.add
                                   ).then_inc(mix_scan, 1)
            dve.wait_ge(mix_u, 1)
            for c in range(CC):
                ts(acc[:, c, :], upad[:, c, 0:T], col(R2_TAPS + c, 1, 1), col(R_CONVB + c), ALU.mult, ALU.add).then_inc(conv_step, 1)
            with dve.Fori(1, TAPS) as j:
                for c in range(CC):
                    dve.wait_ge(conv_step, j * CC + (c + 1 - CC))
                    stt(acc[:, c, :], upad[:, c, bass.ds(j, T)], cols[:, 1, bass.ds(j * CC + c, 1)], acc[:, c, :], ALU.mult, ALU.add
                        ).then_inc(conv_step, 1)
            dve.wait_ge(mix_scan, 1)
            wait_used(dve, u_in(9))
            link(dve.memset(ST, 0.0))

            def halves(a, v):
                return a.rearrange("p h t -> p (h t)").rearrange("p (n a l) -> p n a l", a=2, l=1 << (v - 1))

            def diff(v):
                e = eb[v % 2]
                if v <= LEVELS:
                    c, o, half = halves(cum, v), halves(e, v), 1 << (v - 1)
                    edge = c[:, :, 0, half - 1:half].broadcast_to([P, CC * T // (2 * half), half])
                    link(tt(o[:, :, 0, :], edge, c[:, :, 0, :], ALU.subtract))
                    if v < LEVELS:
                        ins = tt(o[:, :, 1, :], c[:, :, 1, :], edge, ALU.subtract)
                    else:
                        ins = dve.tensor_copy(o[:, :, 1, :], c[:, :, 1, :])
                else:
                    def chunk(a, k):
                        return a[:, :, CHUNK * k:CHUNK * k + CHUNK]

                    def last(k):
                        return cum[:, :, CHUNK * k + CHUNK - 1:CHUNK * k + CHUNK]

                    both = small[:, 60:64].unsqueeze(2)
                    link(tt(both, last(0), last(1), ALU.add))
                    link(tt(chunk(e, 0), both.broadcast_to([P, CC, CHUNK]), chunk(cum, 0), ALU.subtract))
                    link(tt(chunk(e, 1), last(1).broadcast_to([P, CC, CHUNK]), chunk(cum, 1), ALU.subtract))
                    link(dve.tensor_copy(chunk(e, 2), chunk(cum, 2)))
                    ins = tt(chunk(e, 3), chunk(cum, 3), last(2).broadcast_to([P, CC, CHUNK]), ALU.add)
                ins.then_inc(lev_diff, 1)
                dve.wait_ge(lev_diff, v)

            def keep(v):
                dve.wait_ge(lev_s, v + 1)
                ps = lo[:, 2 * (v % 2):2 * (v % 2) + 2, :].rearrange("p a (b t s) -> p (a b) t s", b=2, t=TT)
                dve.copy_predicated(ST, masks[:, v, :].bitcast(U32).unsqueeze(1).unsqueeze(1).broadcast_to([P, CC, TT, P]), ps).then_inc(lev_kept, 1)
                dve.wait_ge(lev_kept, v + 1)

            diff(1)
            keep(0)
            for v in range(1, LEVELS + 2):
                if v <= LEVELS:
                    if v >= 2:
                        dve.wait_ge(lev_qk, v - 1)
                    diff(v + 1)
                dve.wait_ge(lev_exp, v)
                z, e = qk[v % 2], eb[v % 2]
                if v >= 3:
                    dve.wait_ge(lev_s, v - 1)
                if v <= LEVELS:
                    z4, e4, q4, k4 = (halves(a, v) for a in (z, e, qT, kT))
                    link(tt(z4[:, :, 0, :], k4[:, :, 0, :], e4[:, :, 0, :], ALU.mult))
                    tt(z4[:, :, 1, :], q4[:, :, 1, :], e4[:, :, 1, :], ALU.mult).then_inc(lev_qk, 1)
                    keep(v)
                else:
                    link(tt(z[:, :, 0:P], kT[:, :, 0:P], e[:, :, 0:P], ALU.mult))
                    tt(z[:, :, P:T], qT[:, :, P:T], e[:, :, P:T], ALU.mult).then_inc(lev_qk, 1)
            dve.wait_ge(lev_s, LEVELS + 2)
            dve.tensor_copy(S01, lo[:, 0, :].rearrange("p (a b s) -> p a b s", a=2, b=2)).then_inc(lev_kept, 1)
            dve.wait_ge(cn_mean, 1)
            tt(acc, acc, hi[:, 0, 0:T].unsqueeze(1).broadcast_to([P, CC, T]), ALU.subtract).then_inc(cn_d, 1)
            dve.wait_ge(cn_std, 1)
            link(dve.reciprocal(eb[1][:, 1, :], eb[1][:, 0, :]))
            dve.wait_ge(cn_sq, 1)
            tt(acc, acc, eb[1][:, 1, :].unsqueeze(1).broadcast_to([P, CC, T]), ALU.mult).then_inc(cn_y, 1)
            dve.wait_ge(ho_std, 1)
            link(tt(oN, hi[:, 2:4, :].rearrange("p a (b t) -> p (a b) t", b=2), eb[0], ALU.mult))
            dve.wait_ge(mix_g, 1)
            stt(oN, oN, col(R_ONORM), grT, ALU.mult, ALU.mult).then_inc(ho_n, 1)
            wait_used(dve, U_CONV)
            dve.wait_ge(mix_gate, 4)
            tt(merged, gcT, lo[:, :, :].rearrange("p a (b t) -> p (a b) t", b=2), ALU.mult).then_inc(mg_conv, 1)
            wait_used(dve, U_HGRN)
            link(tt(grT2, grT2, hi[:, :, :].rearrange("p a (b t) -> p (a b) t", b=2), ALU.mult))
            dve.wait_ge(mg_conv, 1)
            tt(merged, merged, grT2, ALU.add).then_inc(mg_all, 1)
            residual((U_MIX, U_MIX + 1), x, x_ready)

            def rest_up(w, dst, hi_half, step):
                dve.wait_ge(gs_hi, step)
                tt(dst, w, hi_half.bitcast(F32), ALU.subtract).then_inc(gs_lo, 1)

            def rest_down(w, b, step):
                dve.wait_ge(ds_hi, step)
                tt(d_split[:, b, 1], w, d_split[:, b, 0].bitcast(F32), ALU.subtract).then_inc(ds_lo, 1)

            def rest_x(rows, use):
                for h in range(2):
                    dve.wait_ge(xs_hi, 2 * use + h + 1)
                    half = slice(4 * h, 4 * h + 4)
                    tt(x_split[:, 1, half], rows[:, half], x_split[:, 0, half].bitcast(F32), ALU.subtract).then_inc(xs_lo, 1)

            def xa_piece(p):
                rest_up(cols_of(p)[1], w_split[:, 0, 1, p % 2], w_split[:, 0, 0, p % 2], p + 1)

            def xa_step(k):
                rest_down(xa_rows(k)[1], k % 2, k + 1)

            def first_pieces():
                xa_piece(0)
                xa_piece(1)

            def more_pieces():
                for p in range(2, 6):
                    xa_piece(p)

            norm(1, 1, x, None, col(R_XA, KC), meanwhile=first_pieces)
            rest_x(merged, 0)
            norm(2, 2, cx, None, col(R_MEM, KC), meanwhile=more_pieces)
            for p in range(6, 10):
                xa_piece(p)
            rest_x(merged, 1)
            for p in range(10, 14):
                xa_piece(p)

            def xa_keys(j):
                dve.wait_ge(ffn_gu, 12 + 4 * j)
                dve.tensor_copy(xk[:, 4 * j:4 * j + 4, :], hi[:, 2 * j:2 * j + 2, :].rearrange("p a (b t) -> p (a b) t", b=2)).then_inc(xa_k, 1)

            xa_keys(0)
            xa_piece(14)
            xa_piece(15)
            xa_step(0)
            xa_step(1)
            xa_keys(1)
            for k in range(2, 8):
                xa_step(k)
            dve.wait_ge(md_cols, VECTORS)
            for l in range(2):
                for v in range(2):
                    m = mod[:, l, :, v, :]
                    ins = tt(m, m, cols[:, 2 + l, 0:NMOD * KC].rearrange("p (m c) -> p m c", c=KC), ALU.add)
                    link(ins)
            uses = [(0, 0, 1, 1), (0, 0, 1, 0), (0, 1, 4, 0), (0, 1, 4, 1), (0, 2, 7, 0), (1, 0, 1, 0), (1, 1, 4, 0), (1, 2, 7, 0)]
            for k, (l, j, m, v) in enumerate(uses):
                ins = stt(mod_scale[:, k, :], mod[:, l, m, v, :], 1.0, col(R_NG2 + (3 * l + j) * KC, KC), ALU.add, ALU.mult)
            ins.then_inc(md_scales, 1)
            dve.wait_ge(ffn_dn, 8)
            dve.tensor_copy(xv[:, :, 512:1024], lo[:, 2:4, :]).then_inc(xa_v1, 1)
            xa_step(8)
            xa_step(9)
            for h in range(XH):
                dve.wait_ge(xa_s, h + 1)
                mx, nm = small[:, 8 + 2 * h:10 + 2 * h], small[:, 16 + 2 * h:18 + 2 * h]
                link(dve.tensor_reduce(mx, hi[:, h, :].rearrange("p (t m) -> p t m", t=TT), AX.X, ALU.max))
                ts(nm, mx, -XD ** -0.5, None, ALU.mult).then_inc(xa_nm, 1)

            def xa_out(h):
                dve.wait_ge(xa_pv, h + 1)
                dve.tensor_copy(xo[:, 2 * h:2 * h + 2, :], lo[:, 2 + h % 2, :].rearrange("p (d t) -> p d t", d=2)).then_inc(xa_o, 1)

            for h in range(XH):
                dve.wait_ge(xa_e, TT * (h + 1))
                r = small[:, 8 + 2 * h:10 + 2 * h]
                link(dve.reciprocal(r, small[:, 24 + 2 * h:26 + 2 * h]))
                for t in range(TT):
                    ts(xp[:, h, t, :], xp[:, h, t, :], r[:, t:t + 1], None, ALU.mult).then_inc(xa_p, 1)
                if h:
                    xa_out(h - 1)
            xa_out(XH - 1)
            rest_x(xo, 2)
            for k in range(10, XA_ROWS):
                xa_step(k)
            dve.wait_ge(ffn_dn, XA_ROWS)
            residual((), x, x_ready)

            norm(3, 3, x, 0, col(R_FFN, KC))
            dve.wait_ge(rt_logits, 1)
            lgs = lo[:, 0, 0:128].rearrange("p (t n) -> p t n", t=TT)[:, :, 0:GROUPS + EXPERTS]
            link(tt(lg, lgs, router_b[:].unsqueeze(1).broadcast_to([P, TT, GROUPS + EXPERTS]), ALU.add))
            groups, experts = lg[:, :, 0:GROUPS], lg[:, :, GROUPS:].rearrange("p t (g j) -> p t g j", g=GROUPS)
            gmax, gsum, gp = small[:, 64:66].unsqueeze(2), small[:, 66:68].unsqueeze(2), small[:, 68:70].unsqueeze(2)
            m1, m2 = small[:, 70:72].unsqueeze(2), small[:, 72:74].unsqueeze(2)
            pick = small[:, 74:76].unsqueeze(2)
            ghot, shifted, gexp = part(4184, TT, GROUPS), part(4192, TT, GROUPS), part(4200, TT, GROUPS)
            inside, hot1, hot2, rest = (part(4208 + 16 * k, TT, PER_GROUP) for k in range(4))
            both, prod = part(4272, TT, PER_GROUP), part(4288, TT, PER_GROUP * GROUPS)

            def first_best(dst, v, best, n):
                link(tt(dst, v, best.broadcast_to([P, TT, n]), ALU.is_equal))
                link(tt(dst, dst, desc[:, PER_GROUP - n:].unsqueeze(1).broadcast_to([P, TT, n]), ALU.mult))
                link(dve.tensor_reduce(pick, dst, AX.X, ALU.max))
                link(tt(dst, dst, pick.broadcast_to([P, TT, n]), ALU.is_equal))

            link(dve.tensor_reduce(gmax, groups, AX.X, ALU.max))
            tt(shifted, groups, gmax.broadcast_to([P, TT, GROUPS]), ALU.subtract).then_inc(rt_d, 1)
            first_best(ghot, groups, gmax, GROUPS)
            prod4 = prod.rearrange("p t (g j) -> p t g j", g=GROUPS)
            for t in range(TT):
                link(tt(prod4[:, t], experts[:, t], ghot[:, t].unsqueeze(2).broadcast_to([P, GROUPS, PER_GROUP]), ALU.mult))
                link(dve.tensor_reduce(inside[:, t], prod4[:, t].rearrange("p g j -> p j g"), AX.X, ALU.add))
            link(dve.tensor_reduce(m1, inside, AX.X, ALU.max))
            first_best(hot1, inside, m1, PER_GROUP)
            link(stt(rest, hot1, -3.0e38, inside, ALU.mult, ALU.add))
            link(dve.tensor_reduce(m2, rest, AX.X, ALU.max))
            first_best(hot2, rest, m2, PER_GROUP)
            tt(small[:, 32:34].unsqueeze(2), m2, m1, ALU.subtract).then_inc(rt_d, 1)
            dve.wait_ge(rt_e, 1)
            link(dve.tensor_reduce(gsum, gexp, AX.X, ALU.add))
            link(dve.reciprocal(gp, gsum))
            dve.wait_ge(rt_e, 2)
            link(ts(small[:, 36:38], small[:, 34:36], 1.0, None, ALU.add))
            link(dve.reciprocal(small[:, 38:40], small[:, 36:38]))
            w1, w2 = small[:, 38:40].unsqueeze(2), small[:, 34:36].unsqueeze(2)
            link(tt(w1, w1, gp, ALU.mult))
            link(tt(w2, w2, w1, ALU.mult))
            link(tt(hot1, hot1, w1.broadcast_to([P, TT, PER_GROUP]), ALU.mult))
            link(tt(hot2, hot2, w2.broadcast_to([P, TT, PER_GROUP]), ALU.mult))
            link(tt(both, hot1, hot2, ALU.add))
            comb4 = comb[:, :, :].rearrange("p t (g j) -> p t g j", g=GROUPS)
            for t in range(TT):
                ins = tt(comb4[:, t], ghot[:, t].unsqueeze(2).broadcast_to([P, GROUPS, PER_GROUP]),
                         both[:, t].unsqueeze(1).broadcast_to([P, GROUPS, PER_GROUP]), ALU.mult)
                if t == 0:
                    link(ins)
            link(ins)
            ts(chosen, comb[:, :, :], 0.0, float(CW), ALU.is_gt, ALU.mult).then_inc(rt_comb, 1)
            link(dve.memset(place, -1.0))
            dve.wait_ge(rt_rank, 1)
            ranks = lo[:, 1, 0:TT * EXPERTS].rearrange("p (t n) -> p t n", t=TT)
            link(stt(count, ranks, 1.0, chosen, ALU.add, ALU.mult))
            link(ts(place[:, :, 0:EXPERTS], count, 1.0 / CW, -1.0, ALU.mult, ALU.add))
            link(dve.tensor_reduce(small[:, 80:81], lo[:, 1, TT * EXPERTS:(TT + 1) * EXPERTS], AX.X, ALU.max))
            ts(small[:, 81:82], small[:, 80:81], float(PLACES), None, ALU.is_gt).then_inc(rt_flag, 1)
            dve.wait_ge(rt_flag, 1)
            dve.tensor_copy(overflow[:], small[:, 81:82]).then_inc(rt_flag, 1)
            numbers4 = numbers.unsqueeze(1).unsqueeze(1).broadcast_to([P, TT, 2, PLACES])

            def one_hots(at):
                tt(onehot, numbers4, place[:, :, at].unsqueeze(3).broadcast_to([P, TT, 2, PLACES]), ALU.is_equal).then_inc(ex_onehot, 1)

            def gathered(i=None):
                for j in range(2):
                    dve.wait_ge(ex_gathered, j + 1 if i is None else i * 2 + (j + 3))
                    tt(hg[:, 4 * j:4 * j + 4, :], lo[:, 2 + j, :].rearrange("p (c s) -> p c s", c=4),
                       col(R_FFN + 4 * j, 4).unsqueeze(2).broadcast_to([P, 4, 2 * PLACES]), ALU.mult).then_inc(ex_hg, 1)

            one_hots(slice(0, 2))
            gathered()
            with dve.Fori(0, EXPERTS // 2) as i:
                dve.wait_ge(ex_onehot, i + 1)
                dve.wait_ge(ex_back_turned, i + 1)
                tt(weighted, onehot, comb[:, :, bass.ds(i * 2, 2)].unsqueeze(3).broadcast_to([P, TT, 2, PLACES]), ALU.mult).then_inc(ex_weighted, 1)
                dve.wait_ge(ex_weighted, i + 1)
                one_hots(bass.ds(i * 2 + 2, 2))
                for e in range(2):
                    wait_used(dve, U_MOE + 2 + e, i)
                dve.wait_ge(ex_sgd, i + 1)
                tt(ex_h, ex_sg, lo[:, 1, :], ALU.mult).then_inc(ex_hd, 1)
                gathered(i)
            norm_rows(4, cx)
            dve.wait_ge(ex_done, 1)
            x2 = x[:, :, :].rearrange("p t (h n) -> p (t h) n", h=2)
            tt(x2, x2, hi[:, :, :], ALU.add).then_inc(moe_done, 1)
            dve.wait_ge(moe_done, 1)
            with dve.If(dve.value_load(overflow[0:1, 0:1], min_val=0, max_val=1)):
                ts(chosen, place[:, :, 0:EXPERTS], float(PLACES), None, ALU.is_ge).then_inc(rt_flag, 1)
                dve.wait_ge(rt_flag, 3)
                tt(comb[:, :, :], comb[:, :, :], chosen, ALU.mult).then_inc(dn_added, 1)
                with dve.Fori(0, EXPERTS) as e:
                    for f in range(4):
                        dve.wait_ge(dn_sgd, e * 4 + (f + 1))
                        tt(dn_h[:, f, :], dn_sg[:, f, :], lo[:, f, T:2 * T], ALU.mult).then_inc(dn_hd, 1)
                    dve.wait_ge(dn_down, e + 1)
                    dve.wait_ge(dn_added, e + 1)
                    for t in range(TT):
                        for h in range(2):
                            xs = x[:, t, h * 512:h * 512 + 512]
                            ins = stt(xs, hi[:, 2 * t + h, :], comb[:, t, bass.ds(e, 1)], xs, ALU.mult, ALU.add)
                    ins.then_inc(dn_added, 1)
                dve.wait_ge(dn_added, EXPERTS + 1)
            tt(tmp[:, 0:1], eps[:], eps[:], ALU.add).then_inc(x_ready, TT)

            def split_up(f, c, b, it=None):
                rest_up(up_unit(U_FFN[f], c, b)[1], w_split[:, b, 1], w_split[:, b, 0], nth_up(f, c, b, it))

            def split_down(f, c, b, it=None):
                rest_down(down_unit(U_FFN[f], c, b)[1], b, nth_down(f, c, b, it))

            def cm_up(j, b):
                rest_up(step_of(U_CM + j, b), w_split[:, b, 1], w_split[:, b, 0], CM_UP + 2 * j + b + 1)

            def cm_down(k):
                rest_down(rows_of(U_CMO + k // 4, k % 4), k % 2, CM_DOWN + k + 1)

            def ffn(f, i, src, scale, shift, signal):
                norm(i, i + 1 if i > 4 else 4, src, None, scale, shift, lambda: f in (0, 2, 4) and split_up(f, 0, 0))
                rest_x(merged, nth_xs(f))
                if f in (0, 2, 4):
                    split_up(f, 0, 1)
                    split_down(f, 0, 0)
                    split_down(f, 0, 1)
                if f == 0:
                    dve.wait_ge(gain_loaded, 16)
                    dve.wait_ge(norm_std, TT * 6)
                    link(dve.reciprocal(rstd[:], std[:]))
                    for t in range(TT):
                        ins = stt(x[:, t, :], x[:, t, :], rstd[:, t:t + 1], gate_b[:], ALU.mult, ALU.mult)
                    gate_used(ins)
                    tt(tmp[:, 0:1], eps[:], eps[:], ALU.add).then_inc(x_ready, TT)

                def chunk(c, it=None):
                    nf, nc_ = (f, c + 1) if c + 1 < NCHUNK else (f + 1, 0)
                    more = nc_ or nf in (1, 3)
                    for b in range(2):
                        h32 = ffn_h[:, b, :]
                        dve.wait_ge(ffn_sgd, nth(f, c, b, it))
                        tt(h32, ffn_sg[:, b, :], lo[:, b, T:2 * T], ALU.mult).then_inc(ffn_h32, 1)
                        dve.wait_ge(ffn_h32, nth(f, c, b, it) * 2 - 1)
                        dve.tensor_copy(h_split[:, b, 0], h32).then_inc(ffn_h32, 1)
                        dve.wait_ge(ffn_h32, nth(f, c, b, it) * 2)
                        tt(h_split[:, b, 1], h32, h_split[:, b, 0].bitcast(F32), ALU.subtract).then_inc(ffn_hd, 1)
                        if more:
                            split_up(nf, nc_, b, it)
                        elif f == 3:
                            cm_up(0, b)
                    if more and nc_:
                        for b in range(2):
                            split_down(nf, nc_, b, it)

                with dve.Fori(0, 2) as it:
                    for c in range(4):
                        chunk(c, it)
                for c in range(8, NCHUNK):
                    chunk(c)
                g = (0, 1, 3, 4, 6)[f]
                dve.wait_ge(gate_ready, g + 1)
                dve.wait_ge(ffn_dn, nth_down(f, NCHUNK - 1, 1))
                residual((), src, signal, True)
                if f in (0, 2):
                    for b in range(2):
                        split_down(f + 1, 0, b)

            ffn(0, 4, cx, mod_scale[:, 0], mod[:, 0, 0, 1], ctx_ready)
            ffn(1, 5, x, mod_scale[:, 1], mod[:, 0, 0, 0], x_ready)

            norm(6, 7, x, 0, mod_scale[:, 2], mod[:, 0, 3, 0])
            for z, a in ((qe, HD), (qo, 0), (qbe, HD), (qbo, 0)):
                dve.memset(z[a:a + HD], 0.0).then_inc(at_zero, 1)
            norm(7, 8, cx, T, mod_scale[:, 3], mod[:, 0, 3, 1])
            wait_used(dve, U_ATT + 2)
            dve.tensor_copy(va, lo[:, :, :]).then_inc(at_va, 1)
            dve.wait_ge(bias_loaded, 16 * 16)
            dve.wait_ge(rope_loaded, 64)
            tt(bias, bias, window.unsqueeze(1).broadcast_to([P, 2 * NAH, T]), ALU.add).then_inc(na_bias, 1)
            cosb, sinb = (a.unsqueeze(1).broadcast_to([P, CC, T]) for a in (cos, sin))
            dve.wait_ge(at_rot, 1)
            link(tt(rawq, rawq, cosb, ALU.mult))
            link(tt(rtmp, lo[:, 0:2, :].rearrange("p a (b t) -> p (a b) t", b=2), sinb, ALU.mult))
            tt(qbe[0:HD], rawq[0:HD], rtmp[0:HD], ALU.add).then_inc(at_rope, 1)
            tt(qbo[HD:P], rawq[HD:P], rtmp[HD:P], ALU.add).then_inc(at_rope, 1)
            dve.wait_ge(at_rot, 2)
            link(tt(rawk, rawk, cosb, ALU.mult))
            dve.wait_ge(at_rope, 2)
            link(tt(rtmp, lo[:, 2:4, :].rearrange("p a (b t) -> p (a b) t", b=2), sinb, ALU.mult))
            tt(kbT[:, :, 0:T], rawk, rtmp, ALU.add).then_inc(at_rope, 1)
            link(tt(lam_in[:, 0, :], lam_in[:, 0, :], lam_in[:, 1, :], ALU.mult))
            link(tt(lam_in[:, 2, :], lam_in[:, 2, :], lam_in[:, 3, :], ALU.mult))
            dve.tensor_reduce(small[:, 40:42], lam_in[:, 0::2, :], AX.X, ALU.add).then_inc(lam_d, 1)
            dve.wait_ge(lam_e, 1)
            lam = small[:, 44:45]
            link(tt(lam, small[:, 42:43], small[:, 43:44], ALU.subtract))
            link(ts(lam, lam, LAM_INIT, None, ALU.add))

            def na_max(h):
                dve.wait_ge(na_s, h + 1)
                b = 2 * (h % 2)
                link(dve.tensor_reduce(small[:, 56 + b:58 + b], hi[:, b:b + 2, :], AX.X, ALU.max))
                ts(small[:, 48 + b:50 + b], small[:, 56 + b:58 + b], -HD ** -0.5, None, ALU.mult).then_inc(na_nm, 1)

            def na_out(h):
                dve.wait_ge(na_pv, h + 1)
                dve.tensor_copy(mergeT[:, h // 2, :], lo[:, 2 + (h // 2) % 2, 0:T]).then_inc(na_o, 1)

            def df_max(h):
                dve.wait_ge(df_s, h + 1)
                link(dve.tensor_reduce(small[:, 56:60], hi[:, :, :], AX.X, ALU.max))
                ts(small[:, 48:52], small[:, 56:60], -HD ** -0.5, None, ALU.mult).then_inc(df_nm, 1)

            def df_out(h):
                dve.wait_ge(df_pv, h + 1)
                dve.tensor_copy(dO[:, h, :], lo[:, 2 + h % 2, 0:T]).then_inc(df_o, 1)

            def na_weights(h):
                b = 2 * (h % 2)
                dve.wait_ge(na_e, TT * (h + 1))
                link(dve.reciprocal(small[:, 76 + b:78 + b], small[:, 52 + b:54 + b]))
                for t in range(TT):
                    ts(ap_[:, b + t, :], ap_[:, b + t, :], small[:, 76 + b + t:77 + b + t], None, ALU.mult).then_inc(na_p, 1)

            na_max(0)
            na_max(1)
            na_weights(0)
            for h in range(NAH):
                if h + 1 < NAH:
                    na_weights(h + 1)
                if h + 2 < NAH:
                    na_max(h + 2)
                if h and h % 2 == 0:
                    na_out(h - 1)
            df_max(0)
            na_out(NAH - 1)
            for h in range(DH):
                dve.wait_ge(df_e, 4 * (h + 1))
                r = small[:, 76:80]
                link(dve.reciprocal(r, small[:, 52:56]))
                link(ts(r[:, 2:4], r[:, 2:4], lam, None, ALU.mult))
                for t in range(TT):
                    link(ts(ap_[:, 2 + t, :], ap_[:, 2 + t, :], r[:, 2 + t:3 + t], None, ALU.mult))
                    stt(ap_[:, t, :], ap_[:, t, :], r[:, t:t + 1], ap_[:, 2 + t, :], ALU.mult, ALU.subtract).then_inc(df_p, 1)
                if h + 1 < DH:
                    df_max(h + 1)
                if h:
                    df_out(h - 1)
            df_out(DH - 1)
            dve.wait_ge(df_std, 1)
            dve.wait_ge(df_o, DH)
            stt(mergeT[:, CC:KC, :], dO, subln[:], dsq, ALU.mult, ALU.mult).then_inc(df_n, 1)
            dve.wait_ge(gate_ready, 3)
            residual((U_ATTO, U_ATTO + 1), x, x_ready, True)

            ffn(2, 8, x, mod_scale[:, 4], mod[:, 0, 6, 0], x_ready)
            ffn(3, 9, x, mod_scale[:, 5], mod[:, 1, 0, 0], x_ready)

            norm(10, 11, x, None, mod_scale[:, 6], mod[:, 1, 3, 0])
            rest_x(merged, CM_XS)

            def cm_product(j):
                dve.wait_ge(ffn_gu, CM_UP + 4 * (j + 1))
                dve.wait_ge(cm_cg, j + 1)
                tt(u2[:, 4 * j:4 * j + 4, :], (hi if j else lo)[:, 2:4, :].rearrange("p a (b t) -> p (a b) t", b=2),
                   cgs[:, 4 * j:4 * j + 4, :], ALU.mult).then_inc(cm_u, 1)

            def cm_taps(*chunks):
                dve.wait_ge(cm_u, chunks[0] // 4 + 1)
                for c in chunks:
                    taps = [col(R3_CONV2 + i * KC + c, 1, 2) for i in range(3)]
                    link(ts(vm[:, c, :], u2[:, c, :], taps[1], None, ALU.mult))
                    link(stt(vm[:, c, 1:T], u2[:, c, 0:T - 1], taps[0], vm[:, c, 1:T], ALU.mult, ALU.add))
                    link(stt(vm[:, c, 0:T - 1], u2[:, c, 1:T], taps[2], vm[:, c, 0:T - 1], ALU.mult, ALU.add))

            def cm_unit(j):
                for b in range(2):
                    cm_up(j, b)

            cm_unit(1)
            cm_unit(2)
            cm_product(0)
            for c in range(4):
                cm_up(3 + c // 2, c % 2)
                cm_taps(c)
            cm_product(1)
            cm_up(5, 0)
            cm_taps(4)
            cm_up(5, 1)
            cm_taps(5, 6, 7)
            for j in range(2):
                dve.wait_ge(ffn_gu, CM_UP + 2 * (5 + j))
                v = vm[:, 4 * j:4 * j + 4, :]
                tt(v, v, lo[:, 2 * j:2 * j + 2, :].rearrange("p a (b t) -> p (a b) t", b=2), ALU.mult).then_inc(cm_bg, 1)
            rest_x(vm, CM_XS + 1)
            for k in range(CM_ROWS):
                cm_down(k)
            dve.wait_ge(ffn_dn, CM_DOWN + CM_ROWS)
            dve.wait_ge(gate_ready, 6)
            residual((), x, x_ready, True)
            ffn(4, 11, x, mod_scale[:, 7], mod[:, 1, 6, 0], x_ready)

            dve.wait_ge(gain_loaded, 32)
            dve.wait_ge(norm_turned, 48)
            for t in range(TT):
                rstd_of(13, t)
                stt(xn[:, t, :], x[:, t, :], rstd[:, t:t + 1], gate_b[:], ALU.mult, ALU.mult).then_inc(x_ready, 1)


_INS = ['x', 'mem', 'norm_mix_g', 'w_in', 'conv_w', 'conv_b', 'conv_ln_g', 'conv_ln_b', 'conv_w_out', 'hgrn_lb_logits',
        'hgrn_onorm_g', 'hgrn_w_out', 'w_mix_out', 'norm_xa_g', 'norm_mem_g', 'xa_w_q', 'xa_w_k', 'xa_w_v', 'xa_w_o',
        'norm_ffn_g', 'router_group_w', 'router_group_b', 'router_expert_w', 'router_expert_b', 'moe_w_gate', 'moe_w_up',
        'moe_w_down', 'final_norm_g', 'c_2', 'ctx_2', 'c_ctx_2', 'mod_w_2', 'mod_b_2', 'norm_g_2', 'ffn_w_gate_2',
        'ffn_w_up_2', 'ffn_w_down_2', 'attn_w_in_2', 'attn_w_out_2', 'rpb_pad', 'diff_lambda_2', 'diff_subln_g_2',
        'conv_w_in_2', 'conv_w_out_2', 'conv_w_2', 'final_g_2']


def constants():
    import numpy as np

    f = np.float32
    mats = np.zeros((P, 3, P), f)
    mats[:, 0] = np.eye(P)
    for a in range(0, P, GRID):
        mats[a:a + GRID, 1, a:a + GRID] = 8.0 * np.eye(GRID)[::-1]
    for i in range(0, P, 2):
        mats[i + 1, 2, i], mats[i, 2, i + 1] = -1.0, 1.0
    s, t = np.arange(P)[:, None], np.arange(P)[None, :]
    masks = np.zeros((P, 8, P), f)
    masks[:, 0] = np.eye(P)
    for v in range(1, 8):
        half = 1 << (v - 1)
        masks[:, v] = (s // (2 * half) == t // (2 * half)) & (s // half % 2 == 0) & (t // half % 2 == 1)
    n_freq = HD // 4
    inv = f(10000.0) ** (-np.arange(n_freq, dtype=f) / f(n_freq))
    tok = np.arange(T)
    ang = np.concatenate([(tok // GRID).astype(f)[:, None] * inv, (tok % GRID).astype(f)[:, None] * inv], axis=-1)
    rope = np.zeros((P, 2, T), f)
    pair = np.arange(P) % HD // 2
    rope[:, 0], rope[:, 1] = np.cos(ang).T[pair], np.sin(ang).T[pair]
    qc = GRID - 1 - np.arange(P) % GRID
    start = np.clip(qc - 8, 0, GRID - 16)
    kc = np.arange(T) % GRID
    window = np.where((kc >= start[:, None]) & (kc < start[:, None] + 16), f(0), f(-1e30)).astype(f)
    desc = np.tile(np.arange(PER_GROUP, 0, -1, dtype=f), (P, 1))
    rank = np.zeros((P, P + PLACES), f)
    rank[:, 0:P] = (s < t) / f(CW)
    rank[:, P:] = np.arange(PLACES)
    return {"k_mats": mats, "k_masks": masks, "k_rope": rope, "k_window": window, "k_desc": desc, "k_rank": rank}


def kernel(**inputs):
    import numpy as _np
    import concourse.bacc as _bacc
    from concourse import mybir as _mybir
    from concourse.bass_utils import run_bass_kernel_spmd as _run

    nc = _bacc.Bacc("TRN2", target_bir_lowering=False, num_devices=1)
    tables = constants()
    rpb = _np.asarray(inputs["na_rpb_2"])[0]
    pad = GRID - 16
    tables["rpb_pad"] = _np.pad(rpb, ((0, 0), (0, 0), (pad, P - pad - rpb.shape[-1])))
    arrays, args = {}, []
    for name in _INS + ["k_mats", "k_masks", "k_rope", "k_window", "k_desc", "k_rank"]:
        a = _np.ascontiguousarray(tables[name] if name in tables else inputs[name])
        arrays[f"in_{name}_dram"] = a
        args.append(nc.dram_tensor(f"in_{name}_dram", a.shape, _mybir.dt.from_np(a.dtype), kind="ExternalInput").ap())
    args.append(nc.dram_tensor("out_0_dram", (1, T, D), F32, kind="ExternalOutput").ap())
    program(nc, *args)
    r = _run(nc, [arrays], core_ids=[0])
    return r.results[0]["out_0_dram"]
```
